# Optimizing a Trainium2 kernel written in Bass

```python
import math
import jax, jax.numpy as jnp
from jax import lax
import numpy as np

D_MODEL = 1024
BATCH = 1
SEQ = 1024
DEPTH = 1

D_MIX = D_MODEL
A_GROUPS = 8
A_GROUP_DIM = 64
A_WIDTH = A_GROUPS * A_GROUP_DIM
A_CONV = 3
DN_HEADS = 4
DN_HEAD_DIM = 128
DN_WIDTH = DN_HEADS * DN_HEAD_DIM
DN_CONV = 4
CHUNK = 64
D_FF = 2816
FF_CONV = 3
P_IN = 3 * A_WIDTH + 4 * DN_WIDTH + 2 * DN_HEADS
N_MOD = 6
EPS = 1e-6

kernel_name = "hybrid_shortconv_gdn_convffn_adaln"

def rmsnorm(x, w):
    xf = x.astype(jnp.float32)
    y = xf * lax.rsqrt(jnp.mean(xf * xf, axis=-1, keepdims=True) + EPS)
    return (y * w.astype(jnp.float32)).astype(x.dtype)

def l2norm(x):
    xf = x.astype(jnp.float32)
    return xf * lax.rsqrt(jnp.sum(xf * xf, axis=-1, keepdims=True) + EPS)

def causal_dwconv(x, w):
    width, ch = w.shape
    return lax.conv_general_dilated(
        x, w[:, None, :].astype(x.dtype), window_strides=(1,), padding=[(width - 1, 0)],
        dimension_numbers=('NWC', 'WIO', 'NWC'), feature_group_count=ch)

def to_chunks(t):
    b, l, h = t.shape[:3]
    t = t.reshape(b, l // CHUNK, CHUNK, h, *t.shape[3:])
    return jnp.moveaxis(t, 3, 1)

def gated_delta_rule(q, k, v, g, beta):
    b, l, h, dk = q.shape
    dv = v.shape[-1]
    q, k, v, g, beta = (to_chunks(t) for t in (q * dk ** -0.5, k, v, g, beta))
    g = jnp.cumsum(g, axis=-1)
    pos = jnp.arange(CHUNK)
    causal = pos[:, None] >= pos[None, :]
    strict = pos[:, None] > pos[None, :]
    gdiff = jnp.where(causal, g[..., :, None] - g[..., None, :], 0.0)
    decay = jnp.where(causal, jnp.exp(gdiff), 0.0)
    k_beta = k * beta[..., None]
    lower = jnp.where(strict, jnp.einsum('bhncd,bhnsd->bhncs', k_beta, k) * decay, 0.0)
    rhs = jnp.concatenate([v * beta[..., None], k_beta * jnp.exp(g)[..., None]], axis=-1)
    sol = lax.linalg.triangular_solve(lower, rhs, left_side=True, lower=True, unit_diagonal=True)
    u, w = sol[..., :dv], sol[..., dv:]
    intra = jnp.where(causal, jnp.einsum('bhncd,bhnsd->bhncs', q, k) * decay, 0.0)
    q_dec = q * jnp.exp(g)[..., None]
    k_dec = k * jnp.exp(g[..., -1:] - g)[..., None]
    chunk_decay = jnp.exp(g[..., -1])

    def step(state, inp):
        u_i, w_i, q_i, k_i, a_i, cd_i = inp
        v_new = u_i - jnp.einsum('bhcd,bhde->bhce', w_i, state)
        o_i = jnp.einsum('bhcd,bhde->bhce', q_i, state) + jnp.einsum('bhcs,bhse->bhce', a_i, v_new)
        state = state * cd_i[..., None, None] + jnp.einsum('bhcd,bhce->bhde', k_i, v_new)
        return state, o_i

    xs = tuple(jnp.moveaxis(t, 2, 0) for t in (u, w, q_dec, k_dec, intra, chunk_decay))
    state0 = jnp.zeros((b, h, dk, dv), jnp.float32)
    _, o = lax.scan(step, state0, xs)
    return jnp.transpose(o, (1, 0, 3, 2, 4)).reshape(b, l, h, dv)

def setup_inputs(seed: int = 0) -> dict:
    key = jax.random.key(seed)
    ks = jax.random.split(key, 20)
    f32 = jnp.float32

    def nrm(k, shape, s):
        return jax.random.normal(k, shape, f32) * s

    def gain(k, shape):
        return 1.0 + 0.02 * jax.random.normal(k, shape, f32)

    dt = jnp.exp(jax.random.uniform(ks[10], (DEPTH, DN_HEADS), f32, math.log(1e-3), math.log(1e-1)))
    return {
        'x': nrm(ks[0], (BATCH, SEQ, D_MODEL), 1.0),
        'c': nrm(ks[1], (BATCH, D_MODEL), 1.0),
        'ada_w': nrm(ks[2], (DEPTH, D_MODEL, N_MOD * D_MODEL), 0.5 * D_MODEL ** -0.5),
        'ada_b': nrm(ks[3], (DEPTH, N_MOD * D_MODEL), 0.02),
        'norm1_w': gain(ks[4], (DEPTH, D_MODEL)),
        'w_in': nrm(ks[5], (DEPTH, D_MODEL, P_IN), D_MODEL ** -0.5),
        'conv_a_w': nrm(ks[6], (DEPTH, A_CONV, A_WIDTH), A_CONV ** -0.5),
        'norm_a_w': gain(ks[7], (DEPTH, A_WIDTH)),
        'conv_qkv_w': nrm(ks[8], (DEPTH, DN_CONV, 3 * DN_WIDTH), DN_CONV ** -0.5),
        'a_log': jnp.log(jax.random.uniform(ks[9], (DEPTH, DN_HEADS), f32, 1.0, 16.0)),
        'dt_bias': dt + jnp.log(-jnp.expm1(-dt)),
        'norm_dn_w': gain(ks[11], (DEPTH, DN_HEAD_DIM)),
        'w_out': nrm(ks[12], (DEPTH, D_MIX, D_MODEL), D_MIX ** -0.5),
        'norm2_w': gain(ks[13], (DEPTH, D_MODEL)),
        'w_up': nrm(ks[14], (DEPTH, D_MODEL, 2 * D_FF), D_MODEL ** -0.5),
        'conv_ff_w': nrm(ks[15], (DEPTH, FF_CONV, 2 * D_FF), FF_CONV ** -0.5),
        'w_down': nrm(ks[16], (DEPTH, D_FF, D_MODEL), D_FF ** -0.5),
        'norm_f_w': gain(ks[17], (D_MODEL,)),
    }

def reference(x, c, ada_w, ada_b, norm1_w, w_in, conv_a_w, norm_a_w, conv_qkv_w, a_log,
              dt_bias, norm_dn_w, w_out, norm2_w, w_up, conv_ff_w, w_down, norm_f_w):
    b, l, _ = x.shape
    cut = np.cumsum([A_WIDTH, A_WIDTH, A_WIDTH, 3 * DN_WIDTH, DN_WIDTH, DN_HEADS]).tolist()
    c_act = jax.nn.silu(c)
    for i in range(DEPTH):
        mod = (c_act @ ada_w[i] + ada_b[i])[:, None, :]
        sh1, sc1, gt1, sh2, sc2, gt2 = jnp.split(mod, N_MOD, axis=-1)

        h = rmsnorm(x, norm1_w[i]) * (1.0 + sc1) + sh1
        p = h @ w_in[i]
        a_b, a_c, a_x, qkv, z, beta_logit, alpha = jnp.split(p, cut, axis=-1)

        ya = a_b * causal_dwconv(a_c * a_x, conv_a_w[i])
        ya = rmsnorm(ya.reshape(b, l, A_GROUPS, A_GROUP_DIM),
                     norm_a_w[i].reshape(A_GROUPS, A_GROUP_DIM)).reshape(b, l, A_WIDTH)

        qkv = jax.nn.silu(causal_dwconv(qkv, conv_qkv_w[i]))
        q, k, v = jnp.split(qkv.reshape(b, l, 3 * DN_HEADS, DN_HEAD_DIM), 3, axis=2)
        beta = jax.nn.sigmoid(beta_logit.astype(jnp.float32))
        g = -jnp.exp(a_log[i].astype(jnp.float32)) * jax.nn.softplus(
            alpha.astype(jnp.float32) + dt_bias[i].astype(jnp.float32))
        o = gated_delta_rule(l2norm(q), l2norm(k), v.astype(jnp.float32), g, beta).astype(x.dtype)
        o = rmsnorm(o, norm_dn_w[i]) * jax.nn.silu(z.reshape(b, l, DN_HEADS, DN_HEAD_DIM))
        yb = o.reshape(b, l, DN_WIDTH)

        y = jnp.concatenate([ya, yb], axis=-1) @ w_out[i]
        x = x + gt1 * y

        h = rmsnorm(x, norm2_w[i]) * (1.0 + sc2) + sh2
        gate, up = jnp.split(causal_dwconv(h @ w_up[i], conv_ff_w[i]), 2, axis=-1)
        x = x + gt2 * ((jax.nn.silu(gate) * up) @ w_down[i])
    return rmsnorm(x, norm_f_w)


_drawn_inputs = setup_inputs


def setup_inputs(seed=0):
    import zlib

    import numpy as np

    out = dict(_drawn_inputs(seed))
    spreads = {}
    factors = {'norm1_w': 6.676,
     'norm_a_w': 8.0,
     'a_log': 3.026,
     'norm_dn_w': 8.0,
     'norm2_w': 8.0,
     'norm_f_w': 2.887}
    for name, (base, spread) in spreads.items():
        noise = np.random.default_rng([zlib.crc32(name.encode()), seed]).standard_normal(out[name].shape)
        drawn = base * np.exp(spread * noise) if base else spread * noise
        out[name] = __import__('jax').numpy.asarray(drawn.astype(out[name].dtype))
    for name, factor in factors.items():
        out[name] = (out[name] * factor).astype(out[name].dtype)
    return out
```

```python
import math
from contextlib import ExitStack

import concourse.bass as bass
from concourse import mybir

F32 = mybir.dt.float32
F32R = mybir.dt.float32r
ALU = mybir.AluOpType
ACT = mybir.ActivationFunctionType
AX_X = mybir.AxisListType.X

P = 128
KIB = 1024
BANK = 512


def ds(start, n):
    return bass.ds(start, n)


def build_program(nc, x, c, ada_w, ada_b, norm1_w, w_in, conv_a_w, norm_a_w, conv_qkv_w, a_log,
                  dt_bias, norm_dn_w, w_out, norm2_w, w_up, conv_ff_w, w_down, norm_f_w, out):
    L, D = x.shape[1], x.shape[2]
    DFF = w_down.shape[1]
    AW = conv_a_w.shape[2]
    DNW = conv_qkv_w.shape[2] // 3
    NH = a_log.shape[1]
    KT = D // P
    TT = L // P
    AT = AW // P
    FT = DFF // P
    NMOD = ada_b.shape[1] // D
    EPS = 1e-6
    GROUP = 64
    LEVELS = 7
    assert (L, D, AT, NH, DNW) == (1024, 1024, 4, 4, NH * P) and FT % 2 == 0

    ctx = ExitStack()
    with ctx:
        base = 16512 + 64

        def sb(name, offset, shape, dt=F32):
            return nc.alloc_sbuf_tensor_at(name, [P] + shape, dt, offset=offset)

        o_h = base
        o_q, o_k, o_v, o_z = (base + (64 + 16 * n) * KIB for n in range(4))
        o_a = base + 128 * KIB
        o_w = base + 144 * KIB
        o_c = base + 200 * KIB

        h = sb("h", o_h, [TT, 2, KT, P], F32R)
        q_t = sb("q_t", o_q, [NH, L])
        k_t = sb("k_t", o_k, [NH, L])
        v_t = sb("v_t", o_v, [NH, L])
        z_t = sb("z_t", o_z, [NH, L])
        a_t = sb("a_t", o_a, [AT, L])

        cursor = [o_c]

        def small(name, shape, dt=F32):
            n = 4 * math.prod(shape)
            t = sb(name, cursor[0], shape, dt)
            cursor[0] += (n + 31) // 32 * 32
            assert cursor[0] <= 229344, cursor
            return t

        ident = small("ident", [P])
        ones = small("ones", [P])
        causal = small("causal", [P])
        group_ones = small("group_ones", [P])
        level_mask = sb("level_mask", o_w + 52 * KIB, [LEVELS, P])
        NA_ROWS = KT * 3 + NMOD * KT + AT + 1 + 3 * AT
        NB_ROWS = 4 * 3 * NH + 2 * FT
        NC_ROWS = 2 * 2 * FT
        col_a = small("col_a", [NA_ROWS])
        col_b = small("col_b", [NB_ROWS])
        col_c = small("col_c", [NC_ROWS])
        mod = small("mod", [NMOD * KT])
        c_act = small("c_act", [KT])
        scale1 = small("scale1", [KT])
        scale2 = small("scale2", [KT])
        eps_col = small("eps_col", [1])
        one_col = small("one_col", [1])
        qscale_col = small("qscale_col", [1])
        neg_dn_w = small("neg_dn_w", [1])
        ss = small("ss", [TT])
        var = small("var", [TT])
        rstd = small("rstd", [TT])
        ba = small("ba", [TT, 2 * NH])
        w_ba = small("w_ba", [KT, 2 * NH])
        gate_rows = small("gate_rows", [2, NH])
        g = small("g", [TT, NH])
        beta = small("beta", [TT, NH])
        neg_beta = small("neg_beta", [TT, NH])
        tmp_g = small("tmp_g", [TT, NH])
        tmp_m = small("tmp_m", [TT, NH])
        gc = small("gc", [NH])
        kdec = small("kdec", [NH])
        cdec = small("cdec", [2, NH])

        rows_a = sb("rows_a", o_w + 24 * KIB, [P])
        rows_b = sb("rows_b", o_w + 24 * KIB + 512, [P])
        rows_c = sb("rows_c", o_w + 24 * KIB + 1024, [P])

        ada_first = [sb(f"ada_first{n}", o, [KT, BANK]) for n, o in enumerate((o_q, o_k, o_v, o_a))]
        x_lo4 = sb("x_lo4", o_z, [4, D])
        x_hi4 = sb("x_hi4", o_w + 8 * KIB, [4, D])
        xn = sb("xn", o_w + 36 * KIB, [2, D])
        hf = sb("hf", o_w + 44 * KIB, [2, KT, P])

        WSLOTS = 3
        w_split = sb("w_split", o_w, [WSLOTS, 2, KT, P], F32R)
        w_raw = sb("w_raw", o_w + 24 * KIB, [WSLOTS, KT, P])
        cx = sb("cx", o_w + 36 * KIB, [L])
        sq = sb("sq", o_w + 40 * KIB, [L])
        ada_raw = sb("ada_raw", o_w + 44 * KIB, [2, KT, P])

        def dn(name, n, slots=None):
            shape = [NH, P] if slots is None else [slots, NH, P]
            return sb(name, o_w + 2 * n * KIB, shape)

        kc = dn("kc", 0)
        gb_lt = dn("gb_lt", 1)
        egb = dn("egb", 2)
        dec = dn("dec", 3)
        tm = dn("tm", 4)
        pm = dn("pm", 5)
        mlev = sb("mlev", o_w + 12 * KIB, [LEVELS - 1, NH, P])
        kg = dn("kg", 12, 2)
        qd = dn("qd", 14, 2)
        att = dn("att", 16, 2)
        kd = dn("kd", 18, 2)
        um = dn("um", 20, 2)
        rr = dn("rr", 22)
        vn = dn("vn", 23)
        st = dn("st", 24)
        vc = dn("vc", 25)
        osq = sb("osq", o_w + 52 * KIB, [L])

        wo_split = [sb("wo_split_a", o_w, [4, 2, D], F32R), None]
        wo_split_q = sb("wo_split_q", o_q, [2, 2, D], F32R)
        wo_split_z = sb("wo_split_z", o_z, [2, 2, D], F32R)
        wo_raw = sb("wo_raw", o_w + 32 * KIB, [3, D])
        gate_row = sb("gate_row", o_w + 44 * KIB, [D])
        diag = sb("diag", o_w + 48 * KIB, [KT, P])
        x2 = sb("x2", o_k, [TT, D])
        xn2 = sb("xn2", o_a, [2, D])
        hf2 = sb("hf2", o_a + 8 * KIB, [2, KT, P])

        wg_split = sb("wg_split", o_w, [2, KT, P], F32R)
        wu_split = sb("wu_split", o_w + 8 * KIB, [2, KT, P], F32R)
        wd_split = sb("wd_split", o_w + 16 * KIB, [2, 2, D], F32R)
        act_split = sb("act_split", o_q, [2, 2, L], F32R)
        wg_raw = sb("wg_raw", o_w + 32 * KIB, [KT, P])
        wu_raw = sb("wu_raw", o_w + 36 * KIB, [KT, P])
        wd_raw = sb("wd_raw", o_w + 40 * KIB, [D])
        gate2_row = sb("gate2_row", o_w + 44 * KIB, [D])
        cg = sb("cg", o_z, [L])
        cu = sb("cu", o_z + 4 * KIB, [L])
        normf_row = sb("normf_row", o_z + 8 * KIB, [D])

        ps = ctx.enter_context(nc.psum_tensor("ps", [P, 8, BANK], F32))

        def bank(n, count=1, width=None):
            v = ps[:, n:n + count, :].rearrange("p b n -> p (b n)")
            return v if width is None else v.rearrange("p (q n) -> p q n", n=width)

        def sem(name):
            return ctx.enter_context(nc.semaphore(name))

        def sems(name, count):
            return [sem(f"{name}{n}") for n in range(count)]

        class s:
            x_in = sems("x_in", 4)
            w_raw_in = sems("w_raw_in", 3)
            w_hi_done = sems("w_hi_done", 3)
            w_lo_done = sems("w_lo_done", 3)
            rows_in = sem("rows_in")
            ada_first_in = sems("ada_first_in", 4)
            w_ba_in = sem("w_ba_in")
            gate_rows_in = sem("gate_rows_in")
            sp_past_wait = sem("sp_past_wait")
            cols_ready = sem("cols_ready")
            ada_mm = sem("ada_mm")
            ada_in = sems("ada_in", 2)
            norm_lo = sem("norm_lo")
            ba_mm = sem("ba_mm")
            dn_over = sem("dn_over")
            wo_raw_in = sems("wo_raw_in", 3)
            wo_lo = sem("wo_lo")
            wg_raw_in = sem("wg_raw_in")
            wu_raw_in = sem("wu_raw_in")
            wd_raw_in = sem("wd_raw_in")
            wg_lo = sem("wg_lo")
            wu_lo = sem("wu_lo")
            wd_lo = sem("wd_lo")
            normf_in = sem("normf_in")
            y_ready = sem("y_ready")
            out_done = sem("out_done")
            const_built = sem("const_built")
            consts_ready = sem("consts_ready")
            norm_hi = sem("norm_hi")
            dn_r = sem("dn_r")
            dn_o = sem("dn_o")
            dn_egb = sem("dn_egb")
            dn_kg = sem("dn_kg")
            dn_qd = sem("dn_qd")
            dn_lt = sem("dn_lt")
            dn_p = sem("dn_p")
            dn_m = sem("dn_m")
            ya_hi = sem("ya_hi")
            ya_lo = sem("ya_lo")
            gate_row_ready = sem("gate_row_ready")
            wo_gated = sem("wo_gated")
            wo_hi = sem("wo_hi")
            yb_hi = sem("yb_hi")
            yb_lo = sem("yb_lo")
            wg_hi = sem("wg_hi")
            wu_hi = sem("wu_hi")
            wd_gated = sem("wd_gated")
            wd_hi = sem("wd_hi")
            act_hi = sem("act_hi")
            act_lo = sem("act_lo")
            act_past_wait = sem("act_past_wait")
            tile_mm = sem("tile_mm")
            c_act_ready = sem("c_act_ready")
            norm_turned = sem("norm_turned")
            norm_ss = sem("norm_ss")
            norm_inv = sem("norm_inv")
            norm_rstd = sem("norm_rstd")
            norm_hf = sem("norm_hf")
            gates_in = sem("gates_in")
            gate_act = sem("gate_act")
            stat_mm = sem("stat_mm")
            stat_ln = sem("stat_ln")
            stat_rs = sem("stat_rs")
            ax_taken = sem("ax_taken")
            cx_ready = sem("cx_ready")
            conv_tapped = sem("conv_tapped")
            ya_raw = sem("ya_raw")
            k_norm = sem("k_norm")
            sq_ready = sem("sq_ready")
            conv_step = sem("conv_step")
            silu_done = sem("silu_done")
            ya_norm = sem("ya_norm")
            q_norm = sem("q_norm")
            z_taken = sems("z_taken", 2)
            dn_t0 = sem("dn_t0")
            dn_kt = sem("dn_kt")
            gates_ready = sem("gates_ready")
            dn_gb = sem("dn_gb")
            dn_kc = sem("dn_kc")
            dn_cum = sem("dn_cum")
            dn_cd = sem("dn_cd")
            dn_diff = sem("dn_diff")
            dn_dec = sem("dn_dec")
            dn_kdiff = sem("dn_kdiff")
            dn_kdec = sem("dn_kdec")
            dn_t1 = sem("dn_t1")
            dn_t1_copied = sem("dn_t1_copied")
            dn_pm = sem("dn_pm")
            dn_vc = sem("dn_vc")
            dn_rr = sem("dn_rr")
            dn_o_copied = sem("dn_o_copied")
            gate_mm = sem("gate_mm")
            yb_rs_used = sem("yb_rs_used")
            osq_ready = sem("osq_ready")
            ostat_mm = sem("ostat_mm")
            ostat_ln = sem("ostat_ln")
            ostat_rs = sem("ostat_rs")
            yb_ready = sem("yb_ready")
            out_a_mm = sem("out_a_mm")
            x2_out = sem("x2_out")
            gate_tile_mm = sem("gate_tile_mm")
            ff_tapped = sem("ff_tapped")
            cg_conv = sem("cg_conv")
            cg_silu = sem("cg_silu")
            down_tile_mm = sem("down_tile_mm")
            up_tile_mm = sem("up_tile_mm")
            act_ready = sem("act_ready")
            x2_mlp = sem("x2_mlp")
            rows_turned = sem("rows_turned")
            norm_ms = sem("norm_ms")
            norm_step = sem("norm_step")
            norm_xn = sem("norm_xn")
            ada_first_mm = sem("ada_first_mm")
            mod_step = sem("mod_step")
            gate_step = sem("gate_step")
            mod_taken = sem("mod_taken")
            dn_t2 = sem("dn_t2")
            dn_g_step = sem("dn_g_step")
            dn_d_step = sem("dn_d_step")
            dn_masked = sem("dn_masked")
            dn_l_step = sem("dn_l_step")
            dn_att = sem("dn_att")
            dn_v = sem("dn_v")
            dn_u = sem("dn_u")
            dn_s = sem("dn_s")
            dn_kd = sem("dn_kd")
            dn_tt = sem("dn_tt")
            dn_tm = sem("dn_tm")
            dn_vn = sem("dn_vn")
            dn_st = sem("dn_st")
            diag_ready = sem("diag_ready")
            out_mm = sem("out_mm")
            cg_step = sem("cg_step")
            cu_step = sem("cu_step")
            cu_conv = sem("cu_conv")

        def rows(ap):
            return ap.rearrange("a (r n) -> (a r) n", n=P)

        x_pairs = x.rearrange("b (t p) d -> p (b t) d", p=P)
        out_rows = out.rearrange("b (t p) d -> (b t) p d", p=P)
        ada_v = ada_w.rearrange("o (k p) n -> p (o k) n", p=P)
        win_v = w_in.rearrange("o (k p) n -> p (o k) n", p=P)
        wup_v = w_up.rearrange("o (k p) n -> p (o k) n", p=P)
        wout_v = w_out.rearrange("o (k p) n -> p (o k) n", p=P)
        wdown_v = w_down.rearrange("o (k p) n -> p (o k) n", p=P)

        C_C, C_N1, C_N2, C_ADAB = 0, KT, 2 * KT, 3 * KT
        C_NA = C_ADAB + NMOD * KT
        C_DN = C_NA + AT
        C_CA = C_DN + 1
        C_QKV, C_FF2 = 0, 4 * 3 * NH
        SH1, SC1, GT1, SH2, SC2, GT2 = (m * KT for m in range(6))

        N1, N2, NF = 0, TT, 2 * TT

        AX, AC, AB, Q, K, V, Z = range(7)
        NPOS = 7
        W_BASE = [2 * AW, AW, 0, 3 * AW, 3 * AW + DNW, 3 * AW + 2 * DNW, 3 * AW + 3 * DNW]
        W_SLOT = [0, 1, 2, 0, 1, 2, 1]
        USES = [W_SLOT.count(n) for n in range(WSLOTS)]
        T_BANK = [0, 2, 0, 2, 0, 2, 0]
        ADA_AFTER = {AX: [0], AC: [1], AB: [2], Q: [3], K: [4], V: [5], Z: [6, 7]}

        def use(pos, j):
            slot = W_SLOT[pos]
            return j * USES[slot] + W_SLOT[:pos].count(slot) + 1

        def x_in(tt):
            return s.x_in[tt // 2]

        def raw_in(slot):
            return s.w_raw_in[slot]

        def hi_done(slot):
            return s.w_hi_done[slot]

        def lo_done(slot):
            return s.w_lo_done[slot]

        def wo_part(k):
            if k < 4:
                return wo_split[0][:, k, :, :]
            return (wo_split_q if k < 6 else wo_split_z)[:, k % 2, :, :]

        block = ctx.enter_context(nc.Block())

        @block.sync
        def _(sp):
            sp.dma_start(rows_a[0:KT, :], rows(c)).then_inc(s.rows_in, 16)
            sp.dma_start(rows_a[C_N1:C_N1 + KT, :], rows(norm1_w)).then_inc(s.rows_in, 16)
            sp.dma_start(rows_a[C_N2:C_N2 + KT, :], rows(norm2_w)).then_inc(s.rows_in, 16)
            sp.dma_start(rows_a[C_ADAB:C_ADAB + NMOD * KT, :], rows(ada_b)).then_inc(s.rows_in, 16)
            sp.dma_start(rows_a[C_NA:C_NA + AT, :], rows(norm_a_w)).then_inc(s.rows_in, 16)
            sp.dma_start(rows_a[C_DN:C_DN + 1, :], rows(norm_dn_w)).then_inc(s.rows_in, 16)
            sp.dma_start(rows_a[C_CA:C_CA + 3 * AT, :],
                         conv_a_w.rearrange("o t (r n) -> (o t r) n", n=P)).then_inc(s.rows_in, 16)
            sp.dma_start(rows_b[0:C_FF2, :],
                         conv_qkv_w.rearrange("o t (r n) -> (o t r) n", n=P)).then_inc(s.rows_in, 16)
            sp.dma_start(rows_b[C_FF2:C_FF2 + 2 * FT, :],
                         conv_ff_w[:, 2, :].rearrange("o (r n) -> (o r) n", n=P)).then_inc(s.rows_in, 16)
            sp.dma_start(rows_c[0:NC_ROWS, :],
                         conv_ff_w[:, 0:2, :].rearrange("o t (r n) -> (o t r) n", n=P)).then_inc(s.rows_in, 16)
            for n in range(TT // 2):
                dst = x_lo4[:, 2 * n:2 * n + 2, :] if n < 2 else x_hi4[:, 2 * n - 4:2 * n - 2, :]
                sp.dma_start(dst, x_pairs[:, 2 * n:2 * n + 2, :]).then_inc(x_in(2 * n), 16)
                sp.dma_start(ada_first[n][:, :, :], ada_v[:, :, n * BANK:(n + 1) * BANK]
                             ).then_inc(s.ada_first_in[n], 16)
            nba = 3 * AW + 4 * DNW
            sp.dma_start(w_ba[:, :, :], win_v[:, :, nba:nba + 2 * NH]).then_inc(s.w_ba_in, 16)
            sp.dma_start(gate_rows[:, 0, :], a_log.to_broadcast([P, NH])).then_inc(s.gate_rows_in, 16)
            sp.dma_start(gate_rows[:, 1, :], dt_bias.to_broadcast([P, NH])).then_inc(s.gate_rows_in, 16)

            def wait(sem, value):
                sp.wait_ge(sem, value)
                if not isinstance(value, int):
                    sp.sem_inc(s.sp_past_wait, 1)

            def load_w(pos, j):
                slot = W_SLOT[pos]
                columns = win_v[:, :, W_BASE[pos]:W_BASE[pos] + NH * P][:, :, ds(j * P, P)]
                if pos == AX and isinstance(j, int) and j == 0:
                    sp.wait_ge(s.cols_ready, 3)
                else:
                    wait(lo_done(slot), use(pos, j) - 1)
                sp.dma_start(w_raw[:, slot, :, :],
                             columns).then_inc(raw_in(slot), 16)

            def load_ada(b, j):
                first = GT1 * P + (j * 8 + b) * P
                wait(s.ada_mm, j * 8 + max(b - 1, 0))
                sp.dma_start(ada_raw[:, b % 2, :, :],
                             ada_v[:, :, ds(first, P)]).then_inc(
                                 s.ada_in[b % 2], 16)

            def projection_loads(j, last):
                for pos in range(1, NPOS):
                    load_w(pos, j)
                    for b in ADA_AFTER[pos - 1]:
                        load_ada(b, j)
                if not last:
                    load_w(AX, j + 1)
                for b in ADA_AFTER[Z]:
                    load_ada(b, j)

            load_w(AX, 0)
            sp.wait_ge(s.norm_lo, N1 + TT)
            sp.wait_ge(s.ba_mm, TT)
            with sp.Fori(0, NH - 1) as j:
                projection_loads(j, False)
            projection_loads(NH - 1, True)

            sp.wait_ge(s.dn_over, 1)
            for k in range(3):
                sp.dma_start(wo_raw[:, k, :], wout_v[:, k, :]).then_inc(s.wo_raw_in[k], 16)
            for tt in range(0, TT, 2):
                sp.dma_start(x2[:, tt:tt + 2, :], x_pairs[:, tt:tt + 2, :]).then_inc(x_in(tt), 16)
            for k in range(3, KT):
                sp.wait_ge(s.wo_lo, k - 2)
                sp.dma_start(wo_raw[:, k % 3, :], wout_v[:, k, :]).then_inc(
                    s.wo_raw_in[k % 3], 16)
            sp.wait_ge(s.wo_lo, KT)
            for f in range(1):
                sp.dma_start(wg_raw[:, :, :], wup_v[:, :, 0:P]).then_inc(s.wg_raw_in, 16)
                sp.dma_start(wu_raw[:, :, :], wup_v[:, :, DFF:DFF + P]).then_inc(s.wu_raw_in, 16)
                sp.dma_start(wd_raw[:, :], wdown_v[:, 0, :]).then_inc(s.wd_raw_in, 16)

            def mlp_loads(f):
                wait(s.wg_lo, f)
                sp.dma_start(wg_raw[:, :, :], wup_v[:, :, ds(f * P, P)]).then_inc(s.wg_raw_in, 16)
                wait(s.wu_lo, f)
                sp.dma_start(wu_raw[:, :, :], wup_v[:, :, ds(DFF + f * P, P)]).then_inc(s.wu_raw_in, 16)
                wait(s.wd_lo, f)
                sp.dma_start(wd_raw[:, :], wdown_v[:, ds(f, 1), :]).then_inc(s.wd_raw_in, 16)

            with sp.Fori(1, FT) as f:
                mlp_loads(f)
            sp.wait_ge(s.norm_lo, N2 + TT)
            sp.dma_start(normf_row[:, :], norm_f_w.rearrange("(a n) -> a n", a=1).to_broadcast([P, D])
                         ).then_inc(s.normf_in, 16)
            for tt in range(TT):
                sp.wait_ge(s.y_ready, tt + 1)
                sp.dma_start(out_rows[tt], x2[:, tt, :]).then_inc(s.out_done, 16)
            sp.wait_ge(s.out_done, 16 * TT)

        @block.gpsimd
        def _(pool):
            step = [0]

            def built(ins):
                step[0] += 1
                ins.then_inc(s.const_built, 1)
                pool.wait_ge(s.const_built, step[0])

            built(pool.memset(ident[:, :], 0.0))
            built(pool.affine_select(out=ident[:, :], in_=ident[:, :], compare_op=ALU.not_equal, fill=1.0,
                                     base=0, pattern=[[-1, P]], channel_multiplier=1))
            pool.memset(eps_col[:, :], EPS)
            pool.memset(one_col[:, :], 1.0)
            pool.memset(qscale_col[:, :], math.log(P ** -0.5))
            built(pool.memset(ones[:, :], 1.0))
            built(pool.affine_select(out=causal[:, :], in_=ones[:, :], compare_op=ALU.is_ge, fill=0.0,
                                     base=0, pattern=[[1, P]], channel_multiplier=-1))
            gv = group_ones[:, :].rearrange("p (a n) -> p a n", n=GROUP)
            ov = ones[:, :].rearrange("p (a n) -> p a n", n=GROUP)
            built(pool.affine_select(out=gv, in_=ov, compare_op=ALU.is_ge, fill=0.0,
                                     base=0, pattern=[[-GROUP, P // GROUP], [0, GROUP]], channel_multiplier=1))
            built(pool.affine_select(out=gv, in_=gv, compare_op=ALU.is_ge, fill=0.0,
                                     base=GROUP - 1, pattern=[[GROUP, P // GROUP], [0, GROUP]],
                                     channel_multiplier=-1))
            built(pool.memset(level_mask[:, :, :], 0.0))
            for lev in range(LEVELS):
                b = 1 << lev
                nb = P // (2 * b)
                m = level_mask[:, lev, :].rearrange("p (a h n) -> p a h n", h=2, n=b)[:, :, 1, :]
                built(pool.memset(m, 1.0))
                built(pool.affine_select(out=m, in_=m, compare_op=ALU.is_ge, fill=0.0, base=0,
                                         pattern=[[-2 * b, nb], [0, b]], channel_multiplier=1))
                built(pool.affine_select(out=m, in_=m, compare_op=ALU.is_ge, fill=0.0, base=b - 1,
                                         pattern=[[2 * b, nb], [0, b]], channel_multiplier=-1))
            pool.sem_inc(s.consts_ready, 1)

            def split_lo(w, hi, lo, wait, n, done):
                pool.wait_ge(wait, n)
                pool.tensor_tensor(lo, w, hi.bitcast(F32), ALU.subtract).then_inc(done, 1)

            def proj_lo(pos, j):
                slot = W_SLOT[pos]
                split_lo(w_raw[:, slot, :, :], w_split[:, slot, 0, :, :], w_split[:, slot, 1, :, :],
                         hi_done(slot), use(pos, j), lo_done(slot))

            proj_lo(AX, 0)
            for tt in range(TT):
                split_lo(hf[:, tt % 2, :, :], h[:, tt, 0, :, :], h[:, tt, 1, :, :],
                         s.norm_hi, N1 + tt + 1, s.norm_lo)

            def proj_round(j, last):
                for pos in range(1, NPOS):
                    proj_lo(pos, j)
                if not last:
                    proj_lo(AX, j + 1)

            with pool.Fori(0, NH - 1) as j:
                proj_round(j, False)
            proj_round(NH - 1, True)

            def dn_part(n, slot):
                if not (isinstance(n, int) and n == 0):
                    pool.wait_ge(s.dn_r, n - 1)
                    pool.wait_ge(s.dn_o, n - 1)
                pool.wait_ge(s.dn_egb, n + 1)
                pool.tensor_tensor(kg[:, slot, :, :], kc[:, :, :], egb[:, :, :], ALU.mult).then_inc(s.dn_kg, 1)
                pool.tensor_tensor(qd[:, slot, :, :], q_t[:, :, ds(n * P, P)], egb[:, :, :],
                                   ALU.mult).then_inc(s.dn_qd, 1)
                pool.wait_ge(s.dn_lt, n + 1)
                if not (isinstance(n, int) and n == 0):
                    pool.wait_ge(s.dn_p, n * (LEVELS - 1))
                for lev in range(1, LEVELS):
                    pool.tensor_tensor(mlev[:, lev - 1, :, :], gb_lt[:, :, :],
                                       level_mask[:, lev:lev + 1, :].to_broadcast([P, NH, P]),
                                       ALU.mult).then_inc(s.dn_m, 1)

            dn_part(0, 0)
            with pool.Fori(0, TT // 2 - 1) as i:
                dn_part(2 * i + 1, 1)
                pool.wait_ge(s.ya_hi, i + 1)
                pool.tensor_tensor(h[:, :, 1, ds(i, 1), :].rearrange("p t a n -> p (a t) n"),
                                   a_t[:, ds(i, 1), :].rearrange("p a (t n) -> p (a t) n", n=P),
                                   h[:, :, 0, ds(i, 1), :].bitcast(F32).rearrange("p t a n -> p (a t) n"),
                                   ALU.subtract).then_inc(s.ya_lo, 1)
                dn_part(2 * i + 2, 0)
            dn_part(TT - 1, 1)
            pool.wait_ge(s.ya_hi, AT)
            pool.tensor_tensor(h[:, :, 1, AT - 1, :], a_t[:, AT - 1, :].rearrange("p (t n) -> p t n", n=P),
                               h[:, :, 0, AT - 1, :].bitcast(F32), ALU.subtract).then_inc(s.ya_lo, 1)

            def wo_tile(k):
                pool.wait_ge(s.wo_raw_in[k % 3], 16 * (k // 3 + 1))
                if k == 0:
                    pool.wait_ge(s.gate_row_ready, 1)
                pool.tensor_tensor(wo_raw[:, k % 3, :], wo_raw[:, k % 3, :], gate_row[:, :],
                                   ALU.mult).then_inc(s.wo_gated, 1)
                split_lo(wo_raw[:, k % 3, :], wo_part(k)[:, 0, :], wo_part(k)[:, 1, :],
                         s.wo_hi, k + 1, s.wo_lo)

            for k in range(4):
                wo_tile(k)
            for hd in range(NH):
                pool.wait_ge(s.yb_hi, hd + 1)
                pool.tensor_tensor(h[:, :, 1, AT + hd, :], q_t[:, hd, :].rearrange("p (t n) -> p t n", n=P),
                                   h[:, :, 0, AT + hd, :].bitcast(F32), ALU.subtract).then_inc(s.yb_lo, 1)
            for k in range(4, KT):
                wo_tile(k)

            def gate_lo(f):
                split_lo(wg_raw[:, :, :], wg_split[:, 0, :, :], wg_split[:, 1, :, :], s.wg_hi, f + 1, s.wg_lo)

            def up_lo(f):
                split_lo(wu_raw[:, :, :], wu_split[:, 0, :, :], wu_split[:, 1, :, :], s.wu_hi, f + 1, s.wu_lo)

            def down_tile(f, slot):
                pool.wait_ge(s.wd_raw_in, 16 * (f + 1))
                pool.wait_ge(s.gate_row_ready, 2)
                pool.tensor_tensor(wd_raw[:, :], wd_raw[:, :], gate2_row[:, :], ALU.mult).then_inc(s.wd_gated, 1)
                split_lo(wd_raw[:, :], wd_split[:, slot, 0, :], wd_split[:, slot, 1, :], s.wd_hi, f + 1, s.wd_lo)

            def act_lo(f, slot):
                pool.wait_ge(s.act_hi, f + 1)
                pool.tensor_tensor(act_split[:, slot, 1, :], cg[:, :], act_split[:, slot, 0, :].bitcast(F32),
                                   ALU.subtract).then_inc(s.act_lo, 1)

            gate_lo(0)
            up_lo(0)
            for tt in range(TT):
                split_lo(hf2[:, tt % 2, :, :], h[:, tt, 0, :, :], h[:, tt, 1, :, :],
                         s.norm_hi, N2 + tt + 1, s.norm_lo)

            def mlp_pair(i, last):
                for u in range(2):
                    f = 2 * i + u
                    more = not (last and u == 1)
                    if more:
                        gate_lo(f + 1)
                    down_tile(f, u)
                    act_lo(f, u)
                    if more:
                        up_lo(f + 1)

            with pool.Fori(0, FT // 2 - 1) as i:
                mlp_pair(i, False)
            mlp_pair(FT // 2 - 1, True)

        @block.scalar
        def _(act):
            def wait(sem, value):
                act.wait_ge(sem, value)
                if not isinstance(value, int):
                    act.sem_inc(s.act_past_wait, 1)

            def proj_hi(pos, j, free=None):
                slot = W_SLOT[pos]
                wait(raw_in(slot), 16 * use(pos, j))
                if free is not None:
                    wait(s.tile_mm, free)
                act.activation(w_split[:, slot, 0, :, :], w_raw[:, slot, :, :], ACT.Copy).then_inc(hi_done(slot), 1)

            wait(s.cols_ready, 1)
            act.activation(c_act[:, :], col_a[:, C_C:C_C + KT], ACT.Silu).then_inc(s.c_act_ready, 1)
            proj_hi(AX, 0)

            for tt in range(TT + 1):
                if tt < TT:
                    src = x_lo4[:, tt, :] if tt < 4 else x_hi4[:, tt - 4, :]
                    wait(x_in(tt), 16)
                    if tt >= 2:
                        wait(s.norm_turned, N1 + tt - 1)
                    act.activation(xn[:, tt % 2, :], src, ACT.Square,
                                   accum_out=ss[:, tt:tt + 1]).then_inc(s.norm_ss, 1)
                    wait(s.norm_inv, N1 + tt + 1)
                    act.activation(rstd[:, tt:tt + 1], var[:, tt:tt + 1], ACT.Sqrt).then_inc(s.norm_rstd, 1)
                if tt >= 1:
                    t = tt - 1
                    wait(s.norm_hf, N1 + t + 1)
                    act.activation(h[:, t, 0, :, :], hf[:, t % 2, :, :], ACT.Copy).then_inc(s.norm_hi, 1)

            wait(s.gates_in, 1)
            act.activation(tmp_g[:, :, :], tmp_g[:, :, :], ACT.Exp).then_inc(s.gate_act, 1)
            act.activation(beta[:, :, :], ba[:, :, 0:NH], ACT.Exp, scale=-1.0).then_inc(s.gate_act, 1)
            wait(s.gate_rows_in, 32)
            act.activation(gate_rows[:, 0, :], gate_rows[:, 0, :], ACT.Exp).then_inc(s.gate_act, 1)
            wait(s.gate_act, 1)
            act.activation(tmp_g[:, :, :], tmp_g[:, :, :], ACT.Ln, bias=one_col[:, 0:1]).then_inc(s.gate_act, 1)

            def tap(dst, src, weights, col, done):
                act.activation(dst, src, ACT.Copy, scale=weights[:, ds(col, 1)]).then_inc(done, 1)

            def inverse_norm(n, scale, bias):
                wait(s.stat_mm, n + 1)
                act.activation(sq[:, :], bank(4, 2), ACT.Ln, bias=eps_col[:, 0:1], scale=scale).then_inc(s.stat_ln, 1)
                wait(s.stat_ln, n + 1)
                if bias is None:
                    act.activation(sq[:, :], sq[:, :], ACT.Exp, scale=-0.5).then_inc(s.stat_rs, 1)
                else:
                    act.activation(sq[:, :], sq[:, :], ACT.Exp, scale=-0.5, bias=bias[:, 0:1]).then_inc(s.stat_rs, 1)

            def flat(store, j):
                return store[:, ds(j, 1), :].rearrange("p a n -> p (a n)")

            def proj_round(j, last):
                proj_hi(AC, j, j * NPOS)
                wait(s.tile_mm, j * NPOS + 1)
                act.activation(flat(a_t, j), bank(T_BANK[AX], 2), ACT.Copy).then_inc(s.ax_taken, 1)
                proj_hi(AB, j)
                wait(s.cx_ready, j + 1)
                tap(flat(a_t, j), cx[:, :], col_a, C_CA + 2 * AT + j, s.conv_tapped)
                proj_hi(Q, j)
                wait(s.ya_raw, j + 1)
                wait(s.k_norm, j)
                act.activation(sq[:, :], flat(a_t, j), ACT.Square).then_inc(s.sq_ready, 1)
                proj_hi(K, j, j * NPOS + 2)
                wait(s.tile_mm, j * NPOS + 4)
                tap(flat(q_t, j), bank(T_BANK[Q], 2), col_b, C_QKV + 3 * 3 * NH + j, s.conv_tapped)
                inverse_norm(3 * j, 1.0 / GROUP, None)
                proj_hi(V, j)
                wait(s.conv_step, 11 * j + 5)
                act.activation(flat(q_t, j), flat(q_t, j), ACT.Silu).then_inc(s.silu_done, 1)
                wait(s.silu_done, 3 * j + 1)
                wait(s.ya_norm, j + 1)
                act.activation(sq[:, :], flat(q_t, j), ACT.Square).then_inc(s.sq_ready, 1)
                wait(s.tile_mm, j * NPOS + 5)
                tap(flat(k_t, j), bank(T_BANK[K], 2), col_b, C_QKV + 3 * 3 * NH + NH + j, s.conv_tapped)
                inverse_norm(3 * j + 1, 1.0, qscale_col)
                proj_hi(Z, j)
                wait(s.conv_step, 11 * j + 8)
                act.activation(flat(k_t, j), flat(k_t, j), ACT.Silu).then_inc(s.silu_done, 1)
                wait(s.silu_done, 3 * j + 2)
                wait(s.q_norm, j + 1)
                act.activation(sq[:, :], flat(k_t, j), ACT.Square).then_inc(s.sq_ready, 1)
                wait(s.tile_mm, j * NPOS + 6)
                tap(flat(v_t, j), bank(T_BANK[V], 2), col_b, C_QKV + 3 * 3 * NH + 2 * NH + j, s.conv_tapped)
                inverse_norm(3 * j + 2, 1.0, None)
                if not last:
                    proj_hi(AX, j + 1)
                wait(s.conv_step, 11 * j + 11)
                act.activation(flat(v_t, j), flat(v_t, j), ACT.Silu).then_inc(s.silu_done, 1)
                wait(s.tile_mm, j * NPOS + 7)
                for half in range(2):
                    act.activation(flat(z_t, j)[:, half * BANK:(half + 1) * BANK], bank(T_BANK[Z] + half),
                                   ACT.Silu).then_inc(s.z_taken[half], 1)

            with act.Fori(0, NH - 1) as j:
                proj_round(j, False)
            proj_round(NH - 1, True)

            def dn_alone_start(n, slot):
                if not (isinstance(n, int) and n == 0):
                    wait(s.dn_m, n * (LEVELS - 1))
                    wait(s.dn_t0, n)
                    wait(s.dn_kg, n)
                    wait(s.dn_kt, n)
                else:
                    wait(s.gates_ready, 1)
                    wait(s.k_norm, NH)
                act.activation(gb_lt[:, :, :], g[:, ds(n, 1), :].rearrange("p a h -> p (a h)").unsqueeze(2)
                               .to_broadcast([P, NH, P]), ACT.Copy).then_inc(s.dn_gb, 1)
                act.activation(kc[:, :, :], k_t[:, :, ds(n * P, P)], ACT.Copy).then_inc(s.dn_kc, 1)
                wait(s.dn_cum, n + 1)
                if not (isinstance(n, int) and n == 0):
                    wait(s.dn_qd, n)
                    wait(s.dn_cd, n)
                act.activation(egb[:, :, :], bank(0, 1, P), ACT.Exp).then_inc(s.dn_egb, 1)
                wait(s.dn_diff, n + 1)
                act.activation(dec[:, :, :], dec[:, :, :], ACT.Exp).then_inc(s.dn_dec, 1)
                wait(s.dn_kdiff, n + 1)
                act.activation(kdec[:, :], kdec[:, :], ACT.Exp).then_inc(s.dn_kdec, 1)

            def dn_first_t(n):
                wait(s.dn_t1, n + 1)
                act.activation(tm[:, :, :], bank(4, 1, P), ACT.Copy).then_inc(s.dn_t1_copied, 1)

            def dn_level(n, lev):
                wait(s.dn_p, n * (LEVELS - 1) + lev)
                act.activation(pm[:, :, :], bank(1, 1, P), ACT.Copy).then_inc(s.dn_pm, 1)

            def dn_vc(n):
                if not (isinstance(n, int) and n == 0):
                    wait(s.dn_r, n)
                else:
                    wait(s.silu_done, 3 * NH)
                act.activation(vc[:, :, :], v_t[:, :, ds(n * P, P)], ACT.Copy).then_inc(s.dn_vc, 1)

            def dn_rr(n):
                wait(s.dn_r, n + 1)
                act.activation(rr[:, :, :], bank(5, 1, P), ACT.Copy).then_inc(s.dn_rr, 1)

            def dn_o(n):
                wait(s.dn_o, n + 1)
                act.activation(q_t[:, :, ds(n * P, P)], bank(7, 1, P), ACT.Copy).then_inc(s.dn_o_copied, 1)

            def dn_step(n, slot, alone, dep):
                if alone:
                    dn_alone_start(n, slot)
                if dep:
                    dn_rr(n - 1)
                    if alone:
                        dn_vc(n)
                if alone:
                    dn_first_t(n)
                    dn_level(n, 1)
                    dn_level(n, 2)
                if dep:
                    dn_o(n - 1)
                if alone:
                    for lev in range(3, LEVELS):
                        dn_level(n, lev)

            wait(s.tile_mm, NH * NPOS)
            wait(s.ada_mm, NH * 8)
            for slot in range(WSLOTS):
                wait(lo_done(slot), NH * USES[slot])
            dn_vc(0)
            dn_step(0, 0, True, False)
            with act.Fori(0, TT // 2 - 1) as i:
                dn_step(2 * i + 1, 1, True, True)
                act.activation(h[:, :, 0, ds(i, 1), :].rearrange("p t a n -> p (a t) n"),
                               a_t[:, ds(i, 1), :].rearrange("p a (t n) -> p (a t) n", n=P),
                               ACT.Copy).then_inc(s.ya_hi, 1)
                dn_step(2 * i + 2, 0, True, True)
            dn_step(TT - 1, 1, True, True)
            act.activation(h[:, :, 0, AT - 1, :], a_t[:, AT - 1, :].rearrange("p (t n) -> p t n", n=P),
                           ACT.Copy).then_inc(s.ya_hi, 1)
            dn_step(TT, 0, False, True)

            def wo_hi_part(k):
                wait(s.wo_gated, k + 1)
                act.activation(wo_part(k)[:, 0, :], wo_raw[:, k % 3, :], ACT.Copy).then_inc(s.wo_hi, 1)

            wait(s.gate_mm, 1)
            act.activation(gate_row[:, :], bank(2, 2), ACT.Copy).then_inc(s.gate_row_ready, 1)
            wait(s.dn_o_copied, TT)
            for hd in range(NH):
                if hd:
                    wait(s.yb_rs_used, hd)
                act.activation(osq[:, :], q_t[:, hd, :], ACT.Square).then_inc(s.osq_ready, 1)
                wo_hi_part(hd)
                wait(s.ostat_mm, hd + 1)
                act.activation(osq[:, :], bank(4, 2), ACT.Ln, bias=eps_col[:, 0:1], scale=1.0 / P).then_inc(s.ostat_ln, 1)
                wait(s.ostat_ln, hd + 1)
                act.activation(osq[:, :], osq[:, :], ACT.Exp, scale=-0.5).then_inc(s.ostat_rs, 1)
                wait(s.yb_ready, hd + 1)
                act.activation(h[:, :, 0, AT + hd, :], q_t[:, hd, :].rearrange("p (t n) -> p t n", n=P),
                               ACT.Copy).then_inc(s.yb_hi, 1)
            wait(s.yb_lo, NH)
            for k in range(4, KT):
                wo_hi_part(k)

            wait(s.out_a_mm, 1)
            wait(s.wg_raw_in, 16)
            act.activation(wg_split[:, 0, :, :], wg_raw[:, :, :], ACT.Copy).then_inc(s.wg_hi, 1)
            wait(s.wu_raw_in, 16)
            act.activation(wu_split[:, 0, :, :], wu_raw[:, :, :], ACT.Copy).then_inc(s.wu_hi, 1)
            wait(s.ya_lo, AT)
            for tt in range(TT + 1):
                if tt < TT:
                    wait(s.x2_out, 2 * TT + 2 * (tt + 1))
                    if tt >= 2:
                        wait(s.norm_turned, N2 + tt - 1)
                    act.activation(xn2[:, tt % 2, :], x2[:, tt, :], ACT.Square,
                                   accum_out=ss[:, tt:tt + 1]).then_inc(s.norm_ss, 1)
                    wait(s.norm_inv, N2 + tt + 1)
                    act.activation(rstd[:, tt:tt + 1], var[:, tt:tt + 1], ACT.Sqrt).then_inc(s.norm_rstd, 1)
                if tt >= 1:
                    t = tt - 1
                    wait(s.norm_hf, N2 + t + 1)
                    act.activation(h[:, t, 0, :, :], hf2[:, t % 2, :, :], ACT.Copy).then_inc(s.norm_hi, 1)
            wait(s.gate_mm, 2)
            act.activation(gate2_row[:, :], bank(2, 2), ACT.Copy).then_inc(s.gate_row_ready, 1)

            def mlp_pair(i, first, last):
                for u in range(2):
                    f = 2 * i + u
                    more = not (last and u == 1)
                    wait(s.gate_tile_mm, f + 1)
                    tap(cg[:, :], bank(0, 2), col_b, C_FF2 + f, s.ff_tapped)
                    if more:
                        wait(s.wg_raw_in, 16 * (f + 2))
                        act.activation(wg_split[:, 0, :, :], wg_raw[:, :, :], ACT.Copy).then_inc(s.wg_hi, 1)
                    wait(s.cg_conv, f + 1)
                    act.activation(cg[:, :], cg[:, :], ACT.Silu).then_inc(s.cg_silu, 1)
                    if u == 0 and not first:
                        wait(s.down_tile_mm, i * 2 * TT)
                    wait(s.wd_gated, f + 1)
                    act.activation(wd_split[:, u, 0, :], wd_raw[:, :], ACT.Copy).then_inc(s.wd_hi, 1)
                    wait(s.up_tile_mm, f + 1)
                    tap(cu[:, :], bank(2, 2), col_b, C_FF2 + FT + f, s.ff_tapped)
                    if more:
                        wait(s.wu_raw_in, 16 * (f + 2))
                        act.activation(wu_split[:, 0, :, :], wu_raw[:, :, :], ACT.Copy).then_inc(s.wu_hi, 1)
                    wait(s.act_ready, f + 1)
                    act.activation(act_split[:, u, 0, :], cg[:, :], ACT.Copy).then_inc(s.act_hi, 1)
                    wait(s.act_lo, f + 1)

            mlp_pair(0, True, False)
            with act.Fori(1, FT // 2 - 1) as i:
                mlp_pair(i, False, False)
            mlp_pair(FT // 2 - 1, False, True)

            for tt in range(TT):
                wait(s.x2_mlp, FT // 2 * 2 * TT - 2 * TT + 2 * (tt + 1))
                if tt:
                    wait(s.norm_ss, NF + tt)
                act.activation(cg[:, :], x2[:, tt, :], ACT.Square, accum_out=ss[:, tt:tt + 1]).then_inc(s.norm_ss, 1)
                wait(s.norm_inv, NF + tt + 1)
                act.activation(rstd[:, tt:tt + 1], var[:, tt:tt + 1], ACT.Sqrt).then_inc(s.norm_rstd, 1)

        @block.vector
        def _(dve):
            dve.wait_ge(s.rows_turned, 1)
            dve.tensor_copy(col_a[:, :], bank(0)[:, 0:NA_ROWS]).then_inc(s.cols_ready, 1)
            dve.tensor_copy(col_b[:, :], bank(0)[:, P:P + NB_ROWS]).then_inc(s.cols_ready, 1)
            dve.tensor_copy(col_c[:, :], bank(0)[:, 2 * P:2 * P + NC_ROWS]).then_inc(s.cols_ready, 1)

            def inverse_ms(tt, count):
                dve.wait_ge(s.norm_ss, count)
                dve.tensor_scalar(var[:, tt:tt + 1], ss[:, tt:tt + 1], 1.0 / D, EPS, ALU.mult,
                                  ALU.add).then_inc(s.norm_ms, 1)
                dve.wait_ge(s.norm_ms, count)
                dve.reciprocal(var[:, tt:tt + 1], var[:, tt:tt + 1]).then_inc(s.norm_inv, 1)

            def modulate(tt, first, dst, banks, scale, shift):
                dve.wait_ge(s.norm_turned, first + tt + 1)
                if tt >= 2:
                    dve.wait_ge(s.norm_lo, first + tt - 1)
                dve.tensor_tensor(dst[:, tt % 2, :, :], bank(banks + 2 * (tt % 2), 2, P),
                                  scale.unsqueeze(2).to_broadcast([P, KT, P]), ALU.mult).then_inc(s.norm_step, 1)
                dve.wait_ge(s.norm_step, first + tt + 1)
                dve.tensor_tensor(dst[:, tt % 2, :, :], dst[:, tt % 2, :, :],
                                  shift.unsqueeze(2).to_broadcast([P, KT, P]), ALU.add).then_inc(s.norm_hf, 1)

            for tt in range(TT + 1):
                if tt < TT:
                    src = x_lo4[:, tt, :] if tt < 4 else x_hi4[:, tt - 4, :]
                    inverse_ms(tt, N1 + tt + 1)
                    dve.wait_ge(s.norm_rstd, N1 + tt + 1)
                    dve.tensor_scalar(xn[:, tt % 2, :], src, rstd[:, tt:tt + 1], None,
                                      ALU.mult).then_inc(s.norm_xn, 1)
                if tt == 0:
                    dve.wait_ge(s.ada_first_mm, 1)
                    dve.tensor_tensor(mod[:, 0:2 * KT], bank(1)[:, 0:2 * KT],
                                      col_a[:, C_ADAB:C_ADAB + 2 * KT], ALU.add).then_inc(s.mod_step, 1)
                    dve.wait_ge(s.mod_step, 1)
                    dve.scalar_tensor_tensor(out=scale1[:, :], in0=mod[:, SC1:SC1 + KT], scalar=1.0,
                                             in1=col_a[:, C_N1:C_N1 + KT], op0=ALU.add,
                                             op1=ALU.mult).then_inc(s.mod_step, 1)
                    dve.wait_ge(s.mod_step, 2)
                if tt >= 1:
                    if tt >= 3:
                        dve.wait_ge(s.ba_mm, tt - 2)
                    modulate(tt - 1, N1, hf, 2, scale1[:, :], mod[:, SH1:SH1 + KT])

            dve.wait_ge(s.ba_mm, TT)
            dve.tensor_copy(ba[:, :, :], bank(7)[:, 0:TT * 2 * NH].rearrange("p (t n) -> p t n", n=2 * NH)
                            ).then_inc(s.gate_step, 1)
            dve.wait_ge(s.gate_step, 1)
            dve.wait_ge(s.gate_rows_in, 32)
            dve.tensor_tensor(ba[:, :, NH:2 * NH], ba[:, :, NH:2 * NH],
                              gate_rows[:, 1:2, :].to_broadcast([P, TT, NH]), ALU.add).then_inc(s.gate_step, 1)
            dve.wait_ge(s.gate_step, 2)
            dve.tensor_scalar(tmp_m[:, :, :], ba[:, :, NH:2 * NH], 0.0, None, ALU.max).then_inc(s.gate_step, 1)
            dve.scalar_tensor_tensor(out=tmp_g[:, :, :], in0=ba[:, :, NH:2 * NH], scalar=-1.0,
                                     in1=ba[:, :, NH:2 * NH], op0=ALU.mult, op1=ALU.min).then_inc(s.gates_in, 1)
            dve.wait_ge(s.gate_act, 4)
            dve.tensor_scalar(beta[:, :, :], beta[:, :, :], 1.0, None, ALU.add).then_inc(s.gate_step, 1)
            dve.tensor_tensor(tmp_g[:, :, :], tmp_g[:, :, :], tmp_m[:, :, :], ALU.add).then_inc(s.gate_step, 1)
            dve.wait_ge(s.gate_step, 4)
            dve.reciprocal(beta[:, :, :], beta[:, :, :]).then_inc(s.gate_step, 1)
            dve.wait_ge(s.gate_step, 5)
            dve.scalar_tensor_tensor(out=g[:, :, :], in0=tmp_g[:, :, :], scalar=-1.0,
                                     in1=gate_rows[:, 0:1, :].to_broadcast([P, TT, NH]), op0=ALU.mult,
                                     op1=ALU.mult).then_inc(s.gate_step, 1)
            dve.wait_ge(s.gate_step, 6)
            dve.tensor_scalar(neg_dn_w[:, :], col_a[:, C_DN:C_DN + 1], -1.0, None, ALU.mult).then_inc(s.gate_step, 1)
            dve.wait_ge(s.gate_step, 7)
            dve.tensor_scalar(neg_beta[:, :, :], beta[:, :, :], -1.0, None, ALU.mult).then_inc(s.gates_ready, 1)

            def flat(store, j):
                return store[:, ds(j, 1), :].rearrange("p a n -> p (a n)")

            def conv_tap(dst, src, weight, lag, done):
                dve.scalar_tensor_tensor(out=dst[:, lag:L], in0=src[:, 0:L - lag], scalar=weight,
                                         in1=dst[:, lag:L], op0=ALU.mult, op1=ALU.add).then_inc(done, 1)

            def conv4(j, dst, src, kind):
                col = C_QKV + kind * NH + j
                steps = 11 * j + 2 + 3 * kind
                dve.wait_ge(s.conv_tapped, 4 * j + 2 + kind)
                conv_tap(dst, src, col_b[:, ds(col + 2 * 3 * NH, 1)], 1, s.conv_step)
                dve.wait_ge(s.conv_step, steps + 1)
                conv_tap(dst, src, col_b[:, ds(col + 3 * NH, 1)], 2, s.conv_step)
                dve.wait_ge(s.conv_step, steps + 2)
                conv_tap(dst, src, col_b[:, ds(col, 1)], 3, s.conv_step)

            def proj_round(j):
                dve.wait_ge(s.ax_taken, j + 1)
                dve.wait_ge(s.tile_mm, j * NPOS + 2)
                dve.tensor_tensor(cx[:, :], bank(T_BANK[AC], 2), flat(a_t, j), ALU.mult).then_inc(s.cx_ready, 1)
                dve.wait_ge(s.conv_tapped, 4 * j + 1)
                conv_tap(flat(a_t, j), cx[:, :], col_a[:, ds(C_CA + AT + j, 1)], 1, s.conv_step)
                dve.wait_ge(s.conv_step, 11 * j + 1)
                conv_tap(flat(a_t, j), cx[:, :], col_a[:, ds(C_CA + j, 1)], 2, s.conv_step)
                dve.wait_ge(s.conv_step, 11 * j + 2)
                dve.wait_ge(s.tile_mm, j * NPOS + 3)
                dve.tensor_tensor(flat(a_t, j), bank(T_BANK[AB], 2), flat(a_t, j), ALU.mult).then_inc(s.ya_raw, 1)
                conv4(j, flat(q_t, j), bank(T_BANK[Q], 2), 0)
                dve.wait_ge(s.stat_rs, 3 * j + 1)
                dve.scalar_tensor_tensor(out=flat(a_t, j), in0=flat(a_t, j), scalar=col_a[:, ds(C_NA + j, 1)],
                                         in1=sq[:, :], op0=ALU.mult, op1=ALU.mult).then_inc(s.ya_norm, 1)
                conv4(j, flat(k_t, j), bank(T_BANK[K], 2), 1)
                dve.wait_ge(s.stat_rs, 3 * j + 2)
                dve.tensor_tensor(flat(q_t, j), flat(q_t, j), sq[:, :], ALU.mult).then_inc(s.q_norm, 1)
                conv4(j, flat(v_t, j), bank(T_BANK[V], 2), 2)
                dve.wait_ge(s.stat_rs, 3 * j + 3)
                dve.tensor_tensor(flat(k_t, j), flat(k_t, j), sq[:, :], ALU.mult).then_inc(s.k_norm, 1)
                dve.wait_ge(s.ada_mm, 8 * j + 8)
                dve.tensor_tensor(mod[:, ds(GT1 + j * 8, 8)], bank(6)[:, 0:8],
                                  col_a[:, ds(C_ADAB + GT1 + j * 8, 8)], ALU.add).then_inc(s.mod_taken, 1)

            with dve.Fori(0, NH) as j:
                proj_round(j)
            dve.wait_ge(s.mod_taken, NH)
            dve.scalar_tensor_tensor(out=scale2[:, :], in0=mod[:, SC2:SC2 + KT], scalar=1.0,
                                     in1=col_a[:, C_N2:C_N2 + KT], op0=ALU.add,
                                     op1=ALU.mult).then_inc(s.mod_step, 1)

            def by_head(t):
                return t.unsqueeze(2).to_broadcast([P, NH, P])

            def chunk_cols(t, n):
                return t[:, ds(n, 1), :].rearrange("p a h -> p (a h)")

            def all_heads(t):
                return t[:, :].unsqueeze(1).to_broadcast([P, NH, P])

            def dn_alone_start(n, slot):
                dve.wait_ge(s.dn_egb, n + 1)
                if not (isinstance(n, int) and n == 0):
                    dve.wait_ge(s.dn_t2, n * (LEVELS - 1))
                dve.tensor_tensor(pm[:, :, :], bank(0, 1, P), all_heads(ident), ALU.mult).then_inc(s.dn_g_step, 1)
                dve.wait_ge(s.dn_g_step, 2 * n + 1)
                dve.tensor_reduce(gc[:, :], pm[:, :, :], AX_X, ALU.add).then_inc(s.dn_g_step, 1)
                dve.wait_ge(s.dn_g_step, 2 * n + 2)
                dve.tensor_tensor(dec[:, :, :], bank(0, 1, P), by_head(gc[:, :]), ALU.subtract).then_inc(s.dn_d_step, 1)
                dve.wait_ge(s.dn_d_step, n + 1)
                dve.tensor_scalar(dec[:, :, :], dec[:, :, :], 0.0, None, ALU.min).then_inc(s.dn_diff, 1)
                dve.tensor_tensor(kdec[:, :], bank(0, 1, P)[:, :, P - 1], gc[:, :], ALU.subtract).then_inc(s.dn_kdiff, 1)
                dve.tensor_copy(cdec[:, slot, :], egb[:, :, P - 1]).then_inc(s.dn_cd, 1)
                dve.wait_ge(s.dn_dec, n + 1)
                dve.tensor_tensor(dec[:, :, :], dec[:, :, :], all_heads(causal), ALU.mult).then_inc(s.dn_masked, 1)
                dve.wait_ge(s.dn_masked, n + 1)
                dve.wait_ge(s.dn_kt, n + 1)
                if not (isinstance(n, int) and n == 0):
                    dve.wait_ge(s.dn_o, n - 1)
                dve.tensor_tensor(gb_lt[:, :, :], bank(1, 1, P), dec[:, :, :], ALU.mult).then_inc(s.dn_l_step, 1)
                dve.tensor_tensor(att[:, slot, :, :], bank(2, 1, P), dec[:, :, :], ALU.mult).then_inc(s.dn_att, 1)
                dve.wait_ge(s.dn_l_step, n + 1)
                dve.tensor_tensor(gb_lt[:, :, :], gb_lt[:, :, :], by_head(chunk_cols(beta, n)), ALU.mult).then_inc(s.dn_lt, 1)
                dve.wait_ge(s.dn_lt, n + 1)
                dve.tensor_tensor(pm[:, :, :], gb_lt[:, :, :],
                                  level_mask[:, 0:1, :].to_broadcast([P, NH, P]), ALU.mult).then_inc(s.dn_t0, 1)
                dve.wait_ge(s.dn_t0, n + 1)
                if not (isinstance(n, int) and n == 0):
                    dve.wait_ge(s.dn_v, n - 1)
                dve.tensor_tensor(um[:, slot, :, :], all_heads(ident), pm[:, :, :], ALU.subtract).then_inc(s.dn_u, 1)
                dve.wait_ge(s.dn_kdec, n + 1)
                if not (isinstance(n, int) and n == 0):
                    dve.wait_ge(s.dn_s, n - 1)
                dve.tensor_tensor(kd[:, slot, :, :], bank(3, 1, P), by_head(kdec[:, :]), ALU.mult).then_inc(s.dn_kd, 1)

            def dn_level(n, slot, lev):
                if lev < LEVELS - 1:
                    dve.wait_ge(s.dn_tt, n * (LEVELS - 2) + lev)
                    dve.tensor_tensor(tm[:, :, :], tm[:, :, :], bank(2, 1, P), ALU.subtract).then_inc(s.dn_tm, 1)
                dve.wait_ge(s.dn_t2, n * (LEVELS - 1) + lev)
                dve.tensor_tensor(um[:, slot, :, :], um[:, slot, :, :], bank(3, 1, P), ALU.subtract).then_inc(s.dn_u, 1)

            def dn_v(n):
                dve.wait_ge(s.dn_v, n + 1)
                if not (isinstance(n, int) and n == 0):
                    dve.wait_ge(s.dn_s, n)
                dve.tensor_tensor(vn[:, :, :], bank(6, 1, P), by_head(chunk_cols(neg_beta, n)), ALU.mult).then_inc(s.dn_vn, 1)

            def dn_s(n, slot):
                dve.wait_ge(s.dn_s, n + 1)
                for hd in range(NH):
                    dve.scalar_tensor_tensor(out=st[:, hd, :], in0=st[:, hd, :], scalar=cdec[:, slot, hd:hd + 1],
                                             in1=bank(5, 1, P)[:, hd, :], op0=ALU.mult,
                                             op1=ALU.add).then_inc(s.dn_st, 1)

            def dn_step(n, slot, alone, dep):
                if alone:
                    dn_alone_start(n, slot)
                    dn_level(n, slot, 1)
                if dep:
                    dn_v(n - 1)
                if alone:
                    dn_level(n, slot, 2)
                if dep:
                    dn_s(n - 1, 1 - slot)
                if alone:
                    for lev in range(3, LEVELS):
                        dn_level(n, slot, lev)

            dve.wait_ge(s.tile_mm, NH * NPOS)
            dve.memset(st[:, :, :], 0.0).then_inc(s.dn_st, NH)
            dn_step(0, 0, True, False)
            with dve.Fori(0, TT // 2 - 1) as i:
                dn_step(2 * i + 1, 1, True, True)
                dn_step(2 * i + 2, 0, True, True)
            dn_step(TT - 1, 1, True, True)
            dn_step(TT, 0, False, True)

            dve.wait_ge(s.dn_o_copied, TT)
            dve.wait_ge(s.dn_st, NH * (TT + 1))
            dve.sem_inc(s.dn_over, 1)

            def gate_diag(first_col):
                for k in range(KT):
                    dve.tensor_scalar(diag[:, k, :], ident[:, :], mod[:, first_col + k:first_col + k + 1], None,
                                      ALU.mult).then_inc(s.diag_ready, 1)

            gate_diag(GT1)

            for hd in range(NH):
                dve.wait_ge(s.ostat_rs, hd + 1)
                dve.scalar_tensor_tensor(out=q_t[:, hd, :], in0=q_t[:, hd, :], scalar=neg_dn_w[:, 0:1],
                                         in1=osq[:, :], op0=ALU.mult, op1=ALU.mult).then_inc(s.yb_rs_used, 1)
                dve.wait_ge(s.yb_rs_used, hd + 1)
                dve.tensor_tensor(q_t[:, hd, :], q_t[:, hd, :], z_t[:, hd, :], ALU.mult).then_inc(s.yb_ready, 1)

            def drain_out(n):
                tt, half = n % (2 * TT) // 2, n % 2
                dve.wait_ge(s.out_mm, n + 1)
                if n < 2 * TT:
                    dve.wait_ge(x_in(tt), 32)
                else:
                    dve.wait_ge(s.x2_out, n - 2 * TT + 1)
                piece = x2[:, tt, half * BANK:(half + 1) * BANK]
                dve.tensor_tensor(piece, piece, bank(n % 4 if n < 2 * TT else n % 2), ALU.add).then_inc(s.x2_out, 1)

            def norm2_rows(tt):
                inverse_ms(tt, N2 + tt + 1)
                dve.wait_ge(s.norm_rstd, N2 + tt + 1)
                dve.tensor_scalar(xn2[:, tt % 2, :], x2[:, tt, :], rstd[:, tt:tt + 1], None,
                                  ALU.mult).then_inc(s.norm_xn, 1)

            def norm2_modulate(tt):
                modulate(tt, N2, hf2, 4, scale2[:, :], mod[:, SH2:SH2 + KT])

            for n in range(2 * TT):
                drain_out(n)
            for tt in range(TT):
                drain_out(2 * TT + 2 * tt)
                drain_out(2 * TT + 2 * tt + 1)
                if tt >= 1:
                    norm2_rows(tt - 1)
                if tt >= 2:
                    norm2_modulate(tt - 2)
            norm2_rows(TT - 1)
            norm2_modulate(TT - 2)
            dve.wait_ge(s.gate_mm, 1)
            gate_diag(GT2)
            norm2_modulate(TT - 1)

            def conv3(f, dst, src, first_col, tapped, step, done):
                dve.wait_ge(s.ff_tapped, tapped)
                conv_tap(dst, src, col_c[:, ds(2 * FT + first_col + f, 1)], 1, step)
                dve.wait_ge(step, f + 1)
                conv_tap(dst, src, col_c[:, ds(first_col + f, 1)], 2, done)

            def drain_down(i):
                for n in range(2 * TT):
                    tt, half = n // 2, n % 2
                    dve.wait_ge(s.down_tile_mm, i * 2 * TT + n + 1)
                    piece = x2[:, tt, half * BANK:(half + 1) * BANK]
                    dve.tensor_tensor(piece, piece, bank(4 + n % 4), ALU.add).then_inc(s.x2_mlp, 1)

            def mlp_pair(i, first):
                for u in range(2):
                    f = 2 * i + u
                    conv3(f, cg[:, :], bank(0, 2), 0, 2 * f + 1, s.cg_step, s.cg_conv)
                    if u == 0 and not first:
                        drain_down(i - 1)
                    conv3(f, cu[:, :], bank(2, 2), FT, 2 * f + 2, s.cu_step, s.cu_conv)
                    dve.wait_ge(s.cg_silu, f + 1)
                    dve.wait_ge(s.cu_conv, f + 1)
                    dve.tensor_tensor(cg[:, :], cg[:, :], cu[:, :], ALU.mult).then_inc(s.act_ready, 1)

            mlp_pair(0, True)
            with dve.Fori(1, FT // 2) as i:
                mlp_pair(i, False)

            def final_rows(tt):
                inverse_ms(tt, NF + tt + 1)
                dve.wait_ge(s.norm_rstd, NF + tt + 1)
                dve.wait_ge(s.normf_in, 16)
                dve.scalar_tensor_tensor(out=x2[:, tt, :], in0=x2[:, tt, :], scalar=rstd[:, tt:tt + 1],
                                         in1=normf_row[:, :], op0=ALU.mult, op1=ALU.mult).then_inc(s.y_ready, 1)

            i = FT // 2 - 1
            for n in range(2 * TT):
                tt, half = n // 2, n % 2
                dve.wait_ge(s.down_tile_mm, i * 2 * TT + n + 1)
                piece = x2[:, tt, half * BANK:(half + 1) * BANK]
                dve.tensor_tensor(piece, piece, bank(4 + n % 4), ALU.add).then_inc(s.x2_mlp, 1)
                if half and tt:
                    final_rows(tt - 1)
            final_rows(TT - 1)

        @block.tensor
        def _(pe):
            def three_pass(dst, pairs):
                last = None
                for n, (a_hi, a_lo, b_hi, b_lo) in enumerate(pairs):
                    pe.matmul(dst, a_hi, b_hi, start=(n == 0), stop=False)
                    pe.matmul(dst, a_hi, b_lo, start=False, stop=False)
                    last = pe.matmul(dst, a_lo, b_hi, start=False, stop=(n == len(pairs) - 1))
                return last

            def h_half(part, k, half):
                return h[:, half * (TT // 2):(half + 1) * (TT // 2), part, k, :]

            pe.wait_ge(s.consts_ready, 1)
            pe.wait_ge(s.rows_in, 160)
            pe.transpose(bank(0)[:, 0:NA_ROWS], rows_a[0:NA_ROWS, :], ident[0:NA_ROWS, 0:NA_ROWS])
            pe.transpose(bank(0)[:, P:P + NB_ROWS], rows_b[0:NB_ROWS, :], ident[0:NB_ROWS, 0:NB_ROWS])
            pe.transpose(bank(0)[:, 2 * P:2 * P + NC_ROWS], rows_c[0:NC_ROWS, :],
                         ident[0:NC_ROWS, 0:NC_ROWS]).then_inc(s.rows_turned, 1)

            pe.wait_ge(s.c_act_ready, 1)
            for blk in range(2 * KT):
                pe.wait_ge(s.ada_first_in[blk // 4], 16)
                for k in range(KT):
                    mm = pe.matmul(bank(1)[:, blk:blk + 1], ada_first[blk // 4][:, k, blk % 4 * P:(blk % 4 + 1) * P],
                                   c_act[:, k:k + 1], start=(k == 0), stop=(k == KT - 1))
            mm.then_inc(s.ada_first_mm, 1)

            def turn(tt, first, src, first_bank):
                pe.wait_ge(s.norm_xn, first + tt + 1)
                if tt >= 2:
                    pe.wait_ge(s.norm_step, first + tt - 1)
                for k in range(KT):
                    mm = pe.transpose(bank(first_bank + 2 * (tt % 2), 2, P)[:, k, :],
                                      src[:, tt % 2, k * P:(k + 1) * P], ident[:, :])
                mm.then_inc(s.norm_turned, 1)

            def beta_alpha(tt):
                pe.wait_ge(s.norm_hf, N1 + tt + 1)
                if tt == 0:
                    pe.wait_ge(s.w_ba_in, 16)
                for k in range(KT):
                    mm = pe.matmul(bank(7)[:, tt * 2 * NH:(tt + 1) * 2 * NH], hf[:, tt % 2, k, :], w_ba[:, k, :],
                                   start=(k == 0), stop=(k == KT - 1))
                mm.then_inc(s.ba_mm, 1)

            for tt in range(TT + 1):
                if tt < TT:
                    turn(tt, N1, xn, 2)
                if tt >= 1:
                    beta_alpha(tt - 1)

            def proj_tile(pos, j, free):
                slot = W_SLOT[pos]
                pe.wait_ge(lo_done(slot), use(pos, j))
                for half in range(2):
                    pe.wait_ge(*free[half])
                    mm = three_pass(bank(T_BANK[pos] + half),
                                    [(w_split[:, slot, 0, k, :], w_split[:, slot, 1, k, :],
                                      h_half(0, k, half), h_half(1, k, half)) for k in range(KT)])
                mm.then_inc(s.tile_mm, 1)

            def statistic(n, weights):
                pe.wait_ge(s.sq_ready, n + 1)
                pe.wait_ge(s.stat_ln, n)
                for half in range(2):
                    mm = pe.matmul(bank(4 + half), weights[:, :], sq[:, half * BANK:(half + 1) * BANK],
                                   start=True, stop=True)
                mm.then_inc(s.stat_mm, 1)

            def ada_block(b, j):
                pe.wait_ge(s.ada_in[b % 2], 16 * (4 * j + b // 2 + 1))
                if b == 0:
                    pe.wait_ge(s.mod_taken, j)
                for k in range(KT):
                    mm = pe.matmul(bank(6)[:, b:b + 1], ada_raw[:, b % 2, k, :], c_act[:, k:k + 1],
                                   start=(k == 0), stop=(k == KT - 1))
                mm.then_inc(s.ada_mm, 1)

            def proj_round(j):
                def ada(pos):
                    for b in ADA_AFTER[pos]:
                        ada_block(b, j)

                proj_tile(AX, j, [(s.z_taken[0], j), (s.z_taken[1], j)])
                ada(AX)
                proj_tile(AC, j, [(s.conv_step, 11 * j)] * 2)
                ada(AC)
                proj_tile(AB, j, [(s.ax_taken, j + 1)] * 2)
                ada(AB)
                proj_tile(Q, j, [(s.cx_ready, j + 1)] * 2)
                statistic(3 * j, group_ones)
                ada(Q)
                proj_tile(K, j, [(s.ya_raw, j + 1)] * 2)
                statistic(3 * j + 1, ones)
                ada(K)
                proj_tile(V, j, [(s.conv_step, 11 * j + 5)] * 2)
                statistic(3 * j + 2, ones)
                ada(V)
                proj_tile(Z, j, [(s.conv_step, 11 * j + 8)] * 2)
                ada(Z)

            pe.wait_ge(s.norm_lo, N1 + TT)
            with pe.Fori(0, NH) as j:
                proj_round(j)

            def heads(dst, a, b, done=None, n=1):
                for hd in range(NH):
                    mm = pe.matmul(dst[:, hd, :], a[:, hd, :], b[:, hd, :], start=True, stop=True)
                if done is not None:
                    mm.then_inc(done, n)

            def dn_alone_start(n):
                pe.wait_ge(s.dn_gb, n + 1)
                if not (isinstance(n, int) and n == 0):
                    pe.wait_ge(s.dn_kdiff, n)
                else:
                    pe.wait_ge(s.z_taken[1], NH)
                for hd in range(NH):
                    mm = pe.matmul(bank(0, 1, P)[:, hd, :], gb_lt[:, hd, :], causal[:, :], start=True, stop=True)
                mm.then_inc(s.dn_cum, 1)
                pe.wait_ge(s.dn_kc, n + 1)
                pe.wait_ge(s.dn_u, n * LEVELS)
                if isinstance(n, int) and n == 0:
                    pe.wait_ge(s.conv_step, 11 * NH)
                heads(bank(1, 1, P), kc, kc)
                heads(bank(2, 1, P), kc, q_t[:, :, ds(n * P, P)])
                for hd in range(NH):
                    mm = pe.transpose(bank(3, 1, P)[:, hd, :], kc[:, hd, :], ident[:, :])
                mm.then_inc(s.dn_kt, 1)

            def dn_first_t(n, slot):
                pe.wait_ge(s.dn_u, n * LEVELS + 1)
                if not (isinstance(n, int) and n == 0):
                    pe.wait_ge(s.dn_t1_copied, n)
                for hd in range(NH):
                    mm = pe.transpose(bank(4, 1, P)[:, hd, :], um[:, slot, hd, :], ident[:, :])
                mm.then_inc(s.dn_t1, 1)

            def dn_level(n, slot, lev):
                pe.wait_ge(s.dn_m, n * (LEVELS - 1) + lev)
                if lev == 1:
                    pe.wait_ge(s.dn_t1_copied, n + 1)
                    pe.wait_ge(s.dn_l_step, n + 1)
                    pe.wait_ge(s.dn_kd, n + 1)
                else:
                    pe.wait_ge(s.dn_tm, n * (LEVELS - 2) + lev - 1)
                heads(bank(1, 1, P), mlev[:, lev - 1, :, :], tm, s.dn_p)
                pe.wait_ge(s.dn_pm, n * (LEVELS - 1) + lev)
                pe.wait_ge(s.dn_u, n * LEVELS + lev)
                if lev < LEVELS - 1:
                    heads(bank(2, 1, P), um[:, slot, :, :], pm, s.dn_tt)
                heads(bank(3, 1, P), pm, um[:, slot, :, :], s.dn_t2)

            def dn_r(n, slot):
                pe.wait_ge(s.dn_vc, n + 1)
                pe.wait_ge(s.dn_kg, n + 1)
                pe.wait_ge(s.dn_st, NH * (n + 1))
                for hd in range(NH):
                    pe.matmul(bank(5, 1, P)[:, hd, :], vc[:, hd, :], ident[:, :], start=True, stop=False)
                    mm = pe.matmul(bank(5, 1, P)[:, hd, :], kg[:, slot, hd, :], st[:, hd, :], start=False, stop=True)
                mm.then_inc(s.dn_r, 1)

            def dn_v(n, slot):
                pe.wait_ge(s.dn_rr, n + 1)
                pe.wait_ge(s.dn_vn, n)
                pe.wait_ge(s.dn_u, (n + 1) * LEVELS)
                heads(bank(6, 1, P), um[:, slot, :, :], rr, s.dn_v)

            def dn_o_s(n, slot):
                pe.wait_ge(s.dn_vn, n + 1)
                pe.wait_ge(s.dn_att, n + 1)
                pe.wait_ge(s.dn_qd, n + 1)
                pe.wait_ge(s.dn_o_copied, n)
                for hd in range(NH):
                    pe.matmul(bank(7, 1, P)[:, hd, :], st[:, hd, :], qd[:, slot, hd, :], start=True, stop=False)
                    mm = pe.matmul(bank(7, 1, P)[:, hd, :], vn[:, hd, :], att[:, slot, hd, :], start=False, stop=True)
                mm.then_inc(s.dn_o, 1)
                pe.wait_ge(s.dn_kd, n + 1)
                heads(bank(5, 1, P), kd[:, slot, :, :], vn, s.dn_s)

            def dn_step(n, slot, alone, dep):
                if alone:
                    dn_alone_start(n)
                if dep:
                    dn_r(n - 1, 1 - slot)
                if alone:
                    dn_first_t(n, slot)
                    dn_level(n, slot, 1)
                if dep:
                    dn_v(n - 1, 1 - slot)
                if alone:
                    dn_level(n, slot, 2)
                if dep:
                    dn_o_s(n - 1, 1 - slot)
                if alone:
                    for lev in range(3, LEVELS):
                        dn_level(n, slot, lev)

            dn_step(0, 0, True, False)
            with pe.Fori(0, TT // 2 - 1) as i:
                dn_step(2 * i + 1, 1, True, True)
                dn_step(2 * i + 2, 0, True, True)
            dn_step(TT - 1, 1, True, True)
            dn_step(TT, 0, False, True)

            def gate_row_mm(n):
                pe.wait_ge(s.diag_ready, KT * n)
                for half in range(2):
                    mm = pe.matmul(bank(2 + half), ones[:, :],
                                   diag[:, half * 4:half * 4 + 4, :], start=True, stop=True)
                mm.then_inc(s.gate_mm, 1)

            def out_tile(n):
                group, tt, half = n // (2 * TT), n % (2 * TT) // 2, n % 2
                if group == 0:
                    if n >= 4:
                        pe.wait_ge(s.x2_out, n - 3)
                else:
                    pe.wait_ge(s.x2_out, n - 1)
                if n % (2 * TT) == 0:
                    pe.wait_ge(s.wo_lo, 4 * (group + 1))
                    pe.wait_ge(*((s.ya_lo, AT) if group == 0 else (s.yb_lo, NH)))
                dst = bank(n % 4 if group == 0 else n % 2)
                cols = slice(half * BANK, (half + 1) * BANK)
                mm = three_pass(dst, [(h[:, tt, 0, k, :], h[:, tt, 1, k, :], wo_part(k)[:, 0, cols],
                                       wo_part(k)[:, 1, cols]) for k in range(4 * group, 4 * group + 4)])
                mm.then_inc(s.out_mm, 1)

            gate_row_mm(1)
            pe.wait_ge(s.gate_row_ready, 1)

            def out_stat(hd):
                pe.wait_ge(s.osq_ready, hd + 1)
                pe.wait_ge(s.ostat_ln, hd)
                for half in range(2):
                    mm = pe.matmul(bank(4 + half), ones[:, :], osq[:, half * BANK:(half + 1) * BANK],
                                   start=True, stop=True)
                mm.then_inc(s.ostat_mm, 1)

            for hd in range(NH):
                out_stat(hd)
            for n in range(2 * TT):
                out_tile(n)
            pe.wait_ge(s.out_mm, 2 * TT)
            pe.sem_inc(s.out_a_mm, 1)
            for tt in range(TT):
                out_tile(2 * TT + 2 * tt)
                out_tile(2 * TT + 2 * tt + 1)
                if tt >= 2:
                    turn(tt - 2, N2, xn2, 4)
            turn(TT - 2, N2, xn2, 4)
            turn(TT - 1, N2, xn2, 4)
            gate_row_mm(2)

            def wide_tile(w, first_bank, frees, mm_done, chunks=None):
                for half in range(2):
                    for sem, value in frees[half]:
                        pe.wait_ge(sem, value)
                    mm = three_pass(bank(first_bank + half),
                                    [(w[:, 0, k, :], w[:, 1, k, :], h_half(0, k, half), h_half(1, k, half))
                                     for k in range(KT)])
                mm.then_inc(mm_done, 1)

            def down(i):
                pe.wait_ge(s.act_lo, 2 * i + 2)
                pe.wait_ge(s.wd_lo, 2 * i + 2)
                for n in range(2 * TT):
                    tt, half = n // 2, n % 2
                    if n >= 4:
                        pe.wait_ge(s.x2_mlp, i * 2 * TT + n - 3)
                    elif isinstance(i, int) and i == 0:
                        pe.wait_ge(s.norm_step, N2 + TT)
                    else:
                        pe.wait_ge(s.x2_mlp, i * 2 * TT)
                    toks = slice(tt * P, (tt + 1) * P)
                    cols = slice(half * BANK, (half + 1) * BANK)
                    mm = three_pass(bank(4 + n % 4),
                                    [(act_split[:, u, 0, toks], act_split[:, u, 1, toks],
                                      wd_split[:, u, 0, cols], wd_split[:, u, 1, cols]) for u in range(2)])
                    mm.then_inc(s.down_tile_mm, 1)

            def gate_tile(f, frees):
                pe.wait_ge(s.wg_lo, f + 1)
                wide_tile(wg_split, 0, frees, s.gate_tile_mm)

            def up_tile(f, frees):
                pe.wait_ge(s.wu_lo, f + 1)
                wide_tile(wu_split, 2, frees, s.up_tile_mm)

            def mlp_pair(i, first):
                for u in range(2):
                    f = 2 * i + u
                    if first and u == 0:
                        gate_tile(f, [[(s.norm_lo, N2 + TT // 2), (s.x2_out, 4 * TT)], [(s.norm_lo, N2 + TT)]])
                    else:
                        gate_tile(f, [[(s.cg_conv, f)]] * 2)
                    if u == 0 and not first:
                        down(i - 1)
                    if first and u == 0:
                        up_tile(f, [[(s.gate_row_ready, 2)]] * 2)
                    else:
                        up_tile(f, [[(s.cu_conv, f)]] * 2)

            mlp_pair(0, True)
            with pe.Fori(1, FT // 2) as i:
                mlp_pair(i, False)
            down(FT // 2 - 1)


_INS = ['x', 'c', 'ada_w', 'ada_b', 'norm1_w', 'w_in', 'conv_a_w', 'norm_a_w', 'conv_qkv_w', 'a_log',
        'dt_bias', 'norm_dn_w', 'w_out', 'norm2_w', 'w_up', 'conv_ff_w', 'w_down', 'norm_f_w']


def kernel(**inputs):
    import numpy as _np
    import concourse.bacc as _bacc
    from concourse import mybir as _mybir
    from concourse.bass_utils import run_bass_kernel_spmd as _run

    nc = _bacc.Bacc("TRN2", target_bir_lowering=False, num_devices=1)
    arrays, args = {}, []
    for name in _INS:
        a = _np.ascontiguousarray(inputs[name])
        arrays[f"in_{name}_dram"] = a
        args.append(nc.dram_tensor(f"in_{name}_dram", a.shape, _mybir.dt.from_np(a.dtype), kind="ExternalInput").ap())
    shape = inputs['x'].shape
    args.append(nc.dram_tensor("out_0_dram", shape, _mybir.dt.float32, kind="ExternalOutput").ap())
    build_program(nc, *args)
    r = _run(nc, [arrays], core_ids=[0])
    return r.results[0]["out_0_dram"]
```

```python
import math
from contextlib import ExitStack

import concourse.bass as bass
from concourse import mybir

F32 = mybir.dt.float32
F32R = mybir.dt.float32r
ALU = mybir.AluOpType
ACT = mybir.ActivationFunctionType
AX_X = mybir.AxisListType.X

P = 128
KIB = 1024
BANK = 512


def ds(start, n):
    return bass.ds(start, n)


def build_program(nc, x, c, ada_w, ada_b, norm1_w, w_in, conv_a_w, norm_a_w, conv_qkv_w, a_log,
                  dt_bias, norm_dn_w, w_out, norm2_w, w_up, conv_ff_w, w_down, norm_f_w, out):
    L, D = x.shape[1], x.shape[2]
    DFF = w_down.shape[1]
    AW = conv_a_w.shape[2]
    DNW = conv_qkv_w.shape[2] // 3
    NH = a_log.shape[1]
    KT = D // P
    TT = L // P
    AT = AW // P
    FT = DFF // P
    NMOD = ada_b.shape[1] // D
    EPS = 1e-6
    GROUP = 64
    LEVELS = 7
    assert (L, D, AT, NH, DNW) == (1024, 1024, 4, 4, NH * P) and FT % 2 == 0

    ctx = ExitStack()
    with ctx:
        base = 16512 + 64

        def sb(name, offset, shape, dt=F32):
            return nc.alloc_sbuf_tensor_at(name, [P] + shape, dt, offset=offset)

        o_h = base
        o_q, o_k, o_v, o_z = (base + (64 + 16 * n) * KIB for n in range(4))
        o_a = base + 128 * KIB
        o_w = base + 144 * KIB
        o_c = base + 200 * KIB

        h = sb("h", o_h, [TT, 2, KT, P], F32R)
        q_t = sb("q_t", o_q, [NH, L])
        k_t = sb("k_t", o_k, [NH, L])
        v_t = sb("v_t", o_v, [NH, L])
        z_t = sb("z_t", o_z, [NH, L])
        a_t = sb("a_t", o_a, [AT, L])

        cursor = [o_c]

        def small(name, shape, dt=F32):
            n = 4 * math.prod(shape)
            t = sb(name, cursor[0], shape, dt)
            cursor[0] += (n + 31) // 32 * 32
            assert cursor[0] <= 229344, cursor
            return t

        ident = small("ident", [P])
        ones = small("ones", [P])
        causal = small("causal", [P])
        group_ones = small("group_ones", [P])
        level_mask = sb("level_mask", o_w + 52 * KIB, [LEVELS, P])
        NA_ROWS = KT * 3 + NMOD * KT + AT + 1 + 3 * AT
        NB_ROWS = 4 * 3 * NH + 2 * FT
        NC_ROWS = 2 * 2 * FT
        col_a = small("col_a", [NA_ROWS])
        col_b = small("col_b", [NB_ROWS])
        col_c = small("col_c", [NC_ROWS])
        mod = small("mod", [NMOD * KT])
        c_act = small("c_act", [KT])
        scale1 = small("scale1", [KT])
        scale2 = small("scale2", [KT])
        eps_col = small("eps_col", [1])
        one_col = small("one_col", [1])
        qscale_col = small("qscale_col", [1])
        neg_dn_w = small("neg_dn_w", [1])
        ss = small("ss", [TT])
        var = small("var", [TT])
        rstd = small("rstd", [TT])
        ba = small("ba", [TT, 2 * NH])
        w_ba = small("w_ba", [KT, 2 * NH])
        gate_rows = small("gate_rows", [2, NH])
        g = small("g", [TT, NH])
        beta = small("beta", [TT, NH])
        neg_beta = small("neg_beta", [TT, NH])
        tmp_g = sb("tmp_g", o_w + 52 * KIB + 4 * LEVELS * P, [TT, NH])
        tmp_m = sb("tmp_m", o_w + 52 * KIB + 4 * LEVELS * P + 128, [TT, NH])
        gc = small("gc", [NH])
        kdec = small("kdec", [NH])
        cdec = small("cdec", [2, NH])

        rows_a = sb("rows_a", o_w + 24 * KIB, [P])
        rows_b = sb("rows_b", o_w + 24 * KIB + 512, [P])
        rows_c = sb("rows_c", o_w + 24 * KIB + 1024, [P])

        ada_first = [sb(f"ada_first{n}", o, [KT, BANK]) for n, o in enumerate((o_q, o_k, o_v, o_a))]
        ba_rows = sb("ba_rows", o_q + 8 * KIB, [L])
        x_lo4 = sb("x_lo4", o_z, [4, D])
        x_hi4 = sb("x_hi4", o_w + 8 * KIB, [4, D])
        squares = sb("squares", o_w + 36 * KIB, [2, D])
        hf = sb("hf", o_w + 36 * KIB, [KT, BANK])

        WSLOTS = 3
        w_split = sb("w_split", o_w, [WSLOTS, 2, KT, P], F32R)
        w_raw = sb("w_raw", o_w + 24 * KIB, [WSLOTS, KT, P])
        cx = sb("cx", o_w + 36 * KIB, [L])
        sq = sb("sq", o_w + 40 * KIB, [L])
        ada_raw = sb("ada_raw", o_w + 44 * KIB, [2, KT, P])
        ada_sum = small("ada_sum", [6, P])

        def dn(name, n, slots=None):
            shape = [NH, P] if slots is None else [slots, NH, P]
            return sb(name, o_w + 2 * n * KIB, shape)

        kc = dn("kc", 0)
        gb_lt = dn("gb_lt", 1)
        egb = dn("egb", 2)
        dec = dn("dec", 3)
        tm = dn("tm", 4)
        pm = dn("pm", 5)
        mlev = sb("mlev", o_w + 12 * KIB, [LEVELS - 1, NH, P])
        kg = dn("kg", 12, 2)
        qd = dn("qd", 14, 2)
        att = dn("att", 16, 2)
        kd = dn("kd", 18, 2)
        um = dn("um", 20, 2)
        rr = dn("rr", 22)
        vn = dn("vn", 23)
        st = dn("st", 24)
        vc = dn("vc", 25)
        osq = sb("osq", o_w + 52 * KIB, [L])

        wo_split = [sb("wo_split_a", o_w, [4, 2, D], F32R), None]
        wo_split_q = sb("wo_split_q", o_q, [2, 2, D], F32R)
        wo_split_z = sb("wo_split_z", o_z, [2, 2, D], F32R)
        wo_raw = sb("wo_raw", o_w + 32 * KIB, [3, D])
        gate_row = sb("gate_row", o_w + 44 * KIB, [D])
        diag = sb("diag", o_w + 48 * KIB, [KT, P])
        x2 = sb("x2", o_k, [TT, D])
        xn2 = sb("xn2", o_a, [2, D])
        hf2 = sb("hf2", o_a + 8 * KIB, [2, KT, P])

        wg_split = sb("wg_split", o_w, [2, KT, P], F32R)
        wu_split = sb("wu_split", o_w + 8 * KIB, [2, KT, P], F32R)
        wd_split = sb("wd_split", o_w + 16 * KIB, [2, 2, D], F32R)
        act_split = sb("act_split", o_q, [2, 2, L], F32R)
        wg_raw = sb("wg_raw", o_w + 32 * KIB, [KT, P])
        wu_raw = sb("wu_raw", o_w + 36 * KIB, [KT, P])
        wd_raw = sb("wd_raw", o_w + 40 * KIB, [D])
        gate2_row = sb("gate2_row", o_w + 44 * KIB, [D])
        cg = sb("cg", o_z, [L])
        cu = sb("cu", o_z + 4 * KIB, [L])
        normf_row = sb("normf_row", o_z + 8 * KIB, [D])

        ps = ctx.enter_context(nc.psum_tensor("ps", [P, 8, BANK], F32))

        def bank(n, count=1, width=None):
            v = ps[:, n:n + count, :].rearrange("p b n -> p (b n)")
            return v if width is None else v.rearrange("p (q n) -> p q n", n=width)

        def sem(name):
            return ctx.enter_context(nc.semaphore(name))

        def sems(name, count):
            return [sem(f"{name}{n}") for n in range(count)]

        class s:
            x_in = sems("x_in", 4)
            w_raw_in = sems("w_raw_in", 3)
            rows_in = sem("rows_in")
            ada_first_in = sems("ada_first_in", 4)
            w_ba_in = sem("w_ba_in")
            gate_rows_in = sem("gate_rows_in")
            sp_past_wait = sem("sp_past_wait")
            cols_ready = sem("cols_ready")
            w_lo_done = sem("w_lo_done")
            ada_mm = sem("ada_mm")
            ada_summed = sem("ada_summed")
            ada_in = sems("ada_in", 2)
            norm_lo = sem("norm_lo")
            norm_lo_odd = sem("norm_lo_odd")
            ba_mm = sem("ba_mm")
            dn_over = sem("dn_over")
            wo_raw_in = sems("wo_raw_in", 3)
            wo_lo = sem("wo_lo")
            wg_raw_in = sem("wg_raw_in")
            wu_raw_in = sem("wu_raw_in")
            wd_raw_in = sem("wd_raw_in")
            wg_lo = sem("wg_lo")
            wu_lo = sem("wu_lo")
            wd_lo = sem("wd_lo")
            normf_in = sem("normf_in")
            y_ready = sem("y_ready")
            out_done = sem("out_done")
            const_built = sem("const_built")
            consts_ready = sem("consts_ready")
            w_hi_done = sem("w_hi_done")
            c_act_ready = sem("c_act_ready")
            ada_first_step = sem("ada_first_step")
            norm_hi = sem("norm_hi")
            ada_step = sem("ada_step")
            dn_r = sem("dn_r")
            dn_o = sem("dn_o")
            dn_egb = sem("dn_egb")
            dn_kg = sem("dn_kg")
            dn_qd = sem("dn_qd")
            dn_lt = sem("dn_lt")
            dn_p = sem("dn_p")
            dn_m = sem("dn_m")
            ya_hi = sem("ya_hi")
            ya_lo = sem("ya_lo")
            gate_row_ready = sem("gate_row_ready")
            wo_gated = sem("wo_gated")
            wo_hi = sem("wo_hi")
            yb_hi = sem("yb_hi")
            yb_lo = sem("yb_lo")
            wg_hi = sem("wg_hi")
            wu_hi = sem("wu_hi")
            wd_gated = sem("wd_gated")
            wd_hi = sem("wd_hi")
            act_hi = sem("act_hi")
            act_lo = sem("act_lo")
            act_past_wait = sem("act_past_wait")
            tile_mm = sem("tile_mm")
            norm_inv = sem("norm_inv")
            norm_rstd = sem("norm_rstd")
            norm_ss = sem("norm_ss")
            norm_hf = sem("norm_hf")
            gates_in = sem("gates_in")
            gate_act = sem("gate_act")
            stat_mm = sem("stat_mm")
            stat_ln = sem("stat_ln")
            stat_rs = sem("stat_rs")
            ax_taken = sem("ax_taken")
            cx_ready = sem("cx_ready")
            conv_tapped = sem("conv_tapped")
            ya_raw = sem("ya_raw")
            k_norm = sem("k_norm")
            sq_ready = sem("sq_ready")
            conv_step = sem("conv_step")
            silu_done = sem("silu_done")
            ya_norm = sem("ya_norm")
            q_norm = sem("q_norm")
            z_taken = sems("z_taken", 2)
            dn_t0 = sem("dn_t0")
            dn_kt = sem("dn_kt")
            gates_ready = sem("gates_ready")
            dn_gb = sem("dn_gb")
            dn_kc = sem("dn_kc")
            dn_cum = sem("dn_cum")
            dn_cd = sem("dn_cd")
            dn_diff = sem("dn_diff")
            dn_dec = sem("dn_dec")
            dn_kdiff = sem("dn_kdiff")
            dn_kdec = sem("dn_kdec")
            dn_t1 = sem("dn_t1")
            dn_t1_copied = sem("dn_t1_copied")
            dn_pm = sem("dn_pm")
            dn_vc = sem("dn_vc")
            dn_rr = sem("dn_rr")
            dn_o_copied = sem("dn_o_copied")
            gate_mm = sem("gate_mm")
            yb_rs_used = sem("yb_rs_used")
            osq_ready = sem("osq_ready")
            ostat_mm = sem("ostat_mm")
            ostat_ln = sem("ostat_ln")
            ostat_rs = sem("ostat_rs")
            yb_ready = sem("yb_ready")
            out_a_mm = sem("out_a_mm")
            x2_out = sem("x2_out")
            norm_turned = sem("norm_turned")
            gate_tile_mm = sem("gate_tile_mm")
            ff_tapped = sem("ff_tapped")
            cg_conv = sem("cg_conv")
            cg_silu = sem("cg_silu")
            down_tile_mm = sem("down_tile_mm")
            up_tile_mm = sem("up_tile_mm")
            act_ready = sem("act_ready")
            x2_mlp = sem("x2_mlp")
            rows_turned = sem("rows_turned")
            norm_ms = sem("norm_ms")
            norm_xn = sem("norm_xn")
            ada_acc = sem("ada_acc")
            ada_first_mm = sem("ada_first_mm")
            mod_step = sem("mod_step")
            ba_rows_ready = sem("ba_rows_ready")
            ba_turned = sem("ba_turned")
            gate_step = sem("gate_step")
            mod_taken = sem("mod_taken")
            dn_t2 = sem("dn_t2")
            dn_g_step = sem("dn_g_step")
            dn_d_step = sem("dn_d_step")
            dn_masked = sem("dn_masked")
            dn_l_step = sem("dn_l_step")
            dn_att = sem("dn_att")
            dn_v = sem("dn_v")
            dn_u = sem("dn_u")
            dn_s = sem("dn_s")
            dn_kd = sem("dn_kd")
            dn_tt = sem("dn_tt")
            dn_tm = sem("dn_tm")
            dn_vn = sem("dn_vn")
            dn_st = sem("dn_st")
            diag_ready = sem("diag_ready")
            out_mm = sem("out_mm")
            norm_step = sem("norm_step")
            cg_step = sem("cg_step")
            cu_step = sem("cu_step")
            cu_conv = sem("cu_conv")

        def rows(ap):
            return ap.rearrange("a (r n) -> (a r) n", n=P)

        x_pairs = x.rearrange("b (t p) d -> p (b t) d", p=P)
        out_rows = out.rearrange("b (t p) d -> (b t) p d", p=P)
        ada_v = ada_w.rearrange("o (k p) n -> p (o k) n", p=P)
        win_v = w_in.rearrange("o (k p) n -> p (o k) n", p=P)
        wup_v = w_up.rearrange("o (k p) n -> p (o k) n", p=P)
        wout_v = w_out.rearrange("o (k p) n -> p (o k) n", p=P)
        wdown_v = w_down.rearrange("o (k p) n -> p (o k) n", p=P)

        C_C, C_N1, C_N2, C_ADAB = 0, KT, 2 * KT, 3 * KT
        C_NA = C_ADAB + NMOD * KT
        C_DN = C_NA + AT
        C_CA = C_DN + 1
        C_QKV, C_FF2 = 0, 4 * 3 * NH
        SH1, SC1, GT1, SH2, SC2, GT2 = (m * KT for m in range(6))

        N1, N2, NF = 0, TT, 2 * TT
        UNITS = 2 * KT
        TH = TT // 2
        M2, LO2 = UNITS, UNITS // 2
        TURN_BANKS = 5
        BA_BANK = [7, 0]

        def x_rows(tt):
            return x_lo4[:, tt, :] if tt < TH else x_hi4[:, tt - TH, :]

        def unit(store, part, u):
            half = u // KT
            return store[:, half * TH:(half + 1) * TH, part, u % KT, :]

        def hf_unit(u):
            return hf[:, u % KT, :].rearrange("p (t n) -> p t n", n=P)

        AX, AC, AB, Q, K, V, Z = range(7)
        NPOS = 7
        W_BASE = [2 * AW, AW, 0, 3 * AW, 3 * AW + DNW, 3 * AW + 2 * DNW, 3 * AW + 3 * DNW]
        W_SLOT = [0, 1, 2, 0, 1, 2, 1]
        USES = [W_SLOT.count(n) for n in range(WSLOTS)]
        T_BANK = [0, 2, 0, 2, 0, 2, 0]
        ADA_AFTER = {AX: [0], AC: [1], AB: [2], Q: [3], K: [4, 5], V: [6, 7]}

        def ada_columns_of(b):
            return ada_sum[:, b, :] if b < 6 else ada_raw[:, b % 2, 0, :]

        def use(pos, j):
            slot = W_SLOT[pos]
            return j * USES[slot] + W_SLOT[:pos].count(slot) + 1

        def x_in(tt):
            return s.x_in[tt // 2]

        def raw_in(slot):
            return s.w_raw_in[slot]

        def nth(pos, j):
            return j * NPOS + pos + 1

        def slot_free(pos, j):
            before = [p for p in range(pos) if W_SLOT[p] == W_SLOT[pos]]
            if before:
                return nth(before[-1], j)
            last = max(p for p in range(NPOS) if W_SLOT[p] == W_SLOT[pos])
            return nth(last, j) - NPOS if pos == AX else j * NPOS

        def wo_part(k):
            if k < 4:
                return wo_split[0][:, k, :, :]
            return (wo_split_q if k < 6 else wo_split_z)[:, k % 2, :, :]

        block = ctx.enter_context(nc.Block())

        @block.sync
        def _(sp):
            def load_x(n):
                sp.dma_start(x_lo4[:, 2 * n:2 * n + 2, :] if n < 2 else x_hi4[:, 2 * n - 4:2 * n - 2, :],
                             x_pairs[:, 2 * n:2 * n + 2, :]).then_inc(x_in(2 * n), 16)

            sp.dma_start(rows_a[0:KT, :], rows(c)).then_inc(s.rows_in, 16)
            sp.dma_start(rows_a[C_N1:C_N1 + KT, :], rows(norm1_w)).then_inc(s.rows_in, 16)
            sp.dma_start(rows_a[C_N2:C_N2 + KT, :], rows(norm2_w)).then_inc(s.rows_in, 16)
            sp.dma_start(rows_a[C_ADAB:C_ADAB + NMOD * KT, :], rows(ada_b)).then_inc(s.rows_in, 16)
            sp.dma_start(rows_a[C_NA:C_NA + AT, :], rows(norm_a_w)).then_inc(s.rows_in, 16)
            sp.dma_start(rows_a[C_DN:C_DN + 1, :], rows(norm_dn_w)).then_inc(s.rows_in, 16)
            sp.dma_start(rows_a[C_CA:C_CA + 3 * AT, :],
                         conv_a_w.rearrange("o t (r n) -> (o t r) n", n=P)).then_inc(s.rows_in, 16)
            sp.dma_start(rows_b[0:C_FF2, :],
                         conv_qkv_w.rearrange("o t (r n) -> (o t r) n", n=P)).then_inc(s.rows_in, 16)
            sp.dma_start(rows_b[C_FF2:C_FF2 + 2 * FT, :],
                         conv_ff_w[:, 2, :].rearrange("o (r n) -> (o r) n", n=P)).then_inc(s.rows_in, 16)
            sp.dma_start(rows_c[0:NC_ROWS, :],
                         conv_ff_w[:, 0:2, :].rearrange("o t (r n) -> (o t r) n", n=P)).then_inc(s.rows_in, 16)
            for n in range(TT // 2):
                load_x(n)
            for n in range(4):
                sp.wait_ge(s.x_in[n], 16)
                sp.dma_start(ada_first[n][:, :, :], ada_v[:, :, n * BANK:(n + 1) * BANK]
                             ).then_inc(s.ada_first_in[n], 16)
            nba = 3 * AW + 4 * DNW
            sp.dma_start(w_ba[:, :, :], win_v[:, :, nba:nba + 2 * NH]).then_inc(s.w_ba_in, 16)
            sp.dma_start(gate_rows[:, 0, :], a_log.to_broadcast([P, NH])).then_inc(s.gate_rows_in, 16)
            sp.dma_start(gate_rows[:, 1, :], dt_bias.to_broadcast([P, NH])).then_inc(s.gate_rows_in, 16)

            def wait(sem, value):
                sp.wait_ge(sem, value)
                if not isinstance(value, int):
                    sp.sem_inc(s.sp_past_wait, 1)

            def load_w(pos, j):
                slot = W_SLOT[pos]
                columns = win_v[:, :, W_BASE[pos]:W_BASE[pos] + NH * P][:, :, ds(j * P, P)]
                if pos == AX and isinstance(j, int) and j == 0:
                    sp.wait_ge(s.cols_ready, 3)
                else:
                    wait(s.w_lo_done, slot_free(pos, j))
                sp.dma_start(w_raw[:, slot, :, :],
                             columns).then_inc(raw_in(slot), 16)

            def load_ada(b, j):
                first = GT1 * P + (j * 8 + b) * P
                if b < 2:
                    wait(s.ada_mm, j)
                else:
                    wait(s.ada_summed, j * 8 + b - 1)
                sp.dma_start(ada_raw[:, b % 2, :, :],
                             ada_v[:, :, ds(first, P)]).then_inc(
                                 s.ada_in[b % 2], 16)

            def projection_loads(j, last):
                for pos in range(1, NPOS):
                    load_w(pos, j)
                    for b in ADA_AFTER[pos - 1]:
                        load_ada(b, j)
                if not last:
                    load_w(AX, j + 1)

            load_w(AX, 0)
            sp.wait_ge(s.norm_lo, LO2)
            sp.wait_ge(s.norm_lo_odd, UNITS // 2)
            sp.wait_ge(s.ba_mm, UNITS)
            with sp.Fori(0, NH - 1) as j:
                projection_loads(j, False)
            projection_loads(NH - 1, True)

            sp.wait_ge(s.dn_over, 1)
            for k in range(3):
                sp.dma_start(wo_raw[:, k, :], wout_v[:, k, :]).then_inc(s.wo_raw_in[k], 16)
            for tt in range(0, TT, 2):
                sp.dma_start(x2[:, tt:tt + 2, :], x_pairs[:, tt:tt + 2, :]).then_inc(x_in(tt), 16)
            for k in range(3, KT):
                sp.wait_ge(s.wo_lo, k - 2)
                sp.dma_start(wo_raw[:, k % 3, :], wout_v[:, k, :]).then_inc(
                    s.wo_raw_in[k % 3], 16)
            sp.wait_ge(s.wo_lo, KT)
            for f in range(1):
                sp.dma_start(wg_raw[:, :, :], wup_v[:, :, 0:P]).then_inc(s.wg_raw_in, 16)
                sp.dma_start(wu_raw[:, :, :], wup_v[:, :, DFF:DFF + P]).then_inc(s.wu_raw_in, 16)
                sp.dma_start(wd_raw[:, :], wdown_v[:, 0, :]).then_inc(s.wd_raw_in, 16)

            def mlp_loads(f):
                wait(s.wg_lo, f)
                sp.dma_start(wg_raw[:, :, :], wup_v[:, :, ds(f * P, P)]).then_inc(s.wg_raw_in, 16)
                wait(s.wu_lo, f)
                sp.dma_start(wu_raw[:, :, :], wup_v[:, :, ds(DFF + f * P, P)]).then_inc(s.wu_raw_in, 16)
                wait(s.wd_lo, f)
                sp.dma_start(wd_raw[:, :], wdown_v[:, ds(f, 1), :]).then_inc(s.wd_raw_in, 16)

            with sp.Fori(1, FT) as f:
                mlp_loads(f)
            sp.wait_ge(s.norm_lo, LO2 + TT)
            sp.dma_start(normf_row[:, :], norm_f_w.rearrange("(a n) -> a n", a=1).to_broadcast([P, D])
                         ).then_inc(s.normf_in, 16)
            for tt in range(TT):
                sp.wait_ge(s.y_ready, tt + 1)
                sp.dma_start(out_rows[tt], x2[:, tt, :]).then_inc(s.out_done, 16)
            sp.wait_ge(s.out_done, 16 * TT)

        @block.gpsimd
        def _(pool):
            step = [0]

            def built(ins):
                step[0] += 1
                ins.then_inc(s.const_built, 1)
                pool.wait_ge(s.const_built, step[0])

            built(pool.memset(ident[:, :], 0.0))
            built(pool.affine_select(out=ident[:, :], in_=ident[:, :], compare_op=ALU.not_equal, fill=1.0,
                                     base=0, pattern=[[-1, P]], channel_multiplier=1))
            pool.memset(eps_col[:, :], EPS)
            pool.memset(one_col[:, :], 1.0)
            pool.memset(qscale_col[:, :], math.log(P ** -0.5))
            built(pool.memset(ones[:, :], 1.0))
            built(pool.affine_select(out=causal[:, :], in_=ones[:, :], compare_op=ALU.is_ge, fill=0.0,
                                     base=0, pattern=[[1, P]], channel_multiplier=-1))
            gv = group_ones[:, :].rearrange("p (a n) -> p a n", n=GROUP)
            ov = ones[:, :].rearrange("p (a n) -> p a n", n=GROUP)
            built(pool.affine_select(out=gv, in_=ov, compare_op=ALU.is_ge, fill=0.0,
                                     base=0, pattern=[[-GROUP, P // GROUP], [0, GROUP]], channel_multiplier=1))
            built(pool.affine_select(out=gv, in_=gv, compare_op=ALU.is_ge, fill=0.0,
                                     base=GROUP - 1, pattern=[[GROUP, P // GROUP], [0, GROUP]],
                                     channel_multiplier=-1))
            built(pool.memset(level_mask[:, :, :], 0.0))
            for lev in range(LEVELS):
                b = 1 << lev
                nb = P // (2 * b)
                m = level_mask[:, lev, :].rearrange("p (a h n) -> p a h n", h=2, n=b)[:, :, 1, :]
                built(pool.memset(m, 1.0))
                built(pool.affine_select(out=m, in_=m, compare_op=ALU.is_ge, fill=0.0, base=0,
                                         pattern=[[-2 * b, nb], [0, b]], channel_multiplier=1))
                built(pool.affine_select(out=m, in_=m, compare_op=ALU.is_ge, fill=0.0, base=b - 1,
                                         pattern=[[2 * b, nb], [0, b]], channel_multiplier=-1))
            pool.sem_inc(s.consts_ready, 1)

            def split_lo(w, hi, lo, wait, n, done):
                pool.wait_ge(wait, n)
                pool.tensor_tensor(lo, w, hi.bitcast(F32), ALU.subtract).then_inc(done, 1)

            def proj_lo(pos, j):
                slot = W_SLOT[pos]
                split_lo(w_raw[:, slot, :, :], w_split[:, slot, 0, :, :], w_split[:, slot, 1, :, :],
                         s.w_hi_done, nth(pos, j), s.w_lo_done)

            pool.wait_ge(s.c_act_ready, 1)
            pool.wait_ge(s.ada_first_in[0], 16)
            a = ada_first[0]
            pool.tensor_tensor(a[:, :, :], a[:, :, :], c_act[:, :].unsqueeze(2).to_broadcast([P, KT, BANK]),
                               ALU.mult).then_inc(s.ada_first_step, 1)
            for n, width in enumerate((4, 2, 1)):
                pool.wait_ge(s.ada_first_step, n + 1)
                pool.tensor_tensor(a[:, 0:width, :], a[:, 0:width, :], a[:, width:2 * width, :],
                                   ALU.add).then_inc(s.ada_first_step, 1)
            proj_lo(AX, 0)
            for u in range(0, UNITS, 2):
                split_lo(hf_unit(u), unit(h, 0, u), unit(h, 1, u), s.norm_hi, u + 1, s.norm_lo)

            def ada_block(b, j):
                a, done = ada_raw[:, b % 2, :, :], (j * 8 + b) * 3
                pool.wait_ge(s.ada_in[b % 2], 16 * (4 * j + b // 2 + 1))
                pool.tensor_tensor(a, a, c_act[:, :].unsqueeze(2).to_broadcast([P, KT, P]),
                                   ALU.mult).then_inc(s.ada_step, 1)
                pool.wait_ge(s.ada_step, done + 1)
                pool.tensor_tensor(a[:, 0:4, :], a[:, 0:4, :], a[:, 4:8, :], ALU.add).then_inc(s.ada_step, 1)
                pool.wait_ge(s.ada_step, done + 2)
                pool.tensor_tensor(a[:, 0:2, :], a[:, 0:2, :], a[:, 2:4, :], ALU.add).then_inc(s.ada_step, 1)
                pool.wait_ge(s.ada_step, done + 3)
                if b == 0:
                    pool.wait_ge(s.ada_mm, j)
                pool.tensor_tensor(ada_columns_of(b), a[:, 0, :], a[:, 1, :], ALU.add).then_inc(s.ada_summed, 1)

            def proj_round(j, last):
                for pos in range(1, NPOS):
                    proj_lo(pos, j)
                    for b in ADA_AFTER[pos - 1]:
                        ada_block(b, j)
                if not last:
                    proj_lo(AX, j + 1)

            with pool.Fori(0, NH - 1) as j:
                proj_round(j, False)
            proj_round(NH - 1, True)

            def dn_part(n, slot):
                if not (isinstance(n, int) and n == 0):
                    pool.wait_ge(s.dn_r, n - 1)
                    pool.wait_ge(s.dn_o, n - 1)
                pool.wait_ge(s.dn_egb, n + 1)
                pool.tensor_tensor(kg[:, slot, :, :], kc[:, :, :], egb[:, :, :], ALU.mult).then_inc(s.dn_kg, 1)
                pool.tensor_tensor(qd[:, slot, :, :], q_t[:, :, ds(n * P, P)], egb[:, :, :],
                                   ALU.mult).then_inc(s.dn_qd, 1)
                pool.wait_ge(s.dn_lt, n + 1)
                if not (isinstance(n, int) and n == 0):
                    pool.wait_ge(s.dn_p, n * (LEVELS - 1))
                for lev in range(1, LEVELS):
                    pool.tensor_tensor(mlev[:, lev - 1, :, :], gb_lt[:, :, :],
                                       level_mask[:, lev:lev + 1, :].to_broadcast([P, NH, P]),
                                       ALU.mult).then_inc(s.dn_m, 1)

            dn_part(0, 0)
            with pool.Fori(0, TT // 2 - 1) as i:
                dn_part(2 * i + 1, 1)
                pool.wait_ge(s.ya_hi, i + 1)
                pool.tensor_tensor(h[:, :, 1, ds(i, 1), :].rearrange("p t a n -> p (a t) n"),
                                   a_t[:, ds(i, 1), :].rearrange("p a (t n) -> p (a t) n", n=P),
                                   h[:, :, 0, ds(i, 1), :].bitcast(F32).rearrange("p t a n -> p (a t) n"),
                                   ALU.subtract).then_inc(s.ya_lo, 1)
                dn_part(2 * i + 2, 0)
            dn_part(TT - 1, 1)
            pool.wait_ge(s.ya_hi, AT)
            pool.tensor_tensor(h[:, :, 1, AT - 1, :], a_t[:, AT - 1, :].rearrange("p (t n) -> p t n", n=P),
                               h[:, :, 0, AT - 1, :].bitcast(F32), ALU.subtract).then_inc(s.ya_lo, 1)

            def wo_tile(k):
                pool.wait_ge(s.wo_raw_in[k % 3], 16 * (k // 3 + 1))
                if k == 0:
                    pool.wait_ge(s.gate_row_ready, 1)
                pool.tensor_tensor(wo_raw[:, k % 3, :], wo_raw[:, k % 3, :], gate_row[:, :],
                                   ALU.mult).then_inc(s.wo_gated, 1)
                split_lo(wo_raw[:, k % 3, :], wo_part(k)[:, 0, :], wo_part(k)[:, 1, :],
                         s.wo_hi, k + 1, s.wo_lo)

            for k in range(4):
                wo_tile(k)
            for hd in range(NH):
                pool.wait_ge(s.yb_hi, hd + 1)
                pool.tensor_tensor(h[:, :, 1, AT + hd, :], q_t[:, hd, :].rearrange("p (t n) -> p t n", n=P),
                                   h[:, :, 0, AT + hd, :].bitcast(F32), ALU.subtract).then_inc(s.yb_lo, 1)
            for k in range(4, KT):
                wo_tile(k)

            def gate_lo(f):
                split_lo(wg_raw[:, :, :], wg_split[:, 0, :, :], wg_split[:, 1, :, :], s.wg_hi, f + 1, s.wg_lo)

            def up_lo(f):
                split_lo(wu_raw[:, :, :], wu_split[:, 0, :, :], wu_split[:, 1, :, :], s.wu_hi, f + 1, s.wu_lo)

            def down_tile(f, slot):
                pool.wait_ge(s.wd_raw_in, 16 * (f + 1))
                pool.wait_ge(s.gate_row_ready, 2)
                pool.tensor_tensor(wd_raw[:, :], wd_raw[:, :], gate2_row[:, :], ALU.mult).then_inc(s.wd_gated, 1)
                split_lo(wd_raw[:, :], wd_split[:, slot, 0, :], wd_split[:, slot, 1, :], s.wd_hi, f + 1, s.wd_lo)

            def act_lo(f, slot):
                pool.wait_ge(s.act_hi, f + 1)
                pool.tensor_tensor(act_split[:, slot, 1, :], cg[:, :], act_split[:, slot, 0, :].bitcast(F32),
                                   ALU.subtract).then_inc(s.act_lo, 1)

            gate_lo(0)
            up_lo(0)
            for tt in range(TT):
                split_lo(hf2[:, tt % 2, :, :], h[:, tt, 0, :, :], h[:, tt, 1, :, :],
                         s.norm_hi, M2 + tt + 1, s.norm_lo)

            def mlp_pair(i, last):
                for u in range(2):
                    f = 2 * i + u
                    more = not (last and u == 1)
                    if more:
                        gate_lo(f + 1)
                    down_tile(f, u)
                    act_lo(f, u)
                    if more:
                        up_lo(f + 1)

            with pool.Fori(0, FT // 2 - 1) as i:
                mlp_pair(i, False)
            mlp_pair(FT // 2 - 1, True)

        @block.scalar
        def _(act):
            def wait(sem, value):
                act.wait_ge(sem, value)
                if not isinstance(value, int):
                    act.sem_inc(s.act_past_wait, 1)

            def proj_hi(pos, j, free=None):
                slot = W_SLOT[pos]
                wait(raw_in(slot), 16 * use(pos, j))
                if free is not None:
                    wait(s.tile_mm, free)
                act.activation(w_split[:, slot, 0, :, :], w_raw[:, slot, :, :], ACT.Copy).then_inc(s.w_hi_done, 1)

            wait(s.cols_ready, 1)
            act.activation(c_act[:, :], col_a[:, C_C:C_C + KT], ACT.Silu).then_inc(s.c_act_ready, 1)

            def root(pair):
                wait(s.norm_inv, N1 + 2 * pair + 2)
                act.activation(rstd[:, 2 * pair:2 * pair + 2], var[:, 2 * pair:2 * pair + 2],
                               ACT.Sqrt).then_inc(s.norm_rstd, 2)

            for tt in range(TT):
                wait(x_in(tt), 16)
                if tt >= 2:
                    wait(s.norm_ss, N1 + tt - 1)
                act.activation(squares[:, tt % 2, :], x_rows(tt), ACT.Square,
                               accum_out=ss[:, tt:tt + 1]).then_inc(s.norm_ss, 1)
                if tt % 2 and tt > 1:
                    root(tt // 2 - 1)
            root(TT // 2 - 1)
            proj_hi(AX, 0)
            for u in range(UNITS):
                wait(s.norm_hf, u + 1)
                act.activation(unit(h, 0, u), hf_unit(u), ACT.Copy).then_inc(s.norm_hi, 1)

            wait(s.gates_in, 1)
            act.activation(tmp_g[:, :, :], tmp_g[:, :, :], ACT.Exp).then_inc(s.gate_act, 1)
            act.activation(beta[:, :, :], ba[:, :, 0:NH], ACT.Exp, scale=-1.0).then_inc(s.gate_act, 1)
            wait(s.gate_rows_in, 32)
            act.activation(gate_rows[:, 0, :], gate_rows[:, 0, :], ACT.Exp).then_inc(s.gate_act, 1)
            wait(s.gate_act, 1)
            act.activation(tmp_g[:, :, :], tmp_g[:, :, :], ACT.Ln, bias=one_col[:, 0:1]).then_inc(s.gate_act, 1)

            def tap(dst, src, weights, col, done):
                act.activation(dst, src, ACT.Copy, scale=weights[:, ds(col, 1)]).then_inc(done, 1)

            def inverse_norm(n, scale, bias):
                wait(s.stat_mm, n + 1)
                act.activation(sq[:, :], bank(4, 2), ACT.Ln, bias=eps_col[:, 0:1], scale=scale).then_inc(s.stat_ln, 1)
                wait(s.stat_ln, n + 1)
                if bias is None:
                    act.activation(sq[:, :], sq[:, :], ACT.Exp, scale=-0.5).then_inc(s.stat_rs, 1)
                else:
                    act.activation(sq[:, :], sq[:, :], ACT.Exp, scale=-0.5, bias=bias[:, 0:1]).then_inc(s.stat_rs, 1)

            def flat(store, j):
                return store[:, ds(j, 1), :].rearrange("p a n -> p (a n)")

            def proj_round(j, last):
                proj_hi(AC, j, j * NPOS)
                wait(s.tile_mm, j * NPOS + 1)
                act.activation(flat(a_t, j), bank(T_BANK[AX], 2), ACT.Copy).then_inc(s.ax_taken, 1)
                proj_hi(AB, j)
                wait(s.cx_ready, j + 1)
                tap(flat(a_t, j), cx[:, :], col_a, C_CA + 2 * AT + j, s.conv_tapped)
                proj_hi(Q, j)
                wait(s.ya_raw, j + 1)
                wait(s.k_norm, j)
                act.activation(sq[:, :], flat(a_t, j), ACT.Square).then_inc(s.sq_ready, 1)
                proj_hi(K, j, j * NPOS + 2)
                wait(s.tile_mm, j * NPOS + 4)
                tap(flat(q_t, j), bank(T_BANK[Q], 2), col_b, C_QKV + 3 * 3 * NH + j, s.conv_tapped)
                inverse_norm(3 * j, 1.0 / GROUP, None)
                proj_hi(V, j)
                wait(s.conv_step, 11 * j + 5)
                act.activation(flat(q_t, j), flat(q_t, j), ACT.Silu).then_inc(s.silu_done, 1)
                wait(s.silu_done, 3 * j + 1)
                wait(s.ya_norm, j + 1)
                act.activation(sq[:, :], flat(q_t, j), ACT.Square).then_inc(s.sq_ready, 1)
                wait(s.tile_mm, j * NPOS + 5)
                tap(flat(k_t, j), bank(T_BANK[K], 2), col_b, C_QKV + 3 * 3 * NH + NH + j, s.conv_tapped)
                inverse_norm(3 * j + 1, 1.0, qscale_col)
                proj_hi(Z, j)
                wait(s.conv_step, 11 * j + 8)
                act.activation(flat(k_t, j), flat(k_t, j), ACT.Silu).then_inc(s.silu_done, 1)
                wait(s.silu_done, 3 * j + 2)
                wait(s.q_norm, j + 1)
                act.activation(sq[:, :], flat(k_t, j), ACT.Square).then_inc(s.sq_ready, 1)
                wait(s.tile_mm, j * NPOS + 6)
                tap(flat(v_t, j), bank(T_BANK[V], 2), col_b, C_QKV + 3 * 3 * NH + 2 * NH + j, s.conv_tapped)
                inverse_norm(3 * j + 2, 1.0, None)
                if not last:
                    proj_hi(AX, j + 1)
                wait(s.conv_step, 11 * j + 11)
                act.activation(flat(v_t, j), flat(v_t, j), ACT.Silu).then_inc(s.silu_done, 1)
                wait(s.tile_mm, j * NPOS + 7)
                for half in range(2):
                    act.activation(flat(z_t, j)[:, half * BANK:(half + 1) * BANK], bank(T_BANK[Z] + half),
                                   ACT.Silu).then_inc(s.z_taken[half], 1)

            with act.Fori(0, NH - 1) as j:
                proj_round(j, False)
            proj_round(NH - 1, True)

            def dn_alone_start(n, slot):
                if not (isinstance(n, int) and n == 0):
                    wait(s.dn_m, n * (LEVELS - 1))
                    wait(s.dn_t0, n)
                    wait(s.dn_kg, n)
                    wait(s.dn_kt, n)
                else:
                    wait(s.gates_ready, 1)
                    wait(s.k_norm, NH)
                act.activation(gb_lt[:, :, :], g[:, ds(n, 1), :].rearrange("p a h -> p (a h)").unsqueeze(2)
                               .to_broadcast([P, NH, P]), ACT.Copy).then_inc(s.dn_gb, 1)
                act.activation(kc[:, :, :], k_t[:, :, ds(n * P, P)], ACT.Copy).then_inc(s.dn_kc, 1)
                wait(s.dn_cum, n + 1)
                if not (isinstance(n, int) and n == 0):
                    wait(s.dn_qd, n)
                    wait(s.dn_cd, n)
                act.activation(egb[:, :, :], bank(0, 1, P), ACT.Exp).then_inc(s.dn_egb, 1)
                wait(s.dn_diff, n + 1)
                act.activation(dec[:, :, :], dec[:, :, :], ACT.Exp).then_inc(s.dn_dec, 1)
                wait(s.dn_kdiff, n + 1)
                act.activation(kdec[:, :], kdec[:, :], ACT.Exp).then_inc(s.dn_kdec, 1)

            def dn_first_t(n):
                wait(s.dn_t1, n + 1)
                act.activation(tm[:, :, :], bank(4, 1, P), ACT.Copy).then_inc(s.dn_t1_copied, 1)

            def dn_level(n, lev):
                wait(s.dn_p, n * (LEVELS - 1) + lev)
                act.activation(pm[:, :, :], bank(1, 1, P), ACT.Copy).then_inc(s.dn_pm, 1)

            def dn_vc(n):
                if not (isinstance(n, int) and n == 0):
                    wait(s.dn_r, n)
                else:
                    wait(s.silu_done, 3 * NH)
                act.activation(vc[:, :, :], v_t[:, :, ds(n * P, P)], ACT.Copy).then_inc(s.dn_vc, 1)

            def dn_rr(n):
                wait(s.dn_r, n + 1)
                act.activation(rr[:, :, :], bank(5, 1, P), ACT.Copy).then_inc(s.dn_rr, 1)

            def dn_o(n):
                wait(s.dn_o, n + 1)
                act.activation(q_t[:, :, ds(n * P, P)], bank(7, 1, P), ACT.Copy).then_inc(s.dn_o_copied, 1)

            def dn_step(n, slot, alone, dep):
                if alone:
                    dn_alone_start(n, slot)
                if dep:
                    dn_rr(n - 1)
                    if alone:
                        dn_vc(n)
                if alone:
                    dn_first_t(n)
                    dn_level(n, 1)
                    dn_level(n, 2)
                if dep:
                    dn_o(n - 1)
                if alone:
                    for lev in range(3, LEVELS):
                        dn_level(n, lev)

            wait(s.tile_mm, NH * NPOS)
            wait(s.ada_mm, NH)
            wait(s.w_lo_done, NH * NPOS)
            dn_vc(0)
            dn_step(0, 0, True, False)
            with act.Fori(0, TT // 2 - 1) as i:
                dn_step(2 * i + 1, 1, True, True)
                act.activation(h[:, :, 0, ds(i, 1), :].rearrange("p t a n -> p (a t) n"),
                               a_t[:, ds(i, 1), :].rearrange("p a (t n) -> p (a t) n", n=P),
                               ACT.Copy).then_inc(s.ya_hi, 1)
                dn_step(2 * i + 2, 0, True, True)
            dn_step(TT - 1, 1, True, True)
            act.activation(h[:, :, 0, AT - 1, :], a_t[:, AT - 1, :].rearrange("p (t n) -> p t n", n=P),
                           ACT.Copy).then_inc(s.ya_hi, 1)
            dn_step(TT, 0, False, True)

            def wo_hi_part(k):
                wait(s.wo_gated, k + 1)
                act.activation(wo_part(k)[:, 0, :], wo_raw[:, k % 3, :], ACT.Copy).then_inc(s.wo_hi, 1)

            wait(s.gate_mm, 1)
            act.activation(gate_row[:, :], bank(2, 2), ACT.Copy).then_inc(s.gate_row_ready, 1)
            wait(s.dn_o_copied, TT)
            for hd in range(NH):
                if hd:
                    wait(s.yb_rs_used, hd)
                act.activation(osq[:, :], q_t[:, hd, :], ACT.Square).then_inc(s.osq_ready, 1)
                wo_hi_part(hd)
                wait(s.ostat_mm, hd + 1)
                act.activation(osq[:, :], bank(4, 2), ACT.Ln, bias=eps_col[:, 0:1], scale=1.0 / P).then_inc(s.ostat_ln, 1)
                wait(s.ostat_ln, hd + 1)
                act.activation(osq[:, :], osq[:, :], ACT.Exp, scale=-0.5).then_inc(s.ostat_rs, 1)
                wait(s.yb_ready, hd + 1)
                act.activation(h[:, :, 0, AT + hd, :], q_t[:, hd, :].rearrange("p (t n) -> p t n", n=P),
                               ACT.Copy).then_inc(s.yb_hi, 1)
            wait(s.yb_lo, NH)
            for k in range(4, KT):
                wo_hi_part(k)

            wait(s.out_a_mm, 1)
            wait(s.wg_raw_in, 16)
            act.activation(wg_split[:, 0, :, :], wg_raw[:, :, :], ACT.Copy).then_inc(s.wg_hi, 1)
            wait(s.wu_raw_in, 16)
            act.activation(wu_split[:, 0, :, :], wu_raw[:, :, :], ACT.Copy).then_inc(s.wu_hi, 1)
            wait(s.ya_lo, AT)
            for tt in range(TT + 1):
                if tt < TT:
                    wait(s.x2_out, 2 * TT + 2 * (tt + 1))
                    if tt >= 2:
                        wait(s.norm_turned, M2 + tt - 1)
                    act.activation(xn2[:, tt % 2, :], x2[:, tt, :], ACT.Square,
                                   accum_out=ss[:, tt:tt + 1]).then_inc(s.norm_ss, 1)
                    wait(s.norm_inv, N2 + tt + 1)
                    act.activation(rstd[:, tt:tt + 1], var[:, tt:tt + 1], ACT.Sqrt).then_inc(s.norm_rstd, 1)
                if tt >= 1:
                    t = tt - 1
                    wait(s.norm_hf, M2 + t + 1)
                    act.activation(h[:, t, 0, :, :], hf2[:, t % 2, :, :], ACT.Copy).then_inc(s.norm_hi, 1)
            wait(s.gate_mm, 2)
            act.activation(gate2_row[:, :], bank(2, 2), ACT.Copy).then_inc(s.gate_row_ready, 1)

            def mlp_pair(i, first, last):
                for u in range(2):
                    f = 2 * i + u
                    more = not (last and u == 1)
                    wait(s.gate_tile_mm, f + 1)
                    tap(cg[:, :], bank(0, 2), col_b, C_FF2 + f, s.ff_tapped)
                    if more:
                        wait(s.wg_raw_in, 16 * (f + 2))
                        act.activation(wg_split[:, 0, :, :], wg_raw[:, :, :], ACT.Copy).then_inc(s.wg_hi, 1)
                    wait(s.cg_conv, f + 1)
                    act.activation(cg[:, :], cg[:, :], ACT.Silu).then_inc(s.cg_silu, 1)
                    if u == 0 and not first:
                        wait(s.down_tile_mm, i * 2 * TT)
                    wait(s.wd_gated, f + 1)
                    act.activation(wd_split[:, u, 0, :], wd_raw[:, :], ACT.Copy).then_inc(s.wd_hi, 1)
                    wait(s.up_tile_mm, f + 1)
                    tap(cu[:, :], bank(2, 2), col_b, C_FF2 + FT + f, s.ff_tapped)
                    if more:
                        wait(s.wu_raw_in, 16 * (f + 2))
                        act.activation(wu_split[:, 0, :, :], wu_raw[:, :, :], ACT.Copy).then_inc(s.wu_hi, 1)
                    wait(s.act_ready, f + 1)
                    act.activation(act_split[:, u, 0, :], cg[:, :], ACT.Copy).then_inc(s.act_hi, 1)
                    wait(s.act_lo, f + 1)

            mlp_pair(0, True, False)
            with act.Fori(1, FT // 2 - 1) as i:
                mlp_pair(i, False, False)
            mlp_pair(FT // 2 - 1, False, True)

            for tt in range(TT):
                wait(s.x2_mlp, FT // 2 * 2 * TT - 2 * TT + 2 * (tt + 1))
                if tt:
                    wait(s.norm_ss, NF + tt)
                act.activation(cg[:, :], x2[:, tt, :], ACT.Square, accum_out=ss[:, tt:tt + 1]).then_inc(s.norm_ss, 1)
                wait(s.norm_inv, NF + tt + 1)
                act.activation(rstd[:, tt:tt + 1], var[:, tt:tt + 1], ACT.Sqrt).then_inc(s.norm_rstd, 1)

        @block.vector
        def _(dve):
            dve.wait_ge(s.rows_turned, 1)
            dve.tensor_copy(col_a[:, :], bank(0)[:, 0:NA_ROWS]).then_inc(s.cols_ready, 1)
            dve.tensor_copy(col_b[:, :], bank(0)[:, P:P + NB_ROWS]).then_inc(s.cols_ready, 1)
            dve.tensor_copy(col_c[:, :], bank(0)[:, 2 * P:2 * P + NC_ROWS]).then_inc(s.cols_ready, 1)

            def inverse_ms(tt, count, tiles=1):
                cols = slice(tt, tt + tiles)
                dve.wait_ge(s.norm_ss, count)
                dve.tensor_scalar(var[:, cols], ss[:, cols], 1.0 / D, EPS, ALU.mult,
                                  ALU.add).then_inc(s.norm_ms, tiles)
                dve.wait_ge(s.norm_ms, count)
                dve.reciprocal(var[:, cols], var[:, cols]).then_inc(s.norm_inv, tiles)

            def norm1_rows(pair):
                dve.wait_ge(s.norm_rstd, N1 + 2 * pair + 2)
                for tt in (2 * pair, 2 * pair + 1):
                    dve.tensor_scalar(x_rows(tt), x_rows(tt), rstd[:, tt:tt + 1], None,
                                      ALU.mult).then_inc(s.norm_xn, 1)

            for pair in range(TT // 2):
                inverse_ms(2 * pair, N1 + 2 * pair + 2, 2)
                if pair:
                    norm1_rows(pair - 1)
            norm1_rows(TT // 2 - 1)
            dve.wait_ge(s.c_act_ready, 1)
            for n in range(2, 4):
                a = ada_first[n]
                dve.wait_ge(s.ada_first_in[n], 16)
                dve.tensor_scalar(a[:, 0, :], a[:, 0, :], c_act[:, 0:1], None, ALU.mult).then_inc(s.ada_acc, 1)
                for k in range(1, KT):
                    dve.wait_ge(s.ada_acc, (n - 2) * KT + k)
                    dve.scalar_tensor_tensor(out=a[:, 0, :], in0=a[:, k, :], scalar=c_act[:, k:k + 1],
                                             in1=a[:, 0, :], op0=ALU.mult, op1=ALU.add).then_inc(s.ada_acc, 1)
            dve.wait_ge(s.ada_first_mm, 1)
            dve.tensor_tensor(mod[:, 0:2 * KT], bank(1)[:, 0:2 * KT],
                              col_a[:, C_ADAB:C_ADAB + 2 * KT], ALU.add).then_inc(s.mod_step, 1)
            dve.wait_ge(s.mod_step, 1)
            dve.scalar_tensor_tensor(out=scale1[:, :], in0=mod[:, SC1:SC1 + KT], scalar=1.0,
                                     in1=col_a[:, C_N1:C_N1 + KT], op0=ALU.add,
                                     op1=ALU.mult).then_inc(s.mod_step, 1)
            dve.wait_ge(s.mod_step, 2)
            for u in range(UNITS + 2):
                k = u % KT
                if u < UNITS:
                    dve.wait_ge(s.norm_turned, u + 1)
                    if u >= KT:
                        dve.wait_ge(s.ba_mm, u - KT + 1)
                    if u == 0:
                        dve.wait_ge(s.norm_ss, N1 + TT)
                    elif u >= KT:
                        dve.wait_ge(s.norm_lo if u % 2 == 0 else s.norm_lo_odd, (u - KT) // 2 + 1)
                    dve.tensor_scalar(hf[:, k, :], bank(2 + u % TURN_BANKS), scale1[:, k:k + 1],
                                      mod[:, SH1 + k:SH1 + k + 1], ALU.mult, ALU.add).then_inc(s.norm_hf, 1)
                if u >= 2 and u % 2:
                    v = u - 2
                    dve.wait_ge(s.norm_hi, v + 1)
                    dve.tensor_tensor(unit(h, 1, v), hf_unit(v), unit(h, 0, v).bitcast(F32),
                                      ALU.subtract).then_inc(s.norm_lo_odd, 1)

            for half in range(2):
                dve.wait_ge(s.ba_mm, (half + 1) * KT)
                dve.tensor_copy(ba_rows[0:2 * NH, half * BANK:(half + 1) * BANK],
                                bank(BA_BANK[half])[0:2 * NH, :]).then_inc(s.ba_rows_ready, 1)
            dve.wait_ge(s.ba_turned, 1)
            dve.tensor_copy(ba[:, :, :], bank(BA_BANK[0])[:, 0:TT * 2 * NH].rearrange("p (t n) -> p t n", n=2 * NH)
                            ).then_inc(s.gate_step, 1)
            dve.wait_ge(s.gate_step, 1)
            dve.wait_ge(s.gate_rows_in, 32)
            dve.tensor_tensor(ba[:, :, NH:2 * NH], ba[:, :, NH:2 * NH],
                              gate_rows[:, 1:2, :].to_broadcast([P, TT, NH]), ALU.add).then_inc(s.gate_step, 1)
            dve.wait_ge(s.gate_step, 2)
            dve.tensor_scalar(tmp_m[:, :, :], ba[:, :, NH:2 * NH], 0.0, None, ALU.max).then_inc(s.gate_step, 1)
            dve.scalar_tensor_tensor(out=tmp_g[:, :, :], in0=ba[:, :, NH:2 * NH], scalar=-1.0,
                                     in1=ba[:, :, NH:2 * NH], op0=ALU.mult, op1=ALU.min).then_inc(s.gates_in, 1)
            dve.wait_ge(s.gate_act, 4)
            dve.tensor_scalar(beta[:, :, :], beta[:, :, :], 1.0, None, ALU.add).then_inc(s.gate_step, 1)
            dve.tensor_tensor(tmp_g[:, :, :], tmp_g[:, :, :], tmp_m[:, :, :], ALU.add).then_inc(s.gate_step, 1)
            dve.wait_ge(s.gate_step, 4)
            dve.reciprocal(beta[:, :, :], beta[:, :, :]).then_inc(s.gate_step, 1)
            dve.wait_ge(s.gate_step, 5)
            dve.scalar_tensor_tensor(out=g[:, :, :], in0=tmp_g[:, :, :], scalar=-1.0,
                                     in1=gate_rows[:, 0:1, :].to_broadcast([P, TT, NH]), op0=ALU.mult,
                                     op1=ALU.mult).then_inc(s.gate_step, 1)
            dve.wait_ge(s.gate_step, 6)
            dve.tensor_scalar(neg_dn_w[:, :], col_a[:, C_DN:C_DN + 1], -1.0, None, ALU.mult).then_inc(s.gate_step, 1)
            dve.wait_ge(s.gate_step, 7)
            dve.tensor_scalar(neg_beta[:, :, :], beta[:, :, :], -1.0, None, ALU.mult).then_inc(s.gates_ready, 1)

            def flat(store, j):
                return store[:, ds(j, 1), :].rearrange("p a n -> p (a n)")

            def conv_tap(dst, src, weight, lag, done):
                dve.scalar_tensor_tensor(out=dst[:, lag:L], in0=src[:, 0:L - lag], scalar=weight,
                                         in1=dst[:, lag:L], op0=ALU.mult, op1=ALU.add).then_inc(done, 1)

            def conv4(j, dst, src, kind):
                col = C_QKV + kind * NH + j
                steps = 11 * j + 2 + 3 * kind
                dve.wait_ge(s.conv_tapped, 4 * j + 2 + kind)
                conv_tap(dst, src, col_b[:, ds(col + 2 * 3 * NH, 1)], 1, s.conv_step)
                dve.wait_ge(s.conv_step, steps + 1)
                conv_tap(dst, src, col_b[:, ds(col + 3 * NH, 1)], 2, s.conv_step)
                dve.wait_ge(s.conv_step, steps + 2)
                conv_tap(dst, src, col_b[:, ds(col, 1)], 3, s.conv_step)

            def proj_round(j):
                dve.wait_ge(s.ax_taken, j + 1)
                dve.wait_ge(s.tile_mm, j * NPOS + 2)
                dve.tensor_tensor(cx[:, :], bank(T_BANK[AC], 2), flat(a_t, j), ALU.mult).then_inc(s.cx_ready, 1)
                dve.wait_ge(s.conv_tapped, 4 * j + 1)
                conv_tap(flat(a_t, j), cx[:, :], col_a[:, ds(C_CA + AT + j, 1)], 1, s.conv_step)
                dve.wait_ge(s.conv_step, 11 * j + 1)
                conv_tap(flat(a_t, j), cx[:, :], col_a[:, ds(C_CA + j, 1)], 2, s.conv_step)
                dve.wait_ge(s.conv_step, 11 * j + 2)
                dve.wait_ge(s.tile_mm, j * NPOS + 3)
                dve.tensor_tensor(flat(a_t, j), bank(T_BANK[AB], 2), flat(a_t, j), ALU.mult).then_inc(s.ya_raw, 1)
                conv4(j, flat(q_t, j), bank(T_BANK[Q], 2), 0)
                dve.wait_ge(s.stat_rs, 3 * j + 1)
                dve.scalar_tensor_tensor(out=flat(a_t, j), in0=flat(a_t, j), scalar=col_a[:, ds(C_NA + j, 1)],
                                         in1=sq[:, :], op0=ALU.mult, op1=ALU.mult).then_inc(s.ya_norm, 1)
                conv4(j, flat(k_t, j), bank(T_BANK[K], 2), 1)
                dve.wait_ge(s.stat_rs, 3 * j + 2)
                dve.tensor_tensor(flat(q_t, j), flat(q_t, j), sq[:, :], ALU.mult).then_inc(s.q_norm, 1)
                conv4(j, flat(v_t, j), bank(T_BANK[V], 2), 2)
                dve.wait_ge(s.stat_rs, 3 * j + 3)
                dve.tensor_tensor(flat(k_t, j), flat(k_t, j), sq[:, :], ALU.mult).then_inc(s.k_norm, 1)
                dve.wait_ge(s.ada_mm, j + 1)
                dve.tensor_tensor(mod[:, ds(GT1 + j * 8, 8)], bank(6)[:, 0:8],
                                  col_a[:, ds(C_ADAB + GT1 + j * 8, 8)], ALU.add).then_inc(s.mod_taken, 1)

            with dve.Fori(0, NH) as j:
                proj_round(j)
            dve.wait_ge(s.mod_taken, NH)
            dve.scalar_tensor_tensor(out=scale2[:, :], in0=mod[:, SC2:SC2 + KT], scalar=1.0,
                                     in1=col_a[:, C_N2:C_N2 + KT], op0=ALU.add,
                                     op1=ALU.mult).then_inc(s.mod_step, 1)

            def by_head(t):
                return t.unsqueeze(2).to_broadcast([P, NH, P])

            def chunk_cols(t, n):
                return t[:, ds(n, 1), :].rearrange("p a h -> p (a h)")

            def all_heads(t):
                return t[:, :].unsqueeze(1).to_broadcast([P, NH, P])

            def dn_alone_start(n, slot):
                dve.wait_ge(s.dn_egb, n + 1)
                if not (isinstance(n, int) and n == 0):
                    dve.wait_ge(s.dn_t2, n * (LEVELS - 1))
                dve.tensor_tensor(pm[:, :, :], bank(0, 1, P), all_heads(ident), ALU.mult).then_inc(s.dn_g_step, 1)
                dve.wait_ge(s.dn_g_step, 2 * n + 1)
                dve.tensor_reduce(gc[:, :], pm[:, :, :], AX_X, ALU.add).then_inc(s.dn_g_step, 1)
                dve.wait_ge(s.dn_g_step, 2 * n + 2)
                dve.tensor_tensor(dec[:, :, :], bank(0, 1, P), by_head(gc[:, :]), ALU.subtract).then_inc(s.dn_d_step, 1)
                dve.wait_ge(s.dn_d_step, n + 1)
                dve.tensor_scalar(dec[:, :, :], dec[:, :, :], 0.0, None, ALU.min).then_inc(s.dn_diff, 1)
                dve.tensor_tensor(kdec[:, :], bank(0, 1, P)[:, :, P - 1], gc[:, :], ALU.subtract).then_inc(s.dn_kdiff, 1)
                dve.tensor_copy(cdec[:, slot, :], egb[:, :, P - 1]).then_inc(s.dn_cd, 1)
                dve.wait_ge(s.dn_dec, n + 1)
                dve.tensor_tensor(dec[:, :, :], dec[:, :, :], all_heads(causal), ALU.mult).then_inc(s.dn_masked, 1)
                dve.wait_ge(s.dn_masked, n + 1)
                dve.wait_ge(s.dn_kt, n + 1)
                if not (isinstance(n, int) and n == 0):
                    dve.wait_ge(s.dn_o, n - 1)
                dve.tensor_tensor(gb_lt[:, :, :], bank(1, 1, P), dec[:, :, :], ALU.mult).then_inc(s.dn_l_step, 1)
                dve.tensor_tensor(att[:, slot, :, :], bank(2, 1, P), dec[:, :, :], ALU.mult).then_inc(s.dn_att, 1)
                dve.wait_ge(s.dn_l_step, n + 1)
                dve.tensor_tensor(gb_lt[:, :, :], gb_lt[:, :, :], by_head(chunk_cols(beta, n)), ALU.mult).then_inc(s.dn_lt, 1)
                dve.wait_ge(s.dn_lt, n + 1)
                dve.tensor_tensor(pm[:, :, :], gb_lt[:, :, :],
                                  level_mask[:, 0:1, :].to_broadcast([P, NH, P]), ALU.mult).then_inc(s.dn_t0, 1)
                dve.wait_ge(s.dn_t0, n + 1)
                if not (isinstance(n, int) and n == 0):
                    dve.wait_ge(s.dn_v, n - 1)
                dve.tensor_tensor(um[:, slot, :, :], all_heads(ident), pm[:, :, :], ALU.subtract).then_inc(s.dn_u, 1)
                dve.wait_ge(s.dn_kdec, n + 1)
                if not (isinstance(n, int) and n == 0):
                    dve.wait_ge(s.dn_s, n - 1)
                dve.tensor_tensor(kd[:, slot, :, :], bank(3, 1, P), by_head(kdec[:, :]), ALU.mult).then_inc(s.dn_kd, 1)

            def dn_level(n, slot, lev):
                if lev < LEVELS - 1:
                    dve.wait_ge(s.dn_tt, n * (LEVELS - 2) + lev)
                    dve.tensor_tensor(tm[:, :, :], tm[:, :, :], bank(2, 1, P), ALU.subtract).then_inc(s.dn_tm, 1)
                dve.wait_ge(s.dn_t2, n * (LEVELS - 1) + lev)
                dve.tensor_tensor(um[:, slot, :, :], um[:, slot, :, :], bank(3, 1, P), ALU.subtract).then_inc(s.dn_u, 1)

            def dn_v(n):
                dve.wait_ge(s.dn_v, n + 1)
                if not (isinstance(n, int) and n == 0):
                    dve.wait_ge(s.dn_s, n)
                dve.tensor_tensor(vn[:, :, :], bank(6, 1, P), by_head(chunk_cols(neg_beta, n)), ALU.mult).then_inc(s.dn_vn, 1)

            def dn_s(n, slot):
                dve.wait_ge(s.dn_s, n + 1)
                for hd in range(NH):
                    dve.scalar_tensor_tensor(out=st[:, hd, :], in0=st[:, hd, :], scalar=cdec[:, slot, hd:hd + 1],
                                             in1=bank(5, 1, P)[:, hd, :], op0=ALU.mult,
                                             op1=ALU.add).then_inc(s.dn_st, 1)

            def dn_step(n, slot, alone, dep):
                if alone:
                    dn_alone_start(n, slot)
                    dn_level(n, slot, 1)
                if dep:
                    dn_v(n - 1)
                if alone:
                    dn_level(n, slot, 2)
                if dep:
                    dn_s(n - 1, 1 - slot)
                if alone:
                    for lev in range(3, LEVELS):
                        dn_level(n, slot, lev)

            dve.wait_ge(s.tile_mm, NH * NPOS)
            dve.memset(st[:, :, :], 0.0).then_inc(s.dn_st, NH)
            dn_step(0, 0, True, False)
            with dve.Fori(0, TT // 2 - 1) as i:
                dn_step(2 * i + 1, 1, True, True)
                dn_step(2 * i + 2, 0, True, True)
            dn_step(TT - 1, 1, True, True)
            dn_step(TT, 0, False, True)

            dve.wait_ge(s.dn_o_copied, TT)
            dve.wait_ge(s.dn_st, NH * (TT + 1))
            dve.sem_inc(s.dn_over, 1)

            def gate_diag(first_col):
                for k in range(KT):
                    dve.tensor_scalar(diag[:, k, :], ident[:, :], mod[:, first_col + k:first_col + k + 1], None,
                                      ALU.mult).then_inc(s.diag_ready, 1)

            gate_diag(GT1)

            for hd in range(NH):
                dve.wait_ge(s.ostat_rs, hd + 1)
                dve.scalar_tensor_tensor(out=q_t[:, hd, :], in0=q_t[:, hd, :], scalar=neg_dn_w[:, 0:1],
                                         in1=osq[:, :], op0=ALU.mult, op1=ALU.mult).then_inc(s.yb_rs_used, 1)
                dve.wait_ge(s.yb_rs_used, hd + 1)
                dve.tensor_tensor(q_t[:, hd, :], q_t[:, hd, :], z_t[:, hd, :], ALU.mult).then_inc(s.yb_ready, 1)

            def drain_out(n):
                tt, half = n % (2 * TT) // 2, n % 2
                dve.wait_ge(s.out_mm, n + 1)
                if n < 2 * TT:
                    dve.wait_ge(x_in(tt), 32)
                else:
                    dve.wait_ge(s.x2_out, n - 2 * TT + 1)
                piece = x2[:, tt, half * BANK:(half + 1) * BANK]
                dve.tensor_tensor(piece, piece, bank(n % 4 if n < 2 * TT else n % 2), ALU.add).then_inc(s.x2_out, 1)

            def norm2_rows(tt):
                inverse_ms(tt, N2 + tt + 1)
                dve.wait_ge(s.norm_rstd, N2 + tt + 1)
                dve.tensor_scalar(xn2[:, tt % 2, :], x2[:, tt, :], rstd[:, tt:tt + 1], None,
                                  ALU.mult).then_inc(s.norm_xn, 1)

            def norm2_modulate(tt):
                dst = hf2[:, tt % 2, :, :]
                dve.wait_ge(s.norm_turned, M2 + tt + 1)
                if tt >= 2:
                    dve.wait_ge(s.norm_lo, LO2 + tt - 1)
                dve.tensor_tensor(dst, bank(4 + 2 * (tt % 2), 2, P),
                                  scale2[:, :].unsqueeze(2).to_broadcast([P, KT, P]),
                                  ALU.mult).then_inc(s.norm_step, 1)
                dve.wait_ge(s.norm_step, tt + 1)
                dve.tensor_tensor(dst, dst, mod[:, SH2:SH2 + KT].unsqueeze(2).to_broadcast([P, KT, P]),
                                  ALU.add).then_inc(s.norm_hf, 1)

            for n in range(2 * TT):
                drain_out(n)
            for tt in range(TT):
                drain_out(2 * TT + 2 * tt)
                drain_out(2 * TT + 2 * tt + 1)
                if tt >= 1:
                    norm2_rows(tt - 1)
                if tt >= 2:
                    norm2_modulate(tt - 2)
            norm2_rows(TT - 1)
            norm2_modulate(TT - 2)
            dve.wait_ge(s.gate_mm, 1)
            gate_diag(GT2)
            norm2_modulate(TT - 1)

            def conv3(f, dst, src, first_col, tapped, step, done):
                dve.wait_ge(s.ff_tapped, tapped)
                conv_tap(dst, src, col_c[:, ds(2 * FT + first_col + f, 1)], 1, step)
                dve.wait_ge(step, f + 1)
                conv_tap(dst, src, col_c[:, ds(first_col + f, 1)], 2, done)

            def drain_down(i):
                for n in range(2 * TT):
                    tt, half = n // 2, n % 2
                    dve.wait_ge(s.down_tile_mm, i * 2 * TT + n + 1)
                    piece = x2[:, tt, half * BANK:(half + 1) * BANK]
                    dve.tensor_tensor(piece, piece, bank(4 + n % 4), ALU.add).then_inc(s.x2_mlp, 1)

            def mlp_pair(i, first):
                for u in range(2):
                    f = 2 * i + u
                    conv3(f, cg[:, :], bank(0, 2), 0, 2 * f + 1, s.cg_step, s.cg_conv)
                    if u == 0 and not first:
                        drain_down(i - 1)
                    conv3(f, cu[:, :], bank(2, 2), FT, 2 * f + 2, s.cu_step, s.cu_conv)
                    dve.wait_ge(s.cg_silu, f + 1)
                    dve.wait_ge(s.cu_conv, f + 1)
                    dve.tensor_tensor(cg[:, :], cg[:, :], cu[:, :], ALU.mult).then_inc(s.act_ready, 1)

            mlp_pair(0, True)
            with dve.Fori(1, FT // 2) as i:
                mlp_pair(i, False)

            def final_rows(tt):
                inverse_ms(tt, NF + tt + 1)
                dve.wait_ge(s.norm_rstd, NF + tt + 1)
                dve.wait_ge(s.normf_in, 16)
                dve.scalar_tensor_tensor(out=x2[:, tt, :], in0=x2[:, tt, :], scalar=rstd[:, tt:tt + 1],
                                         in1=normf_row[:, :], op0=ALU.mult, op1=ALU.mult).then_inc(s.y_ready, 1)

            i = FT // 2 - 1
            for n in range(2 * TT):
                tt, half = n // 2, n % 2
                dve.wait_ge(s.down_tile_mm, i * 2 * TT + n + 1)
                piece = x2[:, tt, half * BANK:(half + 1) * BANK]
                dve.tensor_tensor(piece, piece, bank(4 + n % 4), ALU.add).then_inc(s.x2_mlp, 1)
                if half and tt:
                    final_rows(tt - 1)
            final_rows(TT - 1)

        @block.tensor
        def _(pe):
            def three_pass(dst, pairs):
                last = None
                for n, (a_hi, a_lo, b_hi, b_lo) in enumerate(pairs):
                    pe.matmul(dst, a_hi, b_hi, start=(n == 0), stop=False)
                    pe.matmul(dst, a_hi, b_lo, start=False, stop=False)
                    last = pe.matmul(dst, a_lo, b_hi, start=False, stop=(n == len(pairs) - 1))
                return last

            def h_half(part, k, half):
                return h[:, half * (TT // 2):(half + 1) * (TT // 2), part, k, :]

            pe.wait_ge(s.consts_ready, 1)
            pe.wait_ge(s.rows_in, 160)
            pe.transpose(bank(0)[:, 0:NA_ROWS], rows_a[0:NA_ROWS, :], ident[0:NA_ROWS, 0:NA_ROWS])
            pe.transpose(bank(0)[:, P:P + NB_ROWS], rows_b[0:NB_ROWS, :], ident[0:NB_ROWS, 0:NB_ROWS])
            pe.transpose(bank(0)[:, 2 * P:2 * P + NC_ROWS], rows_c[0:NC_ROWS, :],
                         ident[0:NC_ROWS, 0:NC_ROWS]).then_inc(s.rows_turned, 1)

            def turn1(u):
                half, k = u // KT, u % KT
                if k == 0:
                    pe.wait_ge(s.norm_xn, N1 + (half + 1) * TH)
                if u >= TURN_BANKS:
                    pe.wait_ge(s.norm_hf, u - TURN_BANKS + 1)
                for i in range(TH):
                    mm = pe.transpose(bank(2 + u % TURN_BANKS)[:, i * P:(i + 1) * P],
                                      x_rows(half * TH + i)[:, k * P:(k + 1) * P], ident[:, :])
                mm.then_inc(s.norm_turned, 1)

            def beta_alpha(u):
                half, k = u // KT, u % KT
                pe.wait_ge(s.norm_hf, u + 1)
                pe.matmul(bank(BA_BANK[half])[0:2 * NH, :], w_ba[:, k, :], hf[:, k, :],
                          start=(k == 0), stop=(k == KT - 1)).then_inc(s.ba_mm, 1)

            for u in range(TURN_BANKS):
                turn1(u)
            pe.wait_ge(s.c_act_ready, 1)
            for blk in [4, 5, 6, 7, 0, 1, 2, 3, 8, 9, 10, 11, 12, 13, 14, 15]:
                n, cols = blk // 4, slice(blk % 4 * P, (blk % 4 + 1) * P)
                if n == 0:
                    pe.wait_ge(s.ada_first_step, 4)
                elif n == 1:
                    pe.wait_ge(s.ada_first_in[1], 16)
                else:
                    pe.wait_ge(s.ada_acc, (n - 1) * KT)
                for k in range(KT if n == 1 else 1):
                    mm = pe.matmul(bank(1)[:, blk:blk + 1], ada_first[n][:, k, cols],
                                   c_act[:, k:k + 1] if n == 1 else ones[:, 0:1],
                                   start=(k == 0), stop=(n != 1 or k == KT - 1))
            mm.then_inc(s.ada_first_mm, 1)
            pe.wait_ge(s.w_ba_in, 16)
            for u in range(UNITS):
                if u + TURN_BANKS < UNITS:
                    turn1(u + TURN_BANKS)
                beta_alpha(u)
            pe.wait_ge(s.ba_rows_ready, 2)
            for tt in range(TT):
                mm = pe.transpose(bank(BA_BANK[0])[:, tt * 2 * NH:(tt + 1) * 2 * NH],
                                  ba_rows[0:2 * NH, tt * P:(tt + 1) * P], ident[0:2 * NH, 0:2 * NH])
            mm.then_inc(s.ba_turned, 1)

            def turn2(tt):
                pe.wait_ge(s.norm_xn, N2 + tt + 1)
                if tt >= 2:
                    pe.wait_ge(s.norm_step, tt - 1)
                for k in range(KT):
                    mm = pe.transpose(bank(4 + 2 * (tt % 2), 2, P)[:, k, :],
                                      xn2[:, tt % 2, k * P:(k + 1) * P], ident[:, :])
                mm.then_inc(s.norm_turned, 1)

            def proj_tile(pos, j, free):
                slot = W_SLOT[pos]
                pe.wait_ge(s.w_lo_done, nth(pos, j))
                for half in range(2):
                    pe.wait_ge(*free[half])
                    mm = three_pass(bank(T_BANK[pos] + half),
                                    [(w_split[:, slot, 0, k, :], w_split[:, slot, 1, k, :],
                                      h_half(0, k, half), h_half(1, k, half)) for k in range(KT)])
                mm.then_inc(s.tile_mm, 1)

            def statistic(n, weights):
                pe.wait_ge(s.sq_ready, n + 1)
                pe.wait_ge(s.stat_ln, n)
                for half in range(2):
                    mm = pe.matmul(bank(4 + half), weights[:, :], sq[:, half * BANK:(half + 1) * BANK],
                                   start=True, stop=True)
                mm.then_inc(s.stat_mm, 1)

            def ada_columns(j):
                pe.wait_ge(s.ada_summed, 8 * (j + 1))
                pe.wait_ge(s.mod_taken, j)
                for b in range(8):
                    mm = pe.matmul(bank(6)[:, b:b + 1], ada_columns_of(b), ones[:, 0:1], start=True, stop=True)
                mm.then_inc(s.ada_mm, 1)

            def proj_round(j):
                proj_tile(AX, j, [(s.z_taken[0], j), (s.z_taken[1], j)])
                proj_tile(AC, j, [(s.conv_step, 11 * j)] * 2)
                proj_tile(AB, j, [(s.ax_taken, j + 1)] * 2)
                proj_tile(Q, j, [(s.cx_ready, j + 1)] * 2)
                statistic(3 * j, group_ones)
                proj_tile(K, j, [(s.ya_raw, j + 1)] * 2)
                statistic(3 * j + 1, ones)
                proj_tile(V, j, [(s.conv_step, 11 * j + 5)] * 2)
                statistic(3 * j + 2, ones)
                proj_tile(Z, j, [(s.conv_step, 11 * j + 8)] * 2)
                ada_columns(j)

            pe.wait_ge(s.norm_lo, LO2)
            pe.wait_ge(s.norm_lo_odd, UNITS // 2)
            with pe.Fori(0, NH) as j:
                proj_round(j)

            def heads(dst, a, b, done=None, n=1):
                for hd in range(NH):
                    mm = pe.matmul(dst[:, hd, :], a[:, hd, :], b[:, hd, :], start=True, stop=True)
                if done is not None:
                    mm.then_inc(done, n)

            def dn_alone_start(n):
                pe.wait_ge(s.dn_gb, n + 1)
                if not (isinstance(n, int) and n == 0):
                    pe.wait_ge(s.dn_kdiff, n)
                else:
                    pe.wait_ge(s.z_taken[1], NH)
                for hd in range(NH):
                    mm = pe.matmul(bank(0, 1, P)[:, hd, :], gb_lt[:, hd, :], causal[:, :], start=True, stop=True)
                mm.then_inc(s.dn_cum, 1)
                pe.wait_ge(s.dn_kc, n + 1)
                pe.wait_ge(s.dn_u, n * LEVELS)
                if isinstance(n, int) and n == 0:
                    pe.wait_ge(s.conv_step, 11 * NH)
                heads(bank(1, 1, P), kc, kc)
                heads(bank(2, 1, P), kc, q_t[:, :, ds(n * P, P)])
                for hd in range(NH):
                    mm = pe.transpose(bank(3, 1, P)[:, hd, :], kc[:, hd, :], ident[:, :])
                mm.then_inc(s.dn_kt, 1)

            def dn_first_t(n, slot):
                pe.wait_ge(s.dn_u, n * LEVELS + 1)
                if not (isinstance(n, int) and n == 0):
                    pe.wait_ge(s.dn_t1_copied, n)
                for hd in range(NH):
                    mm = pe.transpose(bank(4, 1, P)[:, hd, :], um[:, slot, hd, :], ident[:, :])
                mm.then_inc(s.dn_t1, 1)

            def dn_level(n, slot, lev):
                pe.wait_ge(s.dn_m, n * (LEVELS - 1) + lev)
                if lev == 1:
                    pe.wait_ge(s.dn_t1_copied, n + 1)
                    pe.wait_ge(s.dn_l_step, n + 1)
                    pe.wait_ge(s.dn_kd, n + 1)
                else:
                    pe.wait_ge(s.dn_tm, n * (LEVELS - 2) + lev - 1)
                heads(bank(1, 1, P), mlev[:, lev - 1, :, :], tm, s.dn_p)
                pe.wait_ge(s.dn_pm, n * (LEVELS - 1) + lev)
                pe.wait_ge(s.dn_u, n * LEVELS + lev)
                if lev < LEVELS - 1:
                    heads(bank(2, 1, P), um[:, slot, :, :], pm, s.dn_tt)
                heads(bank(3, 1, P), pm, um[:, slot, :, :], s.dn_t2)

            def dn_r(n, slot):
                pe.wait_ge(s.dn_vc, n + 1)
                pe.wait_ge(s.dn_kg, n + 1)
                pe.wait_ge(s.dn_st, NH * (n + 1))
                for hd in range(NH):
                    pe.matmul(bank(5, 1, P)[:, hd, :], vc[:, hd, :], ident[:, :], start=True, stop=False)
                    mm = pe.matmul(bank(5, 1, P)[:, hd, :], kg[:, slot, hd, :], st[:, hd, :], start=False, stop=True)
                mm.then_inc(s.dn_r, 1)

            def dn_v(n, slot):
                pe.wait_ge(s.dn_rr, n + 1)
                pe.wait_ge(s.dn_vn, n)
                pe.wait_ge(s.dn_u, (n + 1) * LEVELS)
                heads(bank(6, 1, P), um[:, slot, :, :], rr, s.dn_v)

            def dn_o_s(n, slot):
                pe.wait_ge(s.dn_vn, n + 1)
                pe.wait_ge(s.dn_att, n + 1)
                pe.wait_ge(s.dn_qd, n + 1)
                pe.wait_ge(s.dn_o_copied, n)
                for hd in range(NH):
                    pe.matmul(bank(7, 1, P)[:, hd, :], st[:, hd, :], qd[:, slot, hd, :], start=True, stop=False)
                    mm = pe.matmul(bank(7, 1, P)[:, hd, :], vn[:, hd, :], att[:, slot, hd, :], start=False, stop=True)
                mm.then_inc(s.dn_o, 1)
                pe.wait_ge(s.dn_kd, n + 1)
                heads(bank(5, 1, P), kd[:, slot, :, :], vn, s.dn_s)

            def dn_step(n, slot, alone, dep):
                if alone:
                    dn_alone_start(n)
                if dep:
                    dn_r(n - 1, 1 - slot)
                if alone:
                    dn_first_t(n, slot)
                    dn_level(n, slot, 1)
                if dep:
                    dn_v(n - 1, 1 - slot)
                if alone:
                    dn_level(n, slot, 2)
                if dep:
                    dn_o_s(n - 1, 1 - slot)
                if alone:
                    for lev in range(3, LEVELS):
                        dn_level(n, slot, lev)

            dn_step(0, 0, True, False)
            with pe.Fori(0, TT // 2 - 1) as i:
                dn_step(2 * i + 1, 1, True, True)
                dn_step(2 * i + 2, 0, True, True)
            dn_step(TT - 1, 1, True, True)
            dn_step(TT, 0, False, True)

            def gate_row_mm(n):
                pe.wait_ge(s.diag_ready, KT * n)
                for half in range(2):
                    mm = pe.matmul(bank(2 + half), ones[:, :],
                                   diag[:, half * 4:half * 4 + 4, :], start=True, stop=True)
                mm.then_inc(s.gate_mm, 1)

            def out_tile(n):
                group, tt, half = n // (2 * TT), n % (2 * TT) // 2, n % 2
                if group == 0:
                    if n >= 4:
                        pe.wait_ge(s.x2_out, n - 3)
                else:
                    pe.wait_ge(s.x2_out, n - 1)
                if n % (2 * TT) == 0:
                    pe.wait_ge(s.wo_lo, 4 * (group + 1))
                    pe.wait_ge(*((s.ya_lo, AT) if group == 0 else (s.yb_lo, NH)))
                dst = bank(n % 4 if group == 0 else n % 2)
                cols = slice(half * BANK, (half + 1) * BANK)
                mm = three_pass(dst, [(h[:, tt, 0, k, :], h[:, tt, 1, k, :], wo_part(k)[:, 0, cols],
                                       wo_part(k)[:, 1, cols]) for k in range(4 * group, 4 * group + 4)])
                mm.then_inc(s.out_mm, 1)

            gate_row_mm(1)
            pe.wait_ge(s.gate_row_ready, 1)

            def out_stat(hd):
                pe.wait_ge(s.osq_ready, hd + 1)
                pe.wait_ge(s.ostat_ln, hd)
                for half in range(2):
                    mm = pe.matmul(bank(4 + half), ones[:, :], osq[:, half * BANK:(half + 1) * BANK],
                                   start=True, stop=True)
                mm.then_inc(s.ostat_mm, 1)

            for hd in range(NH):
                out_stat(hd)
            for n in range(2 * TT):
                out_tile(n)
            pe.wait_ge(s.out_mm, 2 * TT)
            pe.sem_inc(s.out_a_mm, 1)
            for tt in range(TT):
                out_tile(2 * TT + 2 * tt)
                out_tile(2 * TT + 2 * tt + 1)
                if tt >= 2:
                    turn2(tt - 2)
            turn2(TT - 2)
            turn2(TT - 1)
            gate_row_mm(2)

            def wide_tile(w, first_bank, frees, mm_done, chunks=None):
                for half in range(2):
                    for sem, value in frees[half]:
                        pe.wait_ge(sem, value)
                    mm = three_pass(bank(first_bank + half),
                                    [(w[:, 0, k, :], w[:, 1, k, :], h_half(0, k, half), h_half(1, k, half))
                                     for k in range(KT)])
                mm.then_inc(mm_done, 1)

            def down(i):
                pe.wait_ge(s.act_lo, 2 * i + 2)
                pe.wait_ge(s.wd_lo, 2 * i + 2)
                for n in range(2 * TT):
                    tt, half = n // 2, n % 2
                    if n >= 4:
                        pe.wait_ge(s.x2_mlp, i * 2 * TT + n - 3)
                    elif isinstance(i, int) and i == 0:
                        pe.wait_ge(s.norm_step, TT)
                    else:
                        pe.wait_ge(s.x2_mlp, i * 2 * TT)
                    toks = slice(tt * P, (tt + 1) * P)
                    cols = slice(half * BANK, (half + 1) * BANK)
                    mm = three_pass(bank(4 + n % 4),
                                    [(act_split[:, u, 0, toks], act_split[:, u, 1, toks],
                                      wd_split[:, u, 0, cols], wd_split[:, u, 1, cols]) for u in range(2)])
                    mm.then_inc(s.down_tile_mm, 1)

            def gate_tile(f, frees):
                pe.wait_ge(s.wg_lo, f + 1)
                wide_tile(wg_split, 0, frees, s.gate_tile_mm)

            def up_tile(f, frees):
                pe.wait_ge(s.wu_lo, f + 1)
                wide_tile(wu_split, 2, frees, s.up_tile_mm)

            def mlp_pair(i, first):
                for u in range(2):
                    f = 2 * i + u
                    if first and u == 0:
                        gate_tile(f, [[(s.norm_lo, LO2 + TH), (s.x2_out, 4 * TT)], [(s.norm_lo, LO2 + TT)]])
                    else:
                        gate_tile(f, [[(s.cg_conv, f)]] * 2)
                    if u == 0 and not first:
                        down(i - 1)
                    if first and u == 0:
                        up_tile(f, [[(s.gate_row_ready, 2)]] * 2)
                    else:
                        up_tile(f, [[(s.cu_conv, f)]] * 2)

            mlp_pair(0, True)
            with pe.Fori(1, FT // 2) as i:
                mlp_pair(i, False)
            down(FT // 2 - 1)


_INS = ['x', 'c', 'ada_w', 'ada_b', 'norm1_w', 'w_in', 'conv_a_w', 'norm_a_w', 'conv_qkv_w', 'a_log',
        'dt_bias', 'norm_dn_w', 'w_out', 'norm2_w', 'w_up', 'conv_ff_w', 'w_down', 'norm_f_w']


def kernel(**inputs):
    import numpy as _np
    import concourse.bacc as _bacc
    from concourse import mybir as _mybir
    from concourse.bass_utils import run_bass_kernel_spmd as _run

    nc = _bacc.Bacc("TRN2", target_bir_lowering=False, num_devices=1)
    arrays, args = {}, []
    for name in _INS:
        a = _np.ascontiguousarray(inputs[name])
        arrays[f"in_{name}_dram"] = a
        args.append(nc.dram_tensor(f"in_{name}_dram", a.shape, _mybir.dt.from_np(a.dtype), kind="ExternalInput").ap())
    shape = inputs['x'].shape
    args.append(nc.dram_tensor("out_0_dram", shape, _mybir.dt.float32, kind="ExternalOutput").ap())
    build_program(nc, *args)
    r = _run(nc, [arrays], core_ids=[0])
    return r.results[0]["out_0_dram"]
```

```python
import math
from contextlib import ExitStack

import concourse.bass as bass
from concourse import mybir

F32 = mybir.dt.float32
F32R = mybir.dt.float32r
ALU = mybir.AluOpType
ACT = mybir.ActivationFunctionType
AX_X = mybir.AxisListType.X

P = 128
KIB = 1024
BANK = 512


def ds(start, n):
    return bass.ds(start, n)


def build_program(nc, x, c, ada_w, ada_b, norm1_w, w_in, conv_a_w, norm_a_w, conv_qkv_w, a_log,
                  dt_bias, norm_dn_w, w_out, norm2_w, w_up, conv_ff_w, w_down, norm_f_w, out):
    L, D = x.shape[1], x.shape[2]
    DFF = w_down.shape[1]
    AW = conv_a_w.shape[2]
    DNW = conv_qkv_w.shape[2] // 3
    NH = a_log.shape[1]
    KT = D // P
    TT = L // P
    AT = AW // P
    FT = DFF // P
    NMOD = ada_b.shape[1] // D
    EPS = 1e-6
    GROUP = 64
    LEVELS = 7
    assert (L, D, AT, NH, DNW) == (1024, 1024, 4, 4, NH * P) and FT % 2 == 0

    ctx = ExitStack()
    with ctx:
        base = 16512 + 64

        def sb(name, offset, shape, dt=F32):
            return nc.alloc_sbuf_tensor_at(name, [P] + shape, dt, offset=offset)

        o_h = base
        o_q, o_k, o_v, o_z = (base + (64 + 16 * n) * KIB for n in range(4))
        o_a = base + 128 * KIB
        o_w = base + 144 * KIB
        o_c = base + 200 * KIB

        h = sb("h", o_h, [TT, 2, KT, P], F32R)
        q_t = sb("q_t", o_q, [NH, L])
        k_t = sb("k_t", o_k, [NH, L])
        v_t = sb("v_t", o_v, [NH, L])
        z_t = sb("z_t", o_z, [NH, L])
        a_t = sb("a_t", o_a, [AT, L])

        cursor = [o_c]

        def small(name, shape, dt=F32):
            n = 4 * math.prod(shape)
            t = sb(name, cursor[0], shape, dt)
            cursor[0] += (n + 31) // 32 * 32
            assert cursor[0] <= 229344, cursor
            return t

        ident = small("ident", [P])
        ones = small("ones", [P])
        causal = small("causal", [P])
        group_ones = small("group_ones", [P])
        ones_r = sb("ones_r", o_w + 52 * KIB, [P], F32R)
        group_ones_r = sb("group_ones_r", o_w + 52 * KIB + 4 * P, [P], F32R)
        level_mask = sb("level_mask", o_w + 52 * KIB, [LEVELS, P])
        NA_ROWS = KT * 3 + NMOD * KT + AT + 1 + 3 * AT
        NB_ROWS = 4 * 3 * NH + 2 * FT
        NC_ROWS = 2 * 2 * FT
        col_a = small("col_a", [NA_ROWS])
        col_b = small("col_b", [NB_ROWS])
        col_c = small("col_c", [NC_ROWS])
        mod = small("mod", [NMOD * KT])
        c_act = small("c_act", [KT])
        scale1 = small("scale1", [KT])
        scale2 = small("scale2", [KT])
        eps_col = small("eps_col", [1])
        one_col = small("one_col", [1])
        qscale_col = small("qscale_col", [1])
        neg_dn_w = small("neg_dn_w", [1])
        ss = small("ss", [TT])
        var = small("var", [TT])
        rstd = small("rstd", [TT])
        ba = small("ba", [TT, 2 * NH])
        w_ba = small("w_ba", [KT, 2 * NH])
        gate_rows = small("gate_rows", [2, NH])
        g = small("g", [TT, NH])
        beta = small("beta", [TT, NH])
        neg_beta = small("neg_beta", [TT, NH])
        tmp_g = sb("tmp_g", o_w + 52 * KIB + 4 * LEVELS * P, [TT, NH])
        tmp_m = sb("tmp_m", o_w + 52 * KIB + 4 * LEVELS * P + 128, [TT, NH])
        gc = small("gc", [NH])
        kdec = small("kdec", [NH])
        cdec = small("cdec", [2, NH])

        rows_a = sb("rows_a", o_w + 24 * KIB, [P])
        rows_b = sb("rows_b", o_w + 24 * KIB + 512, [P])
        rows_c = sb("rows_c", o_w + 24 * KIB + 1024, [P])

        ada_first = [sb(f"ada_first{n}", o, [KT, BANK]) for n, o in enumerate((o_q, o_k, o_v, o_a))]
        ba_rows = sb("ba_rows", o_q + 8 * KIB, [L])
        x_lo4 = sb("x_lo4", o_z, [4, D])
        x_hi4 = sb("x_hi4", o_w + 8 * KIB, [4, D])
        squares = sb("squares", o_w + 36 * KIB, [2, D])
        hf = sb("hf", o_w + 36 * KIB, [KT, BANK])

        WSLOTS = 3
        w_split = sb("w_split", o_w, [WSLOTS, 2, KT, P], F32R)
        w_raw = sb("w_raw", o_w + 24 * KIB, [WSLOTS, KT, P])
        cx = sb("cx", o_w + 36 * KIB, [L])
        sq = sb("sq", o_w + 40 * KIB, [L])
        sq_hi = sb("sq_hi", o_w + 36 * KIB, [L], F32R)
        sq_lo = sb("sq_lo", o_w + 40 * KIB, [L], F32R)
        ada_raw = sb("ada_raw", o_w + 44 * KIB, [2, KT, P])
        ada_sum = small("ada_sum", [6, P])

        def dn(name, n, slots=None):
            shape = [NH, P] if slots is None else [slots, NH, P]
            return sb(name, o_w + 2 * n * KIB, shape)

        kc = dn("kc", 0)
        egb = dn("egb", 1)
        dec = dn("dec", 2)
        pm_a = dn("pm_a", 3)
        pm_b = dn("pm_b", 4)
        lt = dn("lt", 5, 2)
        tm = dn("tm", 7, 2)
        um = dn("um", 9, 2)
        um_done = dn("um_done", 11)
        kg = dn("kg", 12, 2)
        qd = dn("qd", 14, 2)
        att = dn("att", 16, 2)
        kd = dn("kd", 18, 2)
        rr = dn("rr", 20)
        vn = dn("vn", 21)
        st = dn("st", 22)
        vc = dn("vc", 23)
        osq = sb("osq", o_w + 32 * KIB, [2, L])

        h_room = sb("h_room", o_h, [TT, 2, 2, BANK])
        wo_raw_a = h_room[:, 0:AT, :, 1, :]
        diag_a = h_room[:, AT, :, 1, :]
        wo_split = [sb("wo_split_0", o_a, [2, 2, D], F32R), sb("wo_split_2", o_w, [2, 2, D], F32R),
                    sb("wo_split_4", o_w + 16 * KIB, [2, 2, D], F32R), sb("wo_split_6", o_z, [2, 2, D], F32R)]
        wo_raw = sb("wo_raw", o_w + 40 * KIB, [2, D])
        gate_row = sb("gate_row", o_w + 48 * KIB, [D])
        diag = sb("diag", o_w + 52 * KIB, [KT, P])
        x2 = sb("x2", o_k, [TT, D])
        xn2 = sb("xn2", o_a, [2, D])
        hf2 = sb("hf2", o_a + 8 * KIB, [2, KT, P])

        wg_split = sb("wg_split", o_w, [2, KT, P], F32R)
        wu_split = sb("wu_split", o_w + 8 * KIB, [2, KT, P], F32R)
        wd_split = sb("wd_split", o_w + 16 * KIB, [2, 2, D], F32R)
        act_split = sb("act_split", o_q, [2, 2, L], F32R)
        wg_raw = sb("wg_raw", o_w + 32 * KIB, [KT, P])
        wu_raw = sb("wu_raw", o_w + 36 * KIB, [KT, P])
        wd_raw = sb("wd_raw", o_w + 40 * KIB, [D])
        gate2_row = sb("gate2_row", o_w + 44 * KIB, [D])
        cg = sb("cg", o_z, [L])
        cu = sb("cu", o_z + 4 * KIB, [L])
        normf_row = sb("normf_row", o_z + 8 * KIB, [D])

        ps = ctx.enter_context(nc.psum_tensor("ps", [P, 8, BANK], F32))

        def bank(n, count=1, width=None):
            v = ps[:, n:n + count, :].rearrange("p b n -> p (b n)")
            return v if width is None else v.rearrange("p (q n) -> p q n", n=width)

        def sem(name):
            return ctx.enter_context(nc.semaphore(name))

        def sems(name, count):
            return [sem(f"{name}{n}") for n in range(count)]

        class s:
            x_in = sems("x_in", 4)
            w_raw_in = sems("w_raw_in", 3)
            rows_in = sem("rows_in")
            ada_first_in = sems("ada_first_in", 4)
            w_ba_in = sem("w_ba_in")
            gate_rows_in = sem("gate_rows_in")
            sp_past_wait = sem("sp_past_wait")
            cols_ready = sem("cols_ready")
            w_lo_done = sem("w_lo_done")
            ada_mm = sem("ada_mm")
            ada_summed = sem("ada_summed")
            ada_in = sems("ada_in", 2)
            norm_lo = sem("norm_lo")
            norm_lo_odd = sem("norm_lo_odd")
            ba_mm = sem("ba_mm")
            tile_mm = sem("tile_mm")
            wo_raw_in = sems("wo_raw_in", 2)
            dn_kc = sem("dn_kc")
            dn_vc = sem("dn_vc")
            dn_over = sem("dn_over")
            wo_lo = sem("wo_lo")
            wg_raw_in = sem("wg_raw_in")
            wu_raw_in = sem("wu_raw_in")
            wd_raw_in = sem("wd_raw_in")
            wg_lo = sem("wg_lo")
            wu_lo = sem("wu_lo")
            wd_lo = sem("wd_lo")
            normf_in = sem("normf_in")
            y_ready = sem("y_ready")
            out_done = sem("out_done")
            const_built = sem("const_built")
            consts_ready = sem("consts_ready")
            w_hi_done = sem("w_hi_done")
            c_act_ready = sem("c_act_ready")
            ada_first_step = sem("ada_first_step")
            norm_hi = sem("norm_hi")
            ada_step = sem("ada_step")
            dn_r = sem("dn_r")
            dn_egb = sem("dn_egb")
            dn_kg = sem("dn_kg")
            dn_o = sem("dn_o")
            dn_qd = sem("dn_qd")
            ya_hi = sem("ya_hi")
            ya_lo = sem("ya_lo")
            wo_hi = sem("wo_hi")
            yb_hi = sem("yb_hi")
            yb_lo = sem("yb_lo")
            stat_mm = sem("stat_mm")
            gates_ready = sem("gates_ready")
            masks_ready = sem("masks_ready")
            gate_row_ready = sem("gate_row_ready")
            wo_gated = sem("wo_gated")
            wg_hi = sem("wg_hi")
            wu_hi = sem("wu_hi")
            wd_gated = sem("wd_gated")
            wd_hi = sem("wd_hi")
            act_hi = sem("act_hi")
            act_lo = sem("act_lo")
            act_past_wait = sem("act_past_wait")
            norm_inv = sem("norm_inv")
            norm_rstd = sem("norm_rstd")
            norm_ss = sem("norm_ss")
            norm_hf = sem("norm_hf")
            gates_in = sem("gates_in")
            gate_act = sem("gate_act")
            stat_ln = sem("stat_ln")
            stat_rs = sem("stat_rs")
            sq_hi_done = sem("sq_hi_done")
            ax_taken = sem("ax_taken")
            cx_ready = sem("cx_ready")
            conv_tapped = sem("conv_tapped")
            ya_raw = sem("ya_raw")
            k_norm = sem("k_norm")
            conv_step = sem("conv_step")
            silu_done = sem("silu_done")
            ya_norm = sem("ya_norm")
            q_norm = sem("q_norm")
            z_taken = sems("z_taken", 2)
            dn_p_b = sem("dn_p_b")
            dn_gb = sem("dn_gb")
            dn_kt = sem("dn_kt")
            dn_cum = sem("dn_cum")
            dn_a = sem("dn_a")
            dn_rr = sem("dn_rr")
            dn_dec = sem("dn_dec")
            dn_kdec = sem("dn_kdec")
            dn_o_copied = sem("dn_o_copied")
            dn_t1 = sem("dn_t1")
            dn_t1_copied = sem("dn_t1_copied")
            dn_b = sem("dn_b")
            dn_v = sem("dn_v")
            dn_um_copied = sem("dn_um_copied")
            gate_mm = sem("gate_mm")
            dn_al = sem("dn_al")
            yb_rs_used = sem("yb_rs_used")
            osq_ready = sem("osq_ready")
            ostat_mm = sem("ostat_mm")
            ostat_ln = sem("ostat_ln")
            ostat_rs = sem("ostat_rs")
            yb_ready = sem("yb_ready")
            out_a_mm = sem("out_a_mm")
            x2_out = sem("x2_out")
            norm_turned = sem("norm_turned")
            gate_tile_mm = sem("gate_tile_mm")
            ff_tapped = sem("ff_tapped")
            cg_conv = sem("cg_conv")
            cg_silu = sem("cg_silu")
            down_tile_mm = sem("down_tile_mm")
            up_tile_mm = sem("up_tile_mm")
            act_ready = sem("act_ready")
            x2_mlp = sem("x2_mlp")
            rows_turned = sem("rows_turned")
            norm_ms = sem("norm_ms")
            norm_xn = sem("norm_xn")
            ada_acc = sem("ada_acc")
            ada_first_mm = sem("ada_first_mm")
            mod_step = sem("mod_step")
            ba_rows_ready = sem("ba_rows_ready")
            ba_turned = sem("ba_turned")
            gate_step = sem("gate_step")
            sq_raw = sem("sq_raw")
            sq_ready = sem("sq_ready")
            mod_taken = sem("mod_taken")
            dn_p_a = sem("dn_p_a")
            dn_t_a = sem("dn_t_a")
            dn_t_b = sem("dn_t_b")
            dn_kk = sem("dn_kk")
            dn_s = sem("dn_s")
            dn_vn = sem("dn_vn")
            dn_st = sem("dn_st")
            diag_ready = sem("diag_ready")
            out_mm = sem("out_mm")
            norm_step = sem("norm_step")
            cg_step = sem("cg_step")
            cu_step = sem("cu_step")
            cu_conv = sem("cu_conv")

        def rows(ap):
            return ap.rearrange("a (r n) -> (a r) n", n=P)

        x_pairs = x.rearrange("b (t p) d -> p (b t) d", p=P)
        out_rows = out.rearrange("b (t p) d -> (b t) p d", p=P)
        ada_v = ada_w.rearrange("o (k p) n -> p (o k) n", p=P)
        win_v = w_in.rearrange("o (k p) n -> p (o k) n", p=P)
        wup_v = w_up.rearrange("o (k p) n -> p (o k) n", p=P)
        wout_v = w_out.rearrange("o (k p) n -> p (o k) n", p=P)
        wdown_v = w_down.rearrange("o (k p) n -> p (o k) n", p=P)

        C_C, C_N1, C_N2, C_ADAB = 0, KT, 2 * KT, 3 * KT
        C_NA = C_ADAB + NMOD * KT
        C_DN = C_NA + AT
        C_CA = C_DN + 1
        C_QKV, C_FF2 = 0, 4 * 3 * NH
        SH1, SC1, GT1, SH2, SC2, GT2 = (m * KT for m in range(6))

        N1, N2, NF = 0, TT, 2 * TT
        UNITS = 2 * KT
        TH = TT // 2
        M2, LO2 = UNITS, UNITS // 2
        TURN_BANKS = 5
        BA_BANK = [7, 0]

        def x_rows(tt):
            return x_lo4[:, tt, :] if tt < TH else x_hi4[:, tt - TH, :]

        def unit(store, part, u):
            half = u // KT
            return store[:, half * TH:(half + 1) * TH, part, u % KT, :]

        def hf_unit(u):
            return hf[:, u % KT, :].rearrange("p (t n) -> p t n", n=P)

        AX, AC, AB, Q, K, V, Z = range(7)
        NPOS = 7
        W_BASE = [2 * AW, AW, 0, 3 * AW, 3 * AW + DNW, 3 * AW + 2 * DNW, 3 * AW + 3 * DNW]
        W_SLOT = [0, 1, 2, 0, 1, 2, 1]
        USES = [W_SLOT.count(n) for n in range(WSLOTS)]
        T_BANK = [0, 2, 0, 2, 0, 2, 0]
        ADA_AFTER = {AX: [0], AC: [1], AB: [2], Q: [3], K: [4, 5], V: [6, 7]}

        def ada_columns_of(b):
            return ada_sum[:, b, :] if b < 6 else ada_raw[:, b % 2, 0, :]

        def use(pos, j):
            slot = W_SLOT[pos]
            return j * USES[slot] + W_SLOT[:pos].count(slot) + 1

        def x_in(tt):
            return s.x_in[tt // 2]

        def raw_in(slot):
            return s.w_raw_in[slot]

        def nth(pos, j):
            return j * NPOS + pos + 1

        def slot_free(pos, j):
            before = [p for p in range(pos) if W_SLOT[p] == W_SLOT[pos]]
            if before:
                return nth(before[-1], j)
            last = max(p for p in range(NPOS) if W_SLOT[p] == W_SLOT[pos])
            return nth(last, j) - NPOS if pos == AX else j * NPOS

        A_LEVELS = [1]
        B_LEVELS = list(range(2, LEVELS))
        LA, LB = len(A_LEVELS), len(B_LEVELS)
        (A_DIAG, A_SUM, A_DIFF, A_MIN, A_KDIFF, A_MASK, A_LT0, A_LT, A_M0, A_UM, A_ATT, A_KD,
         A_CDEC) = range(1, 14)
        A_STEPS = A_CDEC
        B_STEPS = 3 * LB - 1

        def wait_reuse(engine, sem, value):
            if not (isinstance(value, int) and value <= 0):
                engine.wait_ge(sem, value)

        def halves(ap, lev):
            b = 1 << lev
            return ap.rearrange("p h (a t n) -> p t (h a) n", t=2, n=b)

        def compact(ap, lev):
            return ap.rearrange("p (a n) -> p a n", n=1 << lev)

        def wo_part(k):
            return wo_split[k // 2][:, k % 2, :, :]

        def wo_raw_of(k):
            if k < AT:
                return wo_raw_a[:, k, :, :]
            return wo_raw[:, k % 2, :].rearrange("p (a n) -> p a n", n=BANK)

        block = ctx.enter_context(nc.Block())

        @block.sync
        def _(sp):
            def load_x(n):
                sp.dma_start(x_lo4[:, 2 * n:2 * n + 2, :] if n < 2 else x_hi4[:, 2 * n - 4:2 * n - 2, :],
                             x_pairs[:, 2 * n:2 * n + 2, :]).then_inc(x_in(2 * n), 16)

            sp.dma_start(rows_a[0:KT, :], rows(c)).then_inc(s.rows_in, 16)
            sp.dma_start(rows_a[C_N1:C_N1 + KT, :], rows(norm1_w)).then_inc(s.rows_in, 16)
            sp.dma_start(rows_a[C_N2:C_N2 + KT, :], rows(norm2_w)).then_inc(s.rows_in, 16)
            sp.dma_start(rows_a[C_ADAB:C_ADAB + NMOD * KT, :], rows(ada_b)).then_inc(s.rows_in, 16)
            sp.dma_start(rows_a[C_NA:C_NA + AT, :], rows(norm_a_w)).then_inc(s.rows_in, 16)
            sp.dma_start(rows_a[C_DN:C_DN + 1, :], rows(norm_dn_w)).then_inc(s.rows_in, 16)
            sp.dma_start(rows_a[C_CA:C_CA + 3 * AT, :],
                         conv_a_w.rearrange("o t (r n) -> (o t r) n", n=P)).then_inc(s.rows_in, 16)
            sp.dma_start(rows_b[0:C_FF2, :],
                         conv_qkv_w.rearrange("o t (r n) -> (o t r) n", n=P)).then_inc(s.rows_in, 16)
            sp.dma_start(rows_b[C_FF2:C_FF2 + 2 * FT, :],
                         conv_ff_w[:, 2, :].rearrange("o (r n) -> (o r) n", n=P)).then_inc(s.rows_in, 16)
            sp.dma_start(rows_c[0:NC_ROWS, :],
                         conv_ff_w[:, 0:2, :].rearrange("o t (r n) -> (o t r) n", n=P)).then_inc(s.rows_in, 16)
            for n in range(TT // 2):
                load_x(n)
            for n in range(4):
                sp.wait_ge(s.x_in[n], 16)
                sp.dma_start(ada_first[n][:, :, :], ada_v[:, :, n * BANK:(n + 1) * BANK]
                             ).then_inc(s.ada_first_in[n], 16)
            nba = 3 * AW + 4 * DNW
            sp.dma_start(w_ba[:, :, :], win_v[:, :, nba:nba + 2 * NH]).then_inc(s.w_ba_in, 16)
            sp.dma_start(gate_rows[:, 0, :], a_log.to_broadcast([P, NH])).then_inc(s.gate_rows_in, 16)
            sp.dma_start(gate_rows[:, 1, :], dt_bias.to_broadcast([P, NH])).then_inc(s.gate_rows_in, 16)

            def wait(sem, value):
                sp.wait_ge(sem, value)
                if not isinstance(value, int):
                    sp.sem_inc(s.sp_past_wait, 1)

            def load_w(pos, j):
                slot = W_SLOT[pos]
                columns = win_v[:, :, W_BASE[pos]:W_BASE[pos] + NH * P][:, :, ds(j * P, P)]
                if pos == AX and isinstance(j, int) and j == 0:
                    sp.wait_ge(s.cols_ready, 3)
                else:
                    wait(s.w_lo_done, slot_free(pos, j))
                sp.dma_start(w_raw[:, slot, :, :],
                             columns).then_inc(raw_in(slot), 16)

            def load_ada(b, j):
                first = GT1 * P + (j * 8 + b) * P
                if b < 2:
                    wait(s.ada_mm, j)
                else:
                    wait(s.ada_summed, j * 8 + b - 1)
                sp.dma_start(ada_raw[:, b % 2, :, :],
                             ada_v[:, :, ds(first, P)]).then_inc(
                                 s.ada_in[b % 2], 16)

            def projection_loads(j, last):
                for pos in range(1, NPOS):
                    load_w(pos, j)
                    for b in ADA_AFTER[pos - 1]:
                        load_ada(b, j)
                if not last:
                    load_w(AX, j + 1)

            load_w(AX, 0)
            sp.wait_ge(s.norm_lo, LO2)
            sp.wait_ge(s.norm_lo_odd, UNITS // 2)
            sp.wait_ge(s.ba_mm, UNITS)
            with sp.Fori(0, NH - 1) as j:
                projection_loads(j, False)
            projection_loads(NH - 1, True)

            sp.wait_ge(s.tile_mm, NH * NPOS)
            for k in range(AT):
                sp.dma_start(wo_raw_of(k), wout_v[:, k, :].rearrange("p (a n) -> p a n", n=BANK)
                             ).then_inc(s.wo_raw_in[k % 2], 16)
            for tt in range(0, TT, 2):
                sp.wait_ge(*((s.dn_kc, TT) if tt < TH else (s.dn_vc, TT)))
                sp.dma_start(x2[:, tt:tt + 2, :], x_pairs[:, tt:tt + 2, :]).then_inc(x_in(tt), 16)
            sp.wait_ge(s.dn_over, 1)
            for k in range(AT, KT):
                sp.wait_ge(s.wo_lo, k - 1)
                sp.dma_start(wo_raw_of(k), wout_v[:, k, :].rearrange("p (a n) -> p a n", n=BANK)
                             ).then_inc(s.wo_raw_in[k % 2], 16)
            sp.wait_ge(s.wo_lo, KT)
            for f in range(1):
                sp.dma_start(wg_raw[:, :, :], wup_v[:, :, 0:P]).then_inc(s.wg_raw_in, 16)
                sp.dma_start(wu_raw[:, :, :], wup_v[:, :, DFF:DFF + P]).then_inc(s.wu_raw_in, 16)
                sp.dma_start(wd_raw[:, :], wdown_v[:, 0, :]).then_inc(s.wd_raw_in, 16)

            def mlp_loads(f):
                wait(s.wg_lo, f)
                sp.dma_start(wg_raw[:, :, :], wup_v[:, :, ds(f * P, P)]).then_inc(s.wg_raw_in, 16)
                wait(s.wu_lo, f)
                sp.dma_start(wu_raw[:, :, :], wup_v[:, :, ds(DFF + f * P, P)]).then_inc(s.wu_raw_in, 16)
                wait(s.wd_lo, f)
                sp.dma_start(wd_raw[:, :], wdown_v[:, ds(f, 1), :]).then_inc(s.wd_raw_in, 16)

            with sp.Fori(1, FT) as f:
                mlp_loads(f)
            sp.wait_ge(s.norm_lo, LO2 + TT)
            sp.dma_start(normf_row[:, :], norm_f_w.rearrange("(a n) -> a n", a=1).to_broadcast([P, D])
                         ).then_inc(s.normf_in, 16)
            for tt in range(TT):
                sp.wait_ge(s.y_ready, tt + 1)
                sp.dma_start(out_rows[tt], x2[:, tt, :]).then_inc(s.out_done, 16)
            sp.wait_ge(s.out_done, 16 * TT)

        @block.gpsimd
        def _(pool):
            step = [0]

            def built(ins):
                step[0] += 1
                ins.then_inc(s.const_built, 1)
                pool.wait_ge(s.const_built, step[0])

            built(pool.memset(ident[:, :], 0.0))
            built(pool.affine_select(out=ident[:, :], in_=ident[:, :], compare_op=ALU.not_equal, fill=1.0,
                                     base=0, pattern=[[-1, P]], channel_multiplier=1))
            pool.memset(eps_col[:, :], EPS)
            pool.memset(one_col[:, :], 1.0)
            pool.memset(qscale_col[:, :], math.log(P ** -0.5))
            built(pool.memset(ones[:, :], 1.0))
            built(pool.affine_select(out=causal[:, :], in_=ones[:, :], compare_op=ALU.is_ge, fill=0.0,
                                     base=0, pattern=[[1, P]], channel_multiplier=-1))
            gv = group_ones[:, :].rearrange("p (a n) -> p a n", n=GROUP)
            ov = ones[:, :].rearrange("p (a n) -> p a n", n=GROUP)
            built(pool.affine_select(out=gv, in_=ov, compare_op=ALU.is_ge, fill=0.0,
                                     base=0, pattern=[[-GROUP, P // GROUP], [0, GROUP]], channel_multiplier=1))
            built(pool.affine_select(out=gv, in_=gv, compare_op=ALU.is_ge, fill=0.0,
                                     base=GROUP - 1, pattern=[[GROUP, P // GROUP], [0, GROUP]],
                                     channel_multiplier=-1))
            built(pool.tensor_tensor(ones_r[:, :], ones[:, :], ones[:, :], ALU.mult))
            built(pool.tensor_tensor(group_ones_r[:, :], group_ones[:, :], ones[:, :], ALU.mult))
            pool.sem_inc(s.consts_ready, 1)

            def split_lo(w, hi, lo, wait, n, done):
                pool.wait_ge(wait, n)
                pool.tensor_tensor(lo, w, hi.bitcast(F32), ALU.subtract).then_inc(done, 1)

            def proj_lo(pos, j):
                slot = W_SLOT[pos]
                split_lo(w_raw[:, slot, :, :], w_split[:, slot, 0, :, :], w_split[:, slot, 1, :, :],
                         s.w_hi_done, nth(pos, j), s.w_lo_done)

            pool.wait_ge(s.c_act_ready, 1)
            pool.wait_ge(s.ada_first_in[0], 16)
            a = ada_first[0]
            pool.tensor_tensor(a[:, :, :], a[:, :, :], c_act[:, :].unsqueeze(2).to_broadcast([P, KT, BANK]),
                               ALU.mult).then_inc(s.ada_first_step, 1)
            for n, width in enumerate((4, 2, 1)):
                pool.wait_ge(s.ada_first_step, n + 1)
                pool.tensor_tensor(a[:, 0:width, :], a[:, 0:width, :], a[:, width:2 * width, :],
                                   ALU.add).then_inc(s.ada_first_step, 1)
            proj_lo(AX, 0)
            for u in range(0, UNITS, 2):
                split_lo(hf_unit(u), unit(h, 0, u), unit(h, 1, u), s.norm_hi, u + 1, s.norm_lo)

            def ada_block(b, j):
                a, done = ada_raw[:, b % 2, :, :], (j * 8 + b) * 3
                pool.wait_ge(s.ada_in[b % 2], 16 * (4 * j + b // 2 + 1))
                pool.tensor_tensor(a, a, c_act[:, :].unsqueeze(2).to_broadcast([P, KT, P]),
                                   ALU.mult).then_inc(s.ada_step, 1)
                pool.wait_ge(s.ada_step, done + 1)
                pool.tensor_tensor(a[:, 0:4, :], a[:, 0:4, :], a[:, 4:8, :], ALU.add).then_inc(s.ada_step, 1)
                pool.wait_ge(s.ada_step, done + 2)
                pool.tensor_tensor(a[:, 0:2, :], a[:, 0:2, :], a[:, 2:4, :], ALU.add).then_inc(s.ada_step, 1)
                pool.wait_ge(s.ada_step, done + 3)
                if b == 0:
                    pool.wait_ge(s.ada_mm, j)
                pool.tensor_tensor(ada_columns_of(b), a[:, 0, :], a[:, 1, :], ALU.add).then_inc(s.ada_summed, 1)

            def proj_round(j, last):
                for pos in range(1, NPOS):
                    proj_lo(pos, j)
                    for b in ADA_AFTER[pos - 1]:
                        ada_block(b, j)
                if not last:
                    proj_lo(AX, j + 1)

            with pool.Fori(0, NH - 1) as j:
                proj_round(j, False)
            proj_round(NH - 1, True)

            def dn_a(n, slot):
                wait_reuse(pool, s.dn_r, n - 1)
                pool.wait_ge(s.dn_egb, n + 1)
                pool.tensor_tensor(kg[:, slot, :, :], kc[:, :, :], egb[:, :, :], ALU.mult).then_inc(s.dn_kg, 1)
                wait_reuse(pool, s.dn_o, n - 1)
                pool.tensor_tensor(qd[:, slot, :, :], q_t[:, :, ds(n * P, P)], egb[:, :, :],
                                   ALU.mult).then_inc(s.dn_qd, 1)

            def ya_lo(k):
                pool.wait_ge(s.ya_hi, k + 1)
                pool.tensor_tensor(h[:, :, 1, ds(k, 1), :].rearrange("p t a n -> p (a t) n"),
                                   a_t[:, ds(k, 1), :].rearrange("p a (t n) -> p (a t) n", n=P),
                                   h[:, :, 0, ds(k, 1), :].bitcast(F32).rearrange("p t a n -> p (a t) n"),
                                   ALU.subtract).then_inc(s.ya_lo, 1)

            def wo_lo(k):
                split_lo(wo_raw_of(k), wo_part(k)[:, 0, :].rearrange("p (a n) -> p a n", n=BANK),
                         wo_part(k)[:, 1, :].rearrange("p (a n) -> p a n", n=BANK), s.wo_hi, k + 1, s.wo_lo)

            def yb_lo(hd):
                pool.wait_ge(s.yb_hi, hd + 1)
                pool.tensor_tensor(h[:, :, 1, AT + hd, :], q_t[:, hd, :].rearrange("p (t n) -> p t n", n=P),
                                   h[:, :, 0, AT + hd, :].bitcast(F32), ALU.subtract).then_inc(s.yb_lo, 1)

            pool.wait_ge(s.stat_mm, 3 * NH)
            pool.wait_ge(s.gates_ready, 1)
            built(pool.memset(level_mask[:, :, :], 0.0))
            for lev in range(LEVELS):
                b = 1 << lev
                nb = P // (2 * b)
                low = b if lev else 0
                m = level_mask[:, lev, :].rearrange("p (a h n) -> p a h n", h=2, n=b)[:, :, 0 if lev else 1, :]
                built(pool.memset(m, 1.0))
                built(pool.affine_select(out=m, in_=m, compare_op=ALU.is_ge, fill=0.0, base=-low,
                                         pattern=[[-2 * b, nb], [0, b]], channel_multiplier=1))
                built(pool.affine_select(out=m, in_=m, compare_op=ALU.is_ge, fill=0.0, base=low + b - 1,
                                         pattern=[[2 * b, nb], [0, b]], channel_multiplier=-1))
            pool.sem_inc(s.masks_ready, 1)
            dn_a(0, 0)
            dn_a(1, 1)
            ya_lo(0)
            pool.wait_ge(s.gate_row_ready, 1)
            for slot in range(2):
                pool.wait_ge(s.wo_raw_in[slot], 16 * AT // 2)
            for k in range(AT):
                pool.tensor_tensor(wo_raw_of(k), wo_raw_of(k), gate_row[:, :].rearrange("p (a n) -> p a n", n=BANK),
                                   ALU.mult).then_inc(s.wo_gated, 1)
            with pool.Fori(0, TT // 2 - 1) as i:
                dn_a(2 * i + 2, 0)
                ya_lo(i + 1)
                dn_a(2 * i + 3, 1)
            for k in range(AT):
                wo_lo(k)
            for pair in range(2):
                yb_lo(2 * pair)
                yb_lo(2 * pair + 1)
                wo_lo(AT + 2 * pair)
                wo_lo(AT + 2 * pair + 1)

            def gate_lo(f):
                split_lo(wg_raw[:, :, :], wg_split[:, 0, :, :], wg_split[:, 1, :, :], s.wg_hi, f + 1, s.wg_lo)

            def up_lo(f):
                split_lo(wu_raw[:, :, :], wu_split[:, 0, :, :], wu_split[:, 1, :, :], s.wu_hi, f + 1, s.wu_lo)

            def down_tile(f, slot):
                pool.wait_ge(s.wd_raw_in, 16 * (f + 1))
                pool.wait_ge(s.gate_row_ready, 2)
                pool.tensor_tensor(wd_raw[:, :], wd_raw[:, :], gate2_row[:, :], ALU.mult).then_inc(s.wd_gated, 1)
                split_lo(wd_raw[:, :], wd_split[:, slot, 0, :], wd_split[:, slot, 1, :], s.wd_hi, f + 1, s.wd_lo)

            def act_lo(f, slot):
                pool.wait_ge(s.act_hi, f + 1)
                pool.tensor_tensor(act_split[:, slot, 1, :], cg[:, :], act_split[:, slot, 0, :].bitcast(F32),
                                   ALU.subtract).then_inc(s.act_lo, 1)

            gate_lo(0)
            up_lo(0)
            for tt in range(TT):
                split_lo(hf2[:, tt % 2, :, :], h[:, tt, 0, :, :], h[:, tt, 1, :, :],
                         s.norm_hi, M2 + tt + 1, s.norm_lo)

            def mlp_pair(i, last):
                for u in range(2):
                    f = 2 * i + u
                    more = not (last and u == 1)
                    if more:
                        gate_lo(f + 1)
                    down_tile(f, u)
                    if more:
                        up_lo(f + 1)
                    act_lo(f, u)

            with pool.Fori(0, FT // 2 - 1) as i:
                mlp_pair(i, False)
            mlp_pair(FT // 2 - 1, True)

        @block.scalar
        def _(act):
            def wait(sem, value):
                act.wait_ge(sem, value)
                if not isinstance(value, int):
                    act.sem_inc(s.act_past_wait, 1)

            def proj_hi(pos, j, free=None):
                slot = W_SLOT[pos]
                wait(raw_in(slot), 16 * use(pos, j))
                if free is not None:
                    wait(s.tile_mm, free)
                act.activation(w_split[:, slot, 0, :, :], w_raw[:, slot, :, :], ACT.Copy).then_inc(s.w_hi_done, 1)

            wait(s.cols_ready, 1)
            act.activation(c_act[:, :], col_a[:, C_C:C_C + KT], ACT.Silu).then_inc(s.c_act_ready, 1)

            def root(pair):
                wait(s.norm_inv, N1 + 2 * pair + 2)
                act.activation(rstd[:, 2 * pair:2 * pair + 2], var[:, 2 * pair:2 * pair + 2],
                               ACT.Sqrt).then_inc(s.norm_rstd, 2)

            for tt in range(TT):
                wait(x_in(tt), 16)
                if tt >= 2:
                    wait(s.norm_ss, N1 + tt - 1)
                act.activation(squares[:, tt % 2, :], x_rows(tt), ACT.Square,
                               accum_out=ss[:, tt:tt + 1]).then_inc(s.norm_ss, 1)
                if tt % 2 and tt > 1:
                    root(tt // 2 - 1)
            root(TT // 2 - 1)
            proj_hi(AX, 0)
            for u in range(UNITS):
                wait(s.norm_hf, u + 1)
                act.activation(unit(h, 0, u), hf_unit(u), ACT.Copy).then_inc(s.norm_hi, 1)

            wait(s.gates_in, 1)
            act.activation(tmp_g[:, :, :], tmp_g[:, :, :], ACT.Exp).then_inc(s.gate_act, 1)
            act.activation(beta[:, :, :], ba[:, :, 0:NH], ACT.Exp, scale=-1.0).then_inc(s.gate_act, 1)
            wait(s.gate_rows_in, 32)
            act.activation(gate_rows[:, 0, :], gate_rows[:, 0, :], ACT.Exp).then_inc(s.gate_act, 1)
            wait(s.gate_act, 1)
            act.activation(tmp_g[:, :, :], tmp_g[:, :, :], ACT.Ln, bias=one_col[:, 0:1]).then_inc(s.gate_act, 1)

            def tap(dst, src, weights, col, done):
                act.activation(dst, src, ACT.Copy, scale=weights[:, ds(col, 1)]).then_inc(done, 1)

            def inverse_norm(n, scale, bias):
                wait(s.stat_mm, n + 1)
                act.activation(sq[:, :], bank(4, 2), ACT.Ln, bias=eps_col[:, 0:1], scale=scale).then_inc(s.stat_ln, 1)
                wait(s.stat_ln, n + 1)
                if bias is None:
                    act.activation(sq[:, :], sq[:, :], ACT.Exp, scale=-0.5).then_inc(s.stat_rs, 1)
                else:
                    act.activation(sq[:, :], sq[:, :], ACT.Exp, scale=-0.5, bias=bias[:, 0:1]).then_inc(s.stat_rs, 1)

            def flat(store, j):
                return store[:, ds(j, 1), :].rearrange("p a n -> p (a n)")

            def squares_of(store, j, n):
                act.activation(sq_hi[:, :], flat(store, j), ACT.Square).then_inc(s.sq_hi_done, 1)

            def proj_round(j, last):
                proj_hi(AC, j, j * NPOS)
                wait(s.tile_mm, j * NPOS + 1)
                act.activation(flat(a_t, j), bank(T_BANK[AX], 2), ACT.Copy).then_inc(s.ax_taken, 1)
                proj_hi(AB, j)
                wait(s.cx_ready, j + 1)
                tap(flat(a_t, j), cx[:, :], col_a, C_CA + 2 * AT + j, s.conv_tapped)
                proj_hi(Q, j)
                wait(s.ya_raw, j + 1)
                wait(s.k_norm, j)
                squares_of(a_t, j, 0)
                proj_hi(K, j, j * NPOS + 2)
                wait(s.tile_mm, j * NPOS + 4)
                tap(flat(q_t, j), bank(T_BANK[Q], 2), col_b, C_QKV + 3 * 3 * NH + j, s.conv_tapped)
                inverse_norm(3 * j, 1.0 / GROUP, None)
                proj_hi(V, j)
                wait(s.conv_step, 11 * j + 5)
                act.activation(flat(q_t, j), flat(q_t, j), ACT.Silu).then_inc(s.silu_done, 1)
                wait(s.silu_done, 3 * j + 1)
                wait(s.ya_norm, j + 1)
                squares_of(q_t, j, 1)
                wait(s.tile_mm, j * NPOS + 5)
                tap(flat(k_t, j), bank(T_BANK[K], 2), col_b, C_QKV + 3 * 3 * NH + NH + j, s.conv_tapped)
                inverse_norm(3 * j + 1, 1.0, qscale_col)
                proj_hi(Z, j)
                wait(s.conv_step, 11 * j + 8)
                act.activation(flat(k_t, j), flat(k_t, j), ACT.Silu).then_inc(s.silu_done, 1)
                wait(s.silu_done, 3 * j + 2)
                wait(s.q_norm, j + 1)
                squares_of(k_t, j, 2)
                wait(s.tile_mm, j * NPOS + 6)
                tap(flat(v_t, j), bank(T_BANK[V], 2), col_b, C_QKV + 3 * 3 * NH + 2 * NH + j, s.conv_tapped)
                inverse_norm(3 * j + 2, 1.0, None)
                if not last:
                    proj_hi(AX, j + 1)
                wait(s.conv_step, 11 * j + 11)
                act.activation(flat(v_t, j), flat(v_t, j), ACT.Silu).then_inc(s.silu_done, 1)
                wait(s.tile_mm, j * NPOS + 7)
                for half in range(2):
                    act.activation(flat(z_t, j)[:, half * BANK:(half + 1) * BANK], bank(T_BANK[Z] + half),
                                   ACT.Silu).then_inc(s.z_taken[half], 1)

            with act.Fori(0, NH - 1) as j:
                proj_round(j, False)
            proj_round(NH - 1, True)

            def dn_vc(n):
                wait_reuse(act, s.dn_r, n)
                act.activation(vc[:, :, :], v_t[:, :, ds(n * P, P)], ACT.Copy).then_inc(s.dn_vc, 1)

            def dn_step(n, slot, a, b, c):
                if a:
                    wait_reuse(act, s.dn_p_b, LB * (n - 1))
                    act.activation(lt[:, slot, :, :], g[:, ds(n, 1), :].rearrange("p a h -> p (a h)").unsqueeze(2)
                                   .to_broadcast([P, NH, P]), ACT.Copy).then_inc(s.dn_gb, 1)
                    wait_reuse(act, s.dn_kt, n)
                    wait_reuse(act, s.dn_kg, n)
                    act.activation(kc[:, :, :], k_t[:, :, ds(n * P, P)], ACT.Copy).then_inc(s.dn_kc, 1)
                    act.wait_ge(s.dn_cum, n + 1)
                    wait_reuse(act, s.dn_qd, n)
                    wait_reuse(act, s.dn_a, n * A_STEPS)
                    act.activation(egb[:, :, :], bank(0, 1, P), ACT.Exp).then_inc(s.dn_egb, 1)
                if c:
                    act.wait_ge(s.dn_r, n - 1)
                    act.activation(rr[:, :, :], bank(6, 1, P), ACT.Copy).then_inc(s.dn_rr, 1)
                if b:
                    dn_vc(n - 1)
                if a:
                    act.wait_ge(s.dn_a, n * A_STEPS + A_MIN)
                    act.activation(dec[:, :, :], dec[:, :, :], ACT.Exp).then_inc(s.dn_dec, 1)
                    act.wait_ge(s.dn_a, n * A_STEPS + A_KDIFF)
                    act.activation(kdec[:, :], kdec[:, :], ACT.Exp).then_inc(s.dn_kdec, 1)
                if c:
                    act.wait_ge(s.dn_o, n - 1)
                    act.activation(q_t[:, :, ds((n - 2) * P, P)], bank(7, 1, P), ACT.Copy).then_inc(s.dn_o_copied, 1)
                if a:
                    act.wait_ge(s.dn_t1, n + 1)
                    act.activation(tm[:, slot, :, :], bank(0, 1, P), ACT.Copy).then_inc(s.dn_t1_copied, 1)
                if b:
                    act.wait_ge(s.dn_b, (n - 1) * B_STEPS + 3 * (LB - 1))
                    wait_reuse(act, s.dn_v, n - 1)
                    act.activation(um_done[:, :, 0:P // 2], um[:, 1 - slot, :, 0:P // 2],
                                   ACT.Copy).then_inc(s.dn_um_copied, 1)

            def ya_hi(k):
                act.activation(h[:, :, 0, ds(k, 1), :].rearrange("p t a n -> p (a t) n"),
                               a_t[:, ds(k, 1), :].rearrange("p a (t n) -> p (a t) n", n=P),
                               ACT.Copy).then_inc(s.ya_hi, 1)

            def wo_hi(k):
                wait(s.wo_gated, k + 1)
                act.activation(wo_part(k)[:, 0, :].rearrange("p (a n) -> p a n", n=BANK), wo_raw_of(k),
                               ACT.Copy).then_inc(s.wo_hi, 1)

            wait(s.tile_mm, NH * NPOS)
            wait(s.ada_mm, NH)
            wait(s.w_lo_done, NH * NPOS)
            wait(s.gates_ready, 1)
            wait(s.k_norm, NH)
            dn_step(0, 0, True, False, False)
            wait(s.silu_done, 3 * NH)
            dn_step(1, 1, True, True, False)
            wait(s.gate_mm, 1)
            act.activation(gate_row[:, :], bank(6, 2), ACT.Copy).then_inc(s.gate_row_ready, 1)
            ya_hi(0)
            with act.Fori(0, TT // 2 - 1) as i:
                dn_step(2 * i + 2, 0, True, True, True)
                ya_hi(i + 1)
                dn_step(2 * i + 3, 1, True, True, True)
            wait(s.ya_lo, AT)
            wo_hi(0)
            wo_hi(1)
            dn_step(TT, 0, False, True, True)
            wait(s.dn_a, TT * A_STEPS)
            wait(s.dn_al, TT * 3 * LA)
            wait(s.dn_kg, TT)
            wait(s.dn_qd, TT)
            wo_hi(2)
            dn_step(TT + 1, 1, False, False, True)
            wait(s.dn_b, TT * B_STEPS)
            wo_hi(3)

            wait(s.dn_o_copied, TT)
            wait(s.dn_over, 1)
            for pair in range(NH // 2):
                heads = (2 * pair, 2 * pair + 1)
                for hd in heads:
                    if pair:
                        wait(s.yb_rs_used, hd - 1)
                    act.activation(osq[:, hd % 2, :], q_t[:, hd, :], ACT.Square).then_inc(s.osq_ready, 1)
                for hd in heads:
                    wait(s.ostat_mm, hd + 1)
                    act.activation(osq[:, hd % 2, :], bank(4 + 2 * (hd % 2), 2), ACT.Ln, bias=eps_col[:, 0:1],
                                   scale=1.0 / P).then_inc(s.ostat_ln, 1)
                for hd in heads:
                    wait(s.ostat_ln, hd + 1)
                    act.activation(osq[:, hd % 2, :], osq[:, hd % 2, :], ACT.Exp,
                                   scale=-0.5).then_inc(s.ostat_rs, 1)
                for hd in heads:
                    wait(s.yb_ready, hd + 1)
                    act.activation(h[:, :, 0, AT + hd, :], q_t[:, hd, :].rearrange("p (t n) -> p t n", n=P),
                                   ACT.Copy).then_inc(s.yb_hi, 1)
                if pair == 0:
                    wo_hi(4)
                    wo_hi(5)
            wait(s.yb_lo, NH)
            wo_hi(6)
            wo_hi(7)

            wait(s.out_a_mm, 1)
            wait(s.wg_raw_in, 16)
            act.activation(wg_split[:, 0, :, :], wg_raw[:, :, :], ACT.Copy).then_inc(s.wg_hi, 1)
            wait(s.wu_raw_in, 16)
            act.activation(wu_split[:, 0, :, :], wu_raw[:, :, :], ACT.Copy).then_inc(s.wu_hi, 1)
            wait(s.ya_lo, AT)
            for tt in range(TT + 1):
                if tt < TT:
                    wait(s.x2_out, 2 * TT + 2 * (tt + 1))
                    if tt >= 2:
                        wait(s.norm_turned, M2 + tt - 1)
                    act.activation(xn2[:, tt % 2, :], x2[:, tt, :], ACT.Square,
                                   accum_out=ss[:, tt:tt + 1]).then_inc(s.norm_ss, 1)
                    wait(s.norm_inv, N2 + tt + 1)
                    act.activation(rstd[:, tt:tt + 1], var[:, tt:tt + 1], ACT.Sqrt).then_inc(s.norm_rstd, 1)
                if tt >= 1:
                    t = tt - 1
                    wait(s.norm_hf, M2 + t + 1)
                    act.activation(h[:, t, 0, :, :], hf2[:, t % 2, :, :], ACT.Copy).then_inc(s.norm_hi, 1)
            wait(s.gate_mm, 2)
            act.activation(gate2_row[:, :], bank(2, 2), ACT.Copy).then_inc(s.gate_row_ready, 1)

            def mlp_pair(i, first, last):
                for u in range(2):
                    f = 2 * i + u
                    more = not (last and u == 1)
                    wait(s.gate_tile_mm, f + 1)
                    tap(cg[:, :], bank(0, 2), col_b, C_FF2 + f, s.ff_tapped)
                    if more:
                        wait(s.wg_raw_in, 16 * (f + 2))
                        act.activation(wg_split[:, 0, :, :], wg_raw[:, :, :], ACT.Copy).then_inc(s.wg_hi, 1)
                    wait(s.cg_conv, f + 1)
                    act.activation(cg[:, :], cg[:, :], ACT.Silu).then_inc(s.cg_silu, 1)
                    if u == 0 and not first:
                        wait(s.down_tile_mm, i * 2 * TT)
                    wait(s.wd_gated, f + 1)
                    act.activation(wd_split[:, u, 0, :], wd_raw[:, :], ACT.Copy).then_inc(s.wd_hi, 1)
                    wait(s.up_tile_mm, f + 1)
                    tap(cu[:, :], bank(2, 2), col_b, C_FF2 + FT + f, s.ff_tapped)
                    if more:
                        wait(s.wu_raw_in, 16 * (f + 2))
                        act.activation(wu_split[:, 0, :, :], wu_raw[:, :, :], ACT.Copy).then_inc(s.wu_hi, 1)
                    wait(s.act_ready, f + 1)
                    act.activation(act_split[:, u, 0, :], cg[:, :], ACT.Copy).then_inc(s.act_hi, 1)
                    wait(s.act_lo, f + 1)

            mlp_pair(0, True, False)
            with act.Fori(1, FT // 2 - 1) as i:
                mlp_pair(i, False, False)
            mlp_pair(FT // 2 - 1, False, True)

            for tt in range(TT):
                wait(s.x2_mlp, FT // 2 * 2 * TT - 2 * TT + 2 * (tt + 1))
                if tt:
                    wait(s.norm_ss, NF + tt)
                act.activation(cg[:, :], x2[:, tt, :], ACT.Square, accum_out=ss[:, tt:tt + 1]).then_inc(s.norm_ss, 1)
                wait(s.norm_inv, NF + tt + 1)
                act.activation(rstd[:, tt:tt + 1], var[:, tt:tt + 1], ACT.Sqrt).then_inc(s.norm_rstd, 1)

        @block.vector
        def _(dve):
            dve.wait_ge(s.rows_turned, 1)
            dve.tensor_copy(col_a[:, :], bank(0)[:, 0:NA_ROWS]).then_inc(s.cols_ready, 1)
            dve.tensor_copy(col_b[:, :], bank(0)[:, P:P + NB_ROWS]).then_inc(s.cols_ready, 1)
            dve.tensor_copy(col_c[:, :], bank(0)[:, 2 * P:2 * P + NC_ROWS]).then_inc(s.cols_ready, 1)

            def inverse_ms(tt, count, tiles=1):
                cols = slice(tt, tt + tiles)
                dve.wait_ge(s.norm_ss, count)
                dve.tensor_scalar(var[:, cols], ss[:, cols], 1.0 / D, EPS, ALU.mult,
                                  ALU.add).then_inc(s.norm_ms, tiles)
                dve.wait_ge(s.norm_ms, count)
                dve.reciprocal(var[:, cols], var[:, cols]).then_inc(s.norm_inv, tiles)

            def norm1_rows(pair):
                dve.wait_ge(s.norm_rstd, N1 + 2 * pair + 2)
                for tt in (2 * pair, 2 * pair + 1):
                    dve.tensor_scalar(x_rows(tt), x_rows(tt), rstd[:, tt:tt + 1], None,
                                      ALU.mult).then_inc(s.norm_xn, 1)

            for pair in range(TT // 2):
                inverse_ms(2 * pair, N1 + 2 * pair + 2, 2)
                if pair:
                    norm1_rows(pair - 1)
            norm1_rows(TT // 2 - 1)
            dve.wait_ge(s.c_act_ready, 1)
            for n in range(2, 4):
                a = ada_first[n]
                dve.wait_ge(s.ada_first_in[n], 16)
                dve.tensor_scalar(a[:, 0, :], a[:, 0, :], c_act[:, 0:1], None, ALU.mult).then_inc(s.ada_acc, 1)
                for k in range(1, KT):
                    dve.wait_ge(s.ada_acc, (n - 2) * KT + k)
                    dve.scalar_tensor_tensor(out=a[:, 0, :], in0=a[:, k, :], scalar=c_act[:, k:k + 1],
                                             in1=a[:, 0, :], op0=ALU.mult, op1=ALU.add).then_inc(s.ada_acc, 1)
            dve.wait_ge(s.ada_first_mm, 1)
            dve.tensor_tensor(mod[:, 0:2 * KT], bank(1)[:, 0:2 * KT],
                              col_a[:, C_ADAB:C_ADAB + 2 * KT], ALU.add).then_inc(s.mod_step, 1)
            dve.wait_ge(s.mod_step, 1)
            dve.scalar_tensor_tensor(out=scale1[:, :], in0=mod[:, SC1:SC1 + KT], scalar=1.0,
                                     in1=col_a[:, C_N1:C_N1 + KT], op0=ALU.add,
                                     op1=ALU.mult).then_inc(s.mod_step, 1)
            dve.wait_ge(s.mod_step, 2)
            for u in range(UNITS + 2):
                k = u % KT
                if u < UNITS:
                    dve.wait_ge(s.norm_turned, u + 1)
                    if u >= KT:
                        dve.wait_ge(s.ba_mm, u - KT + 1)
                    if u == 0:
                        dve.wait_ge(s.norm_ss, N1 + TT)
                    elif u >= KT:
                        dve.wait_ge(s.norm_lo if u % 2 == 0 else s.norm_lo_odd, (u - KT) // 2 + 1)
                    dve.tensor_scalar(hf[:, k, :], bank(2 + u % TURN_BANKS), scale1[:, k:k + 1],
                                      mod[:, SH1 + k:SH1 + k + 1], ALU.mult, ALU.add).then_inc(s.norm_hf, 1)
                if u >= 2 and u % 2:
                    v = u - 2
                    dve.wait_ge(s.norm_hi, v + 1)
                    dve.tensor_tensor(unit(h, 1, v), hf_unit(v), unit(h, 0, v).bitcast(F32),
                                      ALU.subtract).then_inc(s.norm_lo_odd, 1)

            for half in range(2):
                dve.wait_ge(s.ba_mm, (half + 1) * KT)
                dve.tensor_copy(ba_rows[0:2 * NH, half * BANK:(half + 1) * BANK],
                                bank(BA_BANK[half])[0:2 * NH, :]).then_inc(s.ba_rows_ready, 1)
            dve.wait_ge(s.ba_turned, 1)
            dve.tensor_copy(ba[:, :, :], bank(BA_BANK[0])[:, 0:TT * 2 * NH].rearrange("p (t n) -> p t n", n=2 * NH)
                            ).then_inc(s.gate_step, 1)
            dve.wait_ge(s.gate_step, 1)
            dve.wait_ge(s.gate_rows_in, 32)
            dve.tensor_tensor(ba[:, :, NH:2 * NH], ba[:, :, NH:2 * NH],
                              gate_rows[:, 1:2, :].to_broadcast([P, TT, NH]), ALU.add).then_inc(s.gate_step, 1)
            dve.wait_ge(s.gate_step, 2)
            dve.tensor_scalar(tmp_m[:, :, :], ba[:, :, NH:2 * NH], 0.0, None, ALU.max).then_inc(s.gate_step, 1)
            dve.scalar_tensor_tensor(out=tmp_g[:, :, :], in0=ba[:, :, NH:2 * NH], scalar=-1.0,
                                     in1=ba[:, :, NH:2 * NH], op0=ALU.mult, op1=ALU.min).then_inc(s.gates_in, 1)
            dve.wait_ge(s.gate_act, 4)
            dve.tensor_scalar(beta[:, :, :], beta[:, :, :], 1.0, None, ALU.add).then_inc(s.gate_step, 1)
            dve.tensor_tensor(tmp_g[:, :, :], tmp_g[:, :, :], tmp_m[:, :, :], ALU.add).then_inc(s.gate_step, 1)
            dve.wait_ge(s.gate_step, 4)
            dve.reciprocal(beta[:, :, :], beta[:, :, :]).then_inc(s.gate_step, 1)
            dve.wait_ge(s.gate_step, 5)
            dve.scalar_tensor_tensor(out=g[:, :, :], in0=tmp_g[:, :, :], scalar=-1.0,
                                     in1=gate_rows[:, 0:1, :].to_broadcast([P, TT, NH]), op0=ALU.mult,
                                     op1=ALU.mult).then_inc(s.gate_step, 1)
            dve.wait_ge(s.gate_step, 6)
            dve.tensor_scalar(neg_dn_w[:, :], col_a[:, C_DN:C_DN + 1], -1.0, None, ALU.mult).then_inc(s.gate_step, 1)
            dve.wait_ge(s.gate_step, 7)
            dve.tensor_scalar(neg_beta[:, :, :], beta[:, :, :], -1.0, None, ALU.mult).then_inc(s.gates_ready, 1)

            def flat(store, j):
                return store[:, ds(j, 1), :].rearrange("p a n -> p (a n)")

            def conv_tap(dst, src, weight, lag, done):
                dve.scalar_tensor_tensor(out=dst[:, lag:L], in0=src[:, 0:L - lag], scalar=weight,
                                         in1=dst[:, lag:L], op0=ALU.mult, op1=ALU.add).then_inc(done, 1)

            def conv4(j, dst, src, kind):
                col = C_QKV + kind * NH + j
                steps = 11 * j + 2 + 3 * kind
                dve.wait_ge(s.conv_tapped, 4 * j + 2 + kind)
                conv_tap(dst, src, col_b[:, ds(col + 2 * 3 * NH, 1)], 1, s.conv_step)
                dve.wait_ge(s.conv_step, steps + 1)
                conv_tap(dst, src, col_b[:, ds(col + 3 * NH, 1)], 2, s.conv_step)
                dve.wait_ge(s.conv_step, steps + 2)
                conv_tap(dst, src, col_b[:, ds(col, 1)], 3, s.conv_step)

            def squares_lo(store, j, n):
                dve.wait_ge(*((s.ya_raw, j + 1), (s.silu_done, 3 * j + 1), (s.silu_done, 3 * j + 2))[n])
                dve.wait_ge(*((s.k_norm, j), (s.ya_norm, j + 1), (s.q_norm, j + 1))[n])
                dve.tensor_tensor(sq[:, :], flat(store, j), flat(store, j), ALU.mult).then_inc(s.sq_raw, 1)
                dve.wait_ge(s.sq_raw, 3 * j + n + 1)
                dve.wait_ge(s.sq_hi_done, 3 * j + n + 1)
                dve.tensor_tensor(sq_lo[:, :], sq[:, :], sq_hi[:, :].bitcast(F32),
                                  ALU.subtract).then_inc(s.sq_ready, 1)

            def proj_round(j):
                dve.wait_ge(s.ax_taken, j + 1)
                dve.wait_ge(s.tile_mm, j * NPOS + 2)
                dve.tensor_tensor(cx[:, :], bank(T_BANK[AC], 2), flat(a_t, j), ALU.mult).then_inc(s.cx_ready, 1)
                dve.wait_ge(s.conv_tapped, 4 * j + 1)
                conv_tap(flat(a_t, j), cx[:, :], col_a[:, ds(C_CA + AT + j, 1)], 1, s.conv_step)
                dve.wait_ge(s.conv_step, 11 * j + 1)
                conv_tap(flat(a_t, j), cx[:, :], col_a[:, ds(C_CA + j, 1)], 2, s.conv_step)
                dve.wait_ge(s.conv_step, 11 * j + 2)
                dve.wait_ge(s.tile_mm, j * NPOS + 3)
                dve.tensor_tensor(flat(a_t, j), bank(T_BANK[AB], 2), flat(a_t, j), ALU.mult).then_inc(s.ya_raw, 1)
                squares_lo(a_t, j, 0)
                conv4(j, flat(q_t, j), bank(T_BANK[Q], 2), 0)
                dve.wait_ge(s.stat_rs, 3 * j + 1)
                dve.scalar_tensor_tensor(out=flat(a_t, j), in0=flat(a_t, j), scalar=col_a[:, ds(C_NA + j, 1)],
                                         in1=sq[:, :], op0=ALU.mult, op1=ALU.mult).then_inc(s.ya_norm, 1)
                squares_lo(q_t, j, 1)
                conv4(j, flat(k_t, j), bank(T_BANK[K], 2), 1)
                dve.wait_ge(s.stat_rs, 3 * j + 2)
                dve.tensor_tensor(flat(q_t, j), flat(q_t, j), sq[:, :], ALU.mult).then_inc(s.q_norm, 1)
                squares_lo(k_t, j, 2)
                conv4(j, flat(v_t, j), bank(T_BANK[V], 2), 2)
                dve.wait_ge(s.stat_rs, 3 * j + 3)
                dve.tensor_tensor(flat(k_t, j), flat(k_t, j), sq[:, :], ALU.mult).then_inc(s.k_norm, 1)
                dve.wait_ge(s.ada_mm, j + 1)
                dve.tensor_tensor(mod[:, ds(GT1 + j * 8, 8)], bank(6)[:, 0:8],
                                  col_a[:, ds(C_ADAB + GT1 + j * 8, 8)], ALU.add).then_inc(s.mod_taken, 1)

            with dve.Fori(0, NH) as j:
                proj_round(j)
            dve.wait_ge(s.mod_taken, NH)
            dve.scalar_tensor_tensor(out=scale2[:, :], in0=mod[:, SC2:SC2 + KT], scalar=1.0,
                                     in1=col_a[:, C_N2:C_N2 + KT], op0=ALU.add,
                                     op1=ALU.mult).then_inc(s.mod_step, 1)

            def by_head(t):
                return t.unsqueeze(2).to_broadcast([P, NH, P])

            def chunk_cols(t, n):
                return t[:, ds(n, 1), :].rearrange("p a h -> p (a h)")

            def all_heads(t):
                return t[:, :].unsqueeze(1).to_broadcast([P, NH, P])

            def level(lev, n, index, count, slot, pm, p_bank, t_bank, p_mm, t_mm, sem, steps, part):
                mm_count = n * count + index + 1
                done = n * steps + 3 * index
                if part == "P":
                    dve.wait_ge(p_mm, mm_count)
                    if sem is s.dn_al and index == 0:
                        dve.wait_ge(s.dn_a, n * A_STEPS + A_UM)
                    dve.tensor_tensor(pm[:, :, :], bank(p_bank, 1, P),
                                      level_mask[:, lev:lev + 1, :].to_broadcast([P, NH, P]),
                                      ALU.mult).then_inc(sem, 1)
                    return
                dve.wait_ge(t_mm, mm_count)
                u = halves(um[:, slot, :, :], lev)[:, 1, :, :]
                u_update = compact(bank(t_bank)[:, 2 * P:4 * P], lev)
                if lev < LEVELS - 1:
                    tt = halves(tm[:, slot, :, :], lev)[:, 0, :, :]
                    dve.tensor_tensor(tt, tt, compact(bank(t_bank)[:, 0:2 * P], lev),
                                      ALU.subtract).then_inc(sem, 1)
                    dve.tensor_tensor(u, u, u_update, ALU.subtract).then_inc(sem, 1)
                else:
                    wait_reuse(dve, s.dn_v, n)
                    dve.tensor_tensor(halves(um_done[:, :, :], lev)[:, 1, :, :], u, u_update,
                                      ALU.subtract).then_inc(sem, 1)

            def level_a(n, slot, index, part):
                level(A_LEVELS[index], n, index, LA, slot, pm_a, 1, 3, s.dn_p_a, s.dn_t_a, s.dn_al, 3 * LA, part)

            def level_b(n, slot, index, part):
                level(B_LEVELS[index], n, index, LB, slot, pm_b, 4, 5, s.dn_p_b, s.dn_t_b, s.dn_b, B_STEPS, part)

            def dn_step(n, slot, a, b, c):
                done = n * A_STEPS

                def after(step):
                    dve.wait_ge(s.dn_a, done + step)

                if b:
                    level_b(n - 1, 1 - slot, 0, "P")
                if a:
                    dve.wait_ge(s.dn_egb, n + 1)
                    wait_reuse(dve, s.dn_t_a, LA * n)
                    dve.tensor_tensor(pm_a[:, :, :], bank(0, 1, P), all_heads(ident), ALU.mult).then_inc(s.dn_a, 1)
                    after(A_DIAG)
                    dve.tensor_reduce(gc[:, :], pm_a[:, :, :], AX_X, ALU.add).then_inc(s.dn_a, 1)
                    after(A_SUM)
                    dve.tensor_tensor(dec[:, :, :], bank(0, 1, P), by_head(gc[:, :]), ALU.subtract).then_inc(s.dn_a, 1)
                    after(A_DIFF)
                    dve.tensor_scalar(dec[:, :, :], dec[:, :, :], 0.0, None, ALU.min).then_inc(s.dn_a, 1)
                    dve.tensor_tensor(kdec[:, :], bank(0, 1, P)[:, :, P - 1], gc[:, :],
                                      ALU.subtract).then_inc(s.dn_a, 1)
                if b:
                    level_b(n - 1, 1 - slot, 0, "T")
                if a:
                    dve.wait_ge(s.dn_dec, n + 1)
                    dve.tensor_tensor(dec[:, :, :], dec[:, :, :], all_heads(causal), ALU.mult).then_inc(s.dn_a, 1)
                if b:
                    level_b(n - 1, 1 - slot, 1, "P")
                if a:
                    after(A_MASK)
                    dve.wait_ge(s.dn_kk, n + 1)
                    dve.tensor_tensor(lt[:, slot, :, :], bank(1, 1, P), dec[:, :, :], ALU.mult).then_inc(s.dn_a, 1)
                if c:
                    dve.wait_ge(s.dn_v, n - 1)
                    wait_reuse(dve, s.dn_s, n - 2)
                    dve.tensor_tensor(vn[:, :, :], bank(7, 1, P), by_head(chunk_cols(neg_beta, n - 2)),
                                      ALU.mult).then_inc(s.dn_vn, 1)
                if a:
                    after(A_LT0)
                    dve.tensor_tensor(lt[:, slot, :, :], lt[:, slot, :, :], by_head(chunk_cols(beta, n)),
                                      ALU.mult).then_inc(s.dn_a, 1)
                if b:
                    level_b(n - 1, 1 - slot, 1, "T")
                if a:
                    after(A_LT)
                    dve.tensor_tensor(pm_a[:, :, :], lt[:, slot, :, :],
                                      level_mask[:, 0:1, :].to_broadcast([P, NH, P]), ALU.mult).then_inc(s.dn_a, 1)
                    after(A_M0)
                    wait_reuse(dve, s.dn_t_b, LB * (n - 1))
                    wait_reuse(dve, s.dn_um_copied, n - 1)
                    dve.tensor_tensor(um[:, slot, :, :], all_heads(ident), pm_a[:, :, :],
                                      ALU.subtract).then_inc(s.dn_a, 1)
                if b:
                    level_b(n - 1, 1 - slot, 2, "P")
                if a:
                    dve.wait_ge(s.dn_kt, n + 1)
                    wait_reuse(dve, s.dn_o, n - 1)
                    dve.tensor_tensor(att[:, slot, :, :], bank(2, 1, P), dec[:, :, :], ALU.mult).then_inc(s.dn_a, 1)
                if c:
                    dve.wait_ge(s.dn_s, n - 1)
                    for hd in range(NH):
                        dve.scalar_tensor_tensor(out=st[:, hd, :], in0=st[:, hd, :], scalar=cdec[:, slot, hd:hd + 1],
                                                 in1=bank(6, 1, P)[:, hd, :], op0=ALU.mult,
                                                 op1=ALU.add).then_inc(s.dn_st, 1)
                if b:
                    level_b(n - 1, 1 - slot, 2, "T")
                if a:
                    dve.wait_ge(s.dn_kdec, n + 1)
                    wait_reuse(dve, s.dn_s, n - 1)
                    dve.tensor_tensor(kd[:, slot, :, :], bank(3, 1, P), by_head(kdec[:, :]),
                                      ALU.mult).then_inc(s.dn_a, 1)
                    wait_reuse(dve, s.dn_st, NH * n)
                    dve.tensor_copy(cdec[:, slot, :], egb[:, :, P - 1]).then_inc(s.dn_a, 1)
                for index in range(3, max(LB, 3 + LA)):
                    if b and index < LB:
                        level_b(n - 1, 1 - slot, index, "P")
                    if a and index - 3 < LA:
                        level_a(n, slot, index - 3, "P")
                    if b and index < LB:
                        level_b(n - 1, 1 - slot, index, "T")
                    if a and index - 3 < LA:
                        level_a(n, slot, index - 3, "T")

            def gate_diag(first_col, dst):
                for k in range(KT):
                    dve.tensor_scalar(dst(k), ident[:, :], mod[:, first_col + k:first_col + k + 1], None,
                                      ALU.mult).then_inc(s.diag_ready, 1)

            dve.wait_ge(s.tile_mm, NH * NPOS)
            gate_diag(GT1, lambda k: diag_a[:, k // 4, k % 4 * P:(k % 4 + 1) * P])
            dve.memset(st[:, :, :], 0.0).then_inc(s.dn_st, NH)
            dve.wait_ge(s.masks_ready, 1)
            dn_step(0, 0, True, False, False)
            dn_step(1, 1, True, True, False)
            with dve.Fori(0, TT // 2 - 1) as i:
                dn_step(2 * i + 2, 0, True, True, True)
                dn_step(2 * i + 3, 1, True, True, True)
            dn_step(TT, 0, False, True, True)
            dn_step(TT + 1, 1, False, False, True)

            dve.wait_ge(s.dn_o_copied, TT)
            dve.wait_ge(s.dn_st, NH * (TT + 1))
            dve.sem_inc(s.dn_over, 1)

            def gate_w_out(k):
                dve.wait_ge(s.wo_raw_in[k % 2], 16 * (k // 2 + 1))
                dve.tensor_tensor(wo_raw[:, k % 2, :], wo_raw[:, k % 2, :], gate_row[:, :],
                                  ALU.mult).then_inc(s.wo_gated, 1)

            def yb(hd):
                dve.wait_ge(s.ostat_rs, hd + 1)
                dve.scalar_tensor_tensor(out=q_t[:, hd, :], in0=q_t[:, hd, :], scalar=neg_dn_w[:, 0:1],
                                         in1=osq[:, hd % 2, :], op0=ALU.mult, op1=ALU.mult).then_inc(s.yb_rs_used, 1)
                dve.wait_ge(s.yb_rs_used, hd + 1)
                dve.tensor_tensor(q_t[:, hd, :], q_t[:, hd, :], z_t[:, hd, :], ALU.mult).then_inc(s.yb_ready, 1)

            def drain_out(n):
                tt, half = n % (2 * TT) // 2, n % 2
                dve.wait_ge(s.out_mm, n + 1)
                if n < 2 * TT:
                    dve.wait_ge(x_in(tt), 32)
                else:
                    dve.wait_ge(s.x2_out, n - 2 * TT + 1)
                piece = x2[:, tt, half * BANK:(half + 1) * BANK]
                dve.tensor_tensor(piece, piece, bank(n % 4 if n < 2 * TT else n % 2), ALU.add).then_inc(s.x2_out, 1)

            def norm2_rows(tt):
                inverse_ms(tt, N2 + tt + 1)
                dve.wait_ge(s.norm_rstd, N2 + tt + 1)
                dve.tensor_scalar(xn2[:, tt % 2, :], x2[:, tt, :], rstd[:, tt:tt + 1], None,
                                  ALU.mult).then_inc(s.norm_xn, 1)

            def norm2_modulate(tt):
                dst = hf2[:, tt % 2, :, :]
                dve.wait_ge(s.norm_turned, M2 + tt + 1)
                if tt >= 2:
                    dve.wait_ge(s.norm_lo, LO2 + tt - 1)
                dve.tensor_tensor(dst, bank(4 + 2 * (tt % 2), 2, P),
                                  scale2[:, :].unsqueeze(2).to_broadcast([P, KT, P]),
                                  ALU.mult).then_inc(s.norm_step, 1)
                dve.wait_ge(s.norm_step, tt + 1)
                dve.tensor_tensor(dst, dst, mod[:, SH2:SH2 + KT].unsqueeze(2).to_broadcast([P, KT, P]),
                                  ALU.add).then_inc(s.norm_hf, 1)

            beside = {1: [(yb, 0)], 2: [(yb, 1)], 4: [(gate_w_out, 4)], 5: [(gate_w_out, 5)], 6: [(gate_w_out, 6)],
                      7: [(gate_w_out, 7)], 8: [(yb, 2)], 9: [(yb, 3)]}
            for n in range(2 * TT):
                drain_out(n)
                for what, which in beside.get(n, []):
                    what(which)
            for tt in range(TT):
                drain_out(2 * TT + 2 * tt)
                drain_out(2 * TT + 2 * tt + 1)
                if tt >= 1:
                    norm2_rows(tt - 1)
                if tt >= 2:
                    norm2_modulate(tt - 2)
            norm2_rows(TT - 1)
            norm2_modulate(TT - 2)
            dve.wait_ge(s.gate_mm, 1)
            gate_diag(GT2, lambda k: diag[:, k, :])
            norm2_modulate(TT - 1)

            def conv3(f, dst, src, first_col, tapped, step, done):
                dve.wait_ge(s.ff_tapped, tapped)
                conv_tap(dst, src, col_c[:, ds(2 * FT + first_col + f, 1)], 1, step)
                dve.wait_ge(step, f + 1)
                conv_tap(dst, src, col_c[:, ds(first_col + f, 1)], 2, done)

            def drain_down(i):
                for n in range(2 * TT):
                    tt, half = n // 2, n % 2
                    dve.wait_ge(s.down_tile_mm, i * 2 * TT + n + 1)
                    piece = x2[:, tt, half * BANK:(half + 1) * BANK]
                    dve.tensor_tensor(piece, piece, bank(4 + n % 4), ALU.add).then_inc(s.x2_mlp, 1)

            def mlp_pair(i, first):
                for u in range(2):
                    f = 2 * i + u
                    conv3(f, cg[:, :], bank(0, 2), 0, 2 * f + 1, s.cg_step, s.cg_conv)
                    if u == 0 and not first:
                        drain_down(i - 1)
                    conv3(f, cu[:, :], bank(2, 2), FT, 2 * f + 2, s.cu_step, s.cu_conv)
                    dve.wait_ge(s.cg_silu, f + 1)
                    dve.wait_ge(s.cu_conv, f + 1)
                    dve.tensor_tensor(cg[:, :], cg[:, :], cu[:, :], ALU.mult).then_inc(s.act_ready, 1)

            mlp_pair(0, True)
            with dve.Fori(1, FT // 2) as i:
                mlp_pair(i, False)

            def final_rows(tt):
                inverse_ms(tt, NF + tt + 1)
                dve.wait_ge(s.norm_rstd, NF + tt + 1)
                dve.wait_ge(s.normf_in, 16)
                dve.scalar_tensor_tensor(out=x2[:, tt, :], in0=x2[:, tt, :], scalar=rstd[:, tt:tt + 1],
                                         in1=normf_row[:, :], op0=ALU.mult, op1=ALU.mult).then_inc(s.y_ready, 1)

            i = FT // 2 - 1
            for n in range(2 * TT):
                tt, half = n // 2, n % 2
                dve.wait_ge(s.down_tile_mm, i * 2 * TT + n + 1)
                piece = x2[:, tt, half * BANK:(half + 1) * BANK]
                dve.tensor_tensor(piece, piece, bank((4 + n) % 8), ALU.add).then_inc(s.x2_mlp, 1)
                if half and tt:
                    final_rows(tt - 1)
            final_rows(TT - 1)

        @block.tensor
        def _(pe):
            def three_pass(dst, pairs, first=True, last=True):
                for n, (a_hi, a_lo, b_hi, b_lo) in enumerate(pairs):
                    pe.matmul(dst, a_hi, b_hi, start=(first and n == 0), stop=False)
                    pe.matmul(dst, a_hi, b_lo, start=False, stop=False)
                    mm = pe.matmul(dst, a_lo, b_hi, start=False, stop=(last and n == len(pairs) - 1))
                return mm

            def h_half(part, k, half):
                return h[:, half * (TT // 2):(half + 1) * (TT // 2), part, k, :]

            pe.wait_ge(s.consts_ready, 1)
            pe.wait_ge(s.rows_in, 160)
            pe.transpose(bank(0)[:, 0:NA_ROWS], rows_a[0:NA_ROWS, :], ident[0:NA_ROWS, 0:NA_ROWS])
            pe.transpose(bank(0)[:, P:P + NB_ROWS], rows_b[0:NB_ROWS, :], ident[0:NB_ROWS, 0:NB_ROWS])
            pe.transpose(bank(0)[:, 2 * P:2 * P + NC_ROWS], rows_c[0:NC_ROWS, :],
                         ident[0:NC_ROWS, 0:NC_ROWS]).then_inc(s.rows_turned, 1)

            def turn1(u):
                half, k = u // KT, u % KT
                if k == 0:
                    pe.wait_ge(s.norm_xn, N1 + (half + 1) * TH)
                if u >= TURN_BANKS:
                    pe.wait_ge(s.norm_hf, u - TURN_BANKS + 1)
                for i in range(TH):
                    mm = pe.transpose(bank(2 + u % TURN_BANKS)[:, i * P:(i + 1) * P],
                                      x_rows(half * TH + i)[:, k * P:(k + 1) * P], ident[:, :])
                mm.then_inc(s.norm_turned, 1)

            def beta_alpha(u):
                half, k = u // KT, u % KT
                pe.wait_ge(s.norm_hf, u + 1)
                pe.matmul(bank(BA_BANK[half])[0:2 * NH, :], w_ba[:, k, :], hf[:, k, :],
                          start=(k == 0), stop=(k == KT - 1)).then_inc(s.ba_mm, 1)

            for u in range(TURN_BANKS):
                turn1(u)
            pe.wait_ge(s.c_act_ready, 1)
            for blk in [4, 5, 6, 7, 0, 1, 2, 3, 8, 9, 10, 11, 12, 13, 14, 15]:
                n, cols = blk // 4, slice(blk % 4 * P, (blk % 4 + 1) * P)
                if n == 0:
                    pe.wait_ge(s.ada_first_step, 4)
                elif n == 1:
                    pe.wait_ge(s.ada_first_in[1], 16)
                else:
                    pe.wait_ge(s.ada_acc, (n - 1) * KT)
                for k in range(KT if n == 1 else 1):
                    mm = pe.matmul(bank(1)[:, blk:blk + 1], ada_first[n][:, k, cols],
                                   c_act[:, k:k + 1] if n == 1 else ones[:, 0:1],
                                   start=(k == 0), stop=(n != 1 or k == KT - 1))
            mm.then_inc(s.ada_first_mm, 1)
            pe.wait_ge(s.w_ba_in, 16)
            for u in range(UNITS):
                if u + TURN_BANKS < UNITS:
                    turn1(u + TURN_BANKS)
                beta_alpha(u)
            pe.wait_ge(s.ba_rows_ready, 2)
            for tt in range(TT):
                mm = pe.transpose(bank(BA_BANK[0])[:, tt * 2 * NH:(tt + 1) * 2 * NH],
                                  ba_rows[0:2 * NH, tt * P:(tt + 1) * P], ident[0:2 * NH, 0:2 * NH])
            mm.then_inc(s.ba_turned, 1)

            def turn2(tt):
                pe.wait_ge(s.norm_xn, N2 + tt + 1)
                if tt >= 2:
                    pe.wait_ge(s.norm_step, tt - 1)
                for k in range(KT):
                    mm = pe.transpose(bank(4 + 2 * (tt % 2), 2, P)[:, k, :],
                                      xn2[:, tt % 2, k * P:(k + 1) * P], ident[:, :])
                mm.then_inc(s.norm_turned, 1)

            def proj_tile(pos, j, free):
                slot = W_SLOT[pos]
                pe.wait_ge(s.w_lo_done, nth(pos, j))
                for half in range(2):
                    pe.wait_ge(*free[half])
                    mm = three_pass(bank(T_BANK[pos] + half),
                                    [(w_split[:, slot, 0, k, :], w_split[:, slot, 1, k, :],
                                      h_half(0, k, half), h_half(1, k, half)) for k in range(KT)])
                mm.then_inc(s.tile_mm, 1)

            def statistic(n, weights):
                pe.wait_ge(s.sq_ready, n + 1)
                pe.wait_ge(s.stat_ln, n)
                for half in range(2):
                    cols = slice(half * BANK, (half + 1) * BANK)
                    pe.matmul(bank(4 + half), weights[:, :], sq_hi[:, cols], start=True, stop=False)
                    mm = pe.matmul(bank(4 + half), weights[:, :], sq_lo[:, cols], start=False, stop=True)
                mm.then_inc(s.stat_mm, 1)

            def ada_columns(j):
                pe.wait_ge(s.ada_summed, 8 * (j + 1))
                pe.wait_ge(s.mod_taken, j)
                for b in range(8):
                    mm = pe.matmul(bank(6)[:, b:b + 1], ada_columns_of(b), ones[:, 0:1], start=True, stop=True)
                mm.then_inc(s.ada_mm, 1)

            def proj_round(j):
                proj_tile(AX, j, [(s.z_taken[0], j), (s.z_taken[1], j)])
                proj_tile(AC, j, [(s.conv_step, 11 * j)] * 2)
                proj_tile(AB, j, [(s.ax_taken, j + 1)] * 2)
                proj_tile(Q, j, [(s.cx_ready, j + 1)] * 2)
                statistic(3 * j, group_ones_r)
                proj_tile(K, j, [(s.ya_raw, j + 1)] * 2)
                statistic(3 * j + 1, ones_r)
                proj_tile(V, j, [(s.conv_step, 11 * j + 5)] * 2)
                statistic(3 * j + 2, ones_r)
                proj_tile(Z, j, [(s.conv_step, 11 * j + 8)] * 2)
                ada_columns(j)

            pe.wait_ge(s.norm_lo, LO2)
            pe.wait_ge(s.norm_lo_odd, UNITS // 2)
            with pe.Fori(0, NH) as j:
                proj_round(j)

            def heads(dst, a, b, done=None, n=1):
                for hd in range(NH):
                    mm = pe.matmul(dst[:, hd, :], a[:, hd, :], b[:, hd, :], start=True, stop=True)
                if done is not None:
                    mm.then_inc(done, n)

            def level_p(lt_, tm_, p_bank, done):
                heads(bank(p_bank, 1, P), lt_, tm_, done)

            def level_t(lev, um_, pm, t_bank, done):
                first = lambda ap: ap.rearrange("p (a t n) -> p t a n", t=2, n=1 << lev)[:, 0, :, :]
                second = lambda ap: ap.rearrange("p (a t n) -> p t a n", t=2, n=1 << lev)[:, 1, :, :]
                half = P // 2
                dst = bank(t_bank)
                if lev < LEVELS - 1:
                    for hd in range(NH):
                        pe.matmul(dst[:, hd * half:(hd + 1) * half], um_[:, hd, :], first(pm[:, hd, :]),
                                  start=True, stop=True)
                for hd in range(NH):
                    mm = pe.matmul(dst[:, 2 * P + hd * half:2 * P + (hd + 1) * half], pm[:, hd, :],
                                   second(um_[:, hd, :]), start=True, stop=True)
                mm.then_inc(done, 1)

            def level_b(n, slot, index, part):
                done = n * B_STEPS + 3 * index
                if part == "P":
                    if index == 0:
                        pe.wait_ge(s.dn_al, (n + 1) * 3 * LA)
                    wait_reuse(pe, s.dn_b, done)
                    level_p(lt[:, slot, :, :], tm[:, slot, :, :], 4, s.dn_p_b)
                else:
                    pe.wait_ge(s.dn_b, done + 1)
                    level_t(B_LEVELS[index], um[:, slot, :, :], pm_b, 5, s.dn_t_b)

            def level_a(n, slot, index, part):
                done = n * 3 * LA + 3 * index
                if part == "P":
                    pe.wait_ge(s.dn_t1_copied, n + 1)
                    pe.wait_ge(s.dn_a, n * A_STEPS + A_KD)
                    if index:
                        pe.wait_ge(s.dn_al, done)
                    level_p(lt[:, slot, :, :], tm[:, slot, :, :], 1, s.dn_p_a)
                else:
                    pe.wait_ge(s.dn_al, done + 1)
                    level_t(A_LEVELS[index], um[:, slot, :, :], pm_a, 3, s.dn_t_a)

            def dn_step(n, slot, a, b, c):
                if a:
                    pe.wait_ge(s.dn_gb, n + 1)
                    wait_reuse(pe, s.dn_t1_copied, n)
                    for hd in range(NH):
                        mm = pe.matmul(bank(0, 1, P)[:, hd, :], lt[:, slot, hd, :], causal[:, :], start=True, stop=True)
                    mm.then_inc(s.dn_cum, 1)
                if b:
                    level_b(n - 1, 1 - slot, 0, "P")
                if c:
                    pe.wait_ge(s.dn_vc, n - 1)
                    pe.wait_ge(s.dn_kg, n - 1)
                    pe.wait_ge(s.dn_st, NH * (n - 1))
                    for hd in range(NH):
                        pe.matmul(bank(6, 1, P)[:, hd, :], vc[:, hd, :], ident[:, :], start=True, stop=False)
                        mm = pe.matmul(bank(6, 1, P)[:, hd, :], kg[:, slot, hd, :], st[:, hd, :],
                                       start=False, stop=True)
                    mm.then_inc(s.dn_r, 1)
                if b:
                    level_b(n - 1, 1 - slot, 0, "T")
                if a:
                    pe.wait_ge(s.dn_kc, n + 1)
                    wait_reuse(pe, s.dn_al, n * 3 * LA)
                    heads(bank(1, 1, P), kc, kc, s.dn_kk)
                if b:
                    level_b(n - 1, 1 - slot, 1, "P")
                if c:
                    pe.wait_ge(s.dn_rr, n - 1)
                    wait_reuse(pe, s.dn_o_copied, n - 2)
                    pe.wait_ge(s.dn_b, (n - 1) * B_STEPS)
                    pe.wait_ge(s.dn_um_copied, n - 1)
                    heads(bank(7, 1, P), um_done, rr, s.dn_v)
                if a:
                    wait_reuse(pe, s.dn_a, n * A_STEPS)
                    heads(bank(2, 1, P), kc, q_t[:, :, ds(n * P, P)])
                if b:
                    level_b(n - 1, 1 - slot, 1, "T")
                if a:
                    for hd in range(NH):
                        mm = pe.transpose(bank(3, 1, P)[:, hd, :], kc[:, hd, :], ident[:, :])
                    mm.then_inc(s.dn_kt, 1)
                if c:
                    pe.wait_ge(s.dn_vn, n - 1)
                    pe.wait_ge(s.dn_qd, n - 1)
                    for hd in range(NH):
                        pe.matmul(bank(7, 1, P)[:, hd, :], st[:, hd, :], qd[:, slot, hd, :], start=True, stop=False)
                        mm = pe.matmul(bank(7, 1, P)[:, hd, :], vn[:, hd, :], att[:, slot, hd, :],
                                       start=False, stop=True)
                    mm.then_inc(s.dn_o, 1)
                if b:
                    level_b(n - 1, 1 - slot, 2, "P")
                if c:
                    heads(bank(6, 1, P), kd[:, slot, :, :], vn, s.dn_s)
                if b:
                    level_b(n - 1, 1 - slot, 2, "T")
                if isinstance(n, int) and n == 0:
                    gate_row_mm(1, [diag_a[:, half, :] for half in range(2)], 6)
                if a:
                    pe.wait_ge(s.dn_a, n * A_STEPS + A_UM)
                    for hd in range(NH):
                        mm = pe.transpose(bank(0, 1, P)[:, hd, :], um[:, slot, hd, :], ident[:, :])
                    mm.then_inc(s.dn_t1, 1)
                for index in range(3, max(LB, 3 + LA)):
                    if b and index < LB:
                        level_b(n - 1, 1 - slot, index, "P")
                    if a and index - 3 < LA:
                        level_a(n, slot, index - 3, "P")
                    if b and index < LB:
                        level_b(n - 1, 1 - slot, index, "T")
                    if a and index - 3 < LA:
                        level_a(n, slot, index - 3, "T")

            def gate_row_mm(n, diags, first_bank):
                pe.wait_ge(s.diag_ready, KT * n)
                for half in range(2):
                    mm = pe.matmul(bank(first_bank + half), ones[:, :], diags[half], start=True, stop=True)
                mm.then_inc(s.gate_mm, 1)

            pe.wait_ge(s.z_taken[1], NH)
            pe.wait_ge(s.conv_step, 11 * NH)
            pe.wait_ge(s.stat_ln, 3 * NH)
            pe.wait_ge(s.mod_taken, NH)
            dn_step(0, 0, True, False, False)
            dn_step(1, 1, True, True, False)
            pe.wait_ge(s.gate_row_ready, 1)
            with pe.Fori(0, TT // 2 - 1) as i:
                dn_step(2 * i + 2, 0, True, True, True)
                dn_step(2 * i + 3, 1, True, True, True)
            dn_step(TT, 0, False, True, True)
            dn_step(TT + 1, 1, False, False, True)

            def out_tile(n):
                group, tt, half = n // (2 * TT), n % (2 * TT) // 2, n % 2
                if group == 0:
                    if n >= 4:
                        pe.wait_ge(s.x2_out, n - 3)
                else:
                    pe.wait_ge(s.x2_out, n - 1)
                if n == 0:
                    pe.wait_ge(s.dn_a, TT * A_STEPS)
                    pe.wait_ge(s.dn_al, TT * 3 * LA)
                if n % (2 * TT) == 0:
                    pe.wait_ge(s.wo_lo, 4 * (group + 1))
                    pe.wait_ge(*((s.ya_lo, AT) if group == 0 else (s.yb_lo, NH)))
                dst = bank(n % 4 if group == 0 else n % 2)
                cols = slice(half * BANK, (half + 1) * BANK)
                mm = three_pass(dst, [(h[:, tt, 0, k, :], h[:, tt, 1, k, :], wo_part(k)[:, 0, cols],
                                       wo_part(k)[:, 1, cols]) for k in range(4 * group, 4 * group + 4)])
                mm.then_inc(s.out_mm, 1)

            def out_stat(hd):
                pe.wait_ge(s.osq_ready, hd + 1)
                if hd >= 2:
                    pe.wait_ge(s.ostat_ln, hd - 1)
                for half in range(2):
                    mm = pe.matmul(bank(4 + 2 * (hd % 2) + half), ones[:, :],
                                   osq[:, hd % 2, half * BANK:(half + 1) * BANK], start=True, stop=True)
                mm.then_inc(s.ostat_mm, 1)

            stat_after = {0: [0, 1], 6: [2, 3]}
            for n in range(2 * TT):
                out_tile(n)
                for hd in stat_after.get(n, []):
                    out_stat(hd)
            pe.wait_ge(s.out_mm, 2 * TT)
            pe.sem_inc(s.out_a_mm, 1)

            def wide_tile(w, first_bank, frees, mm_done, token_halves=(0, 1)):
                for half in token_halves:
                    for sem, value in frees[half]:
                        pe.wait_ge(sem, value)
                    mm = three_pass(bank(first_bank + half),
                                    [(w[:, 0, k, :], w[:, 1, k, :], h_half(0, k, half), h_half(1, k, half))
                                     for k in range(KT)])
                if token_halves[-1] == 1:
                    mm.then_inc(mm_done, 1)

            def gate_tile(f, frees, token_halves=(0, 1)):
                pe.wait_ge(s.wg_lo, f + 1)
                wide_tile(wg_split, 0, frees, s.gate_tile_mm, token_halves)

            for tt in range(TT):
                out_tile(2 * TT + 2 * tt)
                out_tile(2 * TT + 2 * tt + 1)
                if tt >= 2:
                    turn2(tt - 2)
            first_frees = [[(s.norm_lo, LO2 + TH), (s.x2_out, 4 * TT)], [(s.norm_lo, LO2 + TT)]]
            gate_tile(0, first_frees, (0,))
            turn2(TT - 2)
            turn2(TT - 1)
            gate_row_mm(2, [diag[:, half * 4:half * 4 + 4, :] for half in range(2)], 2)

            def down_tile(n, dst, us):
                toks = slice(n // 2 * P, (n // 2 + 1) * P)
                cols = slice(n % 2 * BANK, (n % 2 + 1) * BANK)
                return three_pass(dst, [(act_split[:, u, 0, toks], act_split[:, u, 1, toks],
                                         wd_split[:, u, 0, cols], wd_split[:, u, 1, cols]) for u in us],
                                  first=us[0] == 0, last=us[-1] == 1)

            def down(i):
                pe.wait_ge(s.act_lo, 2 * i + 2)
                pe.wait_ge(s.wd_lo, 2 * i + 2)
                for n in range(2 * TT):
                    if n >= 4:
                        pe.wait_ge(s.x2_mlp, i * 2 * TT + n - 3)
                    elif isinstance(i, int) and i == 0:
                        pe.wait_ge(s.norm_step, TT)
                    else:
                        pe.wait_ge(s.x2_mlp, i * 2 * TT)
                    down_tile(n, bank(4 + n % 4), (0, 1)).then_inc(s.down_tile_mm, 1)

            def last_down(i):
                pe.wait_ge(s.act_lo, 2 * i + 1)
                pe.wait_ge(s.wd_lo, 2 * i + 1)
                pe.wait_ge(s.x2_mlp, i * 2 * TT)
                for n in range(8):
                    if n == 4:
                        pe.wait_ge(s.cg_conv, FT)
                    if n == 6:
                        pe.wait_ge(s.cu_conv, FT)
                    down_tile(n, bank((4 + n) % 8), (0,))
                pe.wait_ge(s.act_lo, 2 * i + 2)
                pe.wait_ge(s.wd_lo, 2 * i + 2)
                for n in range(2 * TT):
                    if n >= 8:
                        pe.wait_ge(s.x2_mlp, i * 2 * TT + n - 7)
                    down_tile(n, bank((4 + n) % 8), (1,) if n < 8 else (0, 1)).then_inc(s.down_tile_mm, 1)

            def up_tile(f, frees):
                pe.wait_ge(s.wu_lo, f + 1)
                wide_tile(wu_split, 2, frees, s.up_tile_mm)

            def mlp_pair(i, first):
                for u in range(2):
                    f = 2 * i + u
                    if first and u == 0:
                        gate_tile(f, first_frees, (1,))
                    else:
                        gate_tile(f, [[(s.cg_conv, f)]] * 2)
                    if u == 0 and not first:
                        down(i - 1)
                    if first and u == 0:
                        up_tile(f, [[(s.gate_row_ready, 2)]] * 2)
                    else:
                        up_tile(f, [[(s.cu_conv, f)]] * 2)

            mlp_pair(0, True)
            with pe.Fori(1, FT // 2) as i:
                mlp_pair(i, False)
            last_down(FT // 2 - 1)


_INS = ['x', 'c', 'ada_w', 'ada_b', 'norm1_w', 'w_in', 'conv_a_w', 'norm_a_w', 'conv_qkv_w', 'a_log',
        'dt_bias', 'norm_dn_w', 'w_out', 'norm2_w', 'w_up', 'conv_ff_w', 'w_down', 'norm_f_w']


def kernel(**inputs):
    import numpy as _np
    import concourse.bacc as _bacc
    from concourse import mybir as _mybir
    from concourse.bass_utils import run_bass_kernel_spmd as _run

    nc = _bacc.Bacc("TRN2", target_bir_lowering=False, num_devices=1)
    arrays, args = {}, []
    for name in _INS:
        a = _np.ascontiguousarray(inputs[name])
        arrays[f"in_{name}_dram"] = a
        args.append(nc.dram_tensor(f"in_{name}_dram", a.shape, _mybir.dt.from_np(a.dtype), kind="ExternalInput").ap())
    shape = inputs['x'].shape
    args.append(nc.dram_tensor("out_0_dram", shape, _mybir.dt.float32, kind="ExternalOutput").ap())
    build_program(nc, *args)
    r = _run(nc, [arrays], core_ids=[0])
    return r.results[0]["out_0_dram"]
```
